# Optimizing a Trainium2 kernel written in Bass

```python
import math
import jax, jax.numpy as jnp
from jax import lax
import numpy as np

D_MODEL = 1024
BATCH = 1
SEQ = 256
DEPTH = 2
DEC_BATCH = 8
DEC_SEQ = 1
PAST_LEN = 2048
PAGE_SIZE = 128

N_EVEN = (DEPTH + 1) // 2
N_ODD = DEPTH // 2

MIX_WIDTH = D_MODEL
GLA_HEADS = 4
GLA_VALUE = MIX_WIDTH // 2
GLA_DV = GLA_VALUE // GLA_HEADS
GLA_DK = GLA_DV // 2
GLA_LOWRANK = 16
GATE_NORMALIZER = 16.0
GLA_CHUNK = 64
CONV_CH = MIX_WIDTH - GLA_VALUE
CONV_K = 3

IN0_WIDTHS = (GLA_HEADS * GLA_DK, GLA_HEADS * GLA_DK, GLA_VALUE, GLA_VALUE, GLA_LOWRANK,
              CONV_CH, CONV_CH, CONV_CH)
IN0_DIM = sum(IN0_WIDTHS)

S5_WIDTH = D_MODEL
S5_GROUP = 16
S5_GROUPS = S5_WIDTH // S5_GROUP
S5_STATE = 64

D_FF = 11 * 256
N_EXPERTS = 8
TOP_K = 2
D_FF_EXPERT = 7 * D_MODEL // 2
EPS = 1e-6

kernel_name = "hybrid_gla_shortconv_s5_moe_decode_step"

def rmsnorm(x, g):
    xf = x.astype(jnp.float32)
    y = xf * lax.rsqrt(jnp.mean(xf * xf, axis=-1, keepdims=True) + EPS)
    return (y * g.astype(jnp.float32)).astype(x.dtype)

def _split_in0(p):
    bounds, acc = [], 0
    for w in IN0_WIDTHS[:-1]:
        acc += w
        bounds.append(acc)
    return jnp.split(p, bounds, axis=-1)

def gla_chunked(q, k, v, logg, s0):
    f32 = jnp.float32
    bsz, t = q.shape[:2]
    L = math.gcd(t, GLA_CHUNK)
    n = t // L
    shp = lambda z, d: z.astype(f32).reshape(bsz, n, L, GLA_HEADS, d)
    q = shp(q, GLA_DK) * (GLA_DK ** -0.5)
    k = shp(k, GLA_DK)
    v = shp(v, GLA_DV)
    b = jnp.cumsum(shp(logg, GLA_DK), axis=2)
    b_last = b[:, :, -1]
    q_in = q * jnp.exp(b)
    att = jnp.einsum('bnihd,bnjhd->bnhij', q_in, k * jnp.exp(-b))
    att = jnp.where(jnp.tril(jnp.ones((L, L), bool)), att, 0.0)
    o = jnp.einsum('bnhij,bnjhv->bnihv', att, v)
    ds = jnp.einsum('bnjhd,bnjhv->bnhdv', k * jnp.exp(b_last[:, :, None] - b), v)
    decay = jnp.exp(b_last)

    def step(s, inp):
        d, dsn = inp
        return s * d[..., None] + dsn, s

    s_final, s_start = lax.scan(step, s0.astype(f32),
                                (jnp.moveaxis(decay, 1, 0), jnp.moveaxis(ds, 1, 0)))
    s_start = jnp.moveaxis(s_start, 0, 1)
    o = o + jnp.einsum('bnihd,bnhdv->bnihv', q_in, s_start)
    return o.reshape(bsz, t, GLA_HEADS, GLA_DV), s_final

def gla_conv_mixer(h, w_in, w_gate_up, b_gate_up, g_head, w_conv, w_out, s_gla, conv_buf):
    f32 = jnp.float32
    bsz, t, _ = h.shape
    q, k, v, og, glr, ch, cb, cc = _split_in0(h @ w_in)
    logg = jax.nn.log_sigmoid((glr @ w_gate_up + b_gate_up).astype(f32)) / GATE_NORMALIZER
    hd = lambda z, d: z.reshape(bsz, t, GLA_HEADS, d)
    o, s_new = gla_chunked(hd(q, GLA_DK), hd(k, GLA_DK), hd(v, GLA_DV), hd(logg, GLA_DK), s_gla)
    o = rmsnorm(o, g_head).reshape(bsz, t, GLA_VALUE) * jax.nn.silu(og.astype(f32))
    u = cc * ch
    up = jnp.concatenate([conv_buf.astype(u.dtype), u], axis=1)
    wc = w_conv.astype(u.dtype)
    y = sum(wc[j] * up[:, j:j + t] for j in range(CONV_K))
    y = cb * y
    mixed = jnp.concatenate([o.astype(h.dtype), y], axis=-1)
    return mixed @ w_out, s_new, up[:, t:]

def s5_mixer(h, w_in, a_re, a_im, log_dt, b_re, b_im, c_re, c_im, d_skip, w_glu, s_re, s_im):
    f32 = jnp.float32
    bsz, t, _ = h.shape
    u = (h @ w_in).astype(f32).reshape(bsz, t, S5_GROUPS, S5_GROUP)
    a_re, a_im = a_re.astype(f32), a_im.astype(f32)
    b_re, b_im, c_re, c_im = b_re.astype(f32), b_im.astype(f32), c_re.astype(f32), c_im.astype(f32)
    dt = jnp.exp(log_dt.astype(f32))[:, None]
    mag = jnp.exp(dt * a_re)
    ab_re, ab_im = mag * jnp.cos(dt * a_im), mag * jnp.sin(dt * a_im)
    den = a_re * a_re + a_im * a_im
    nr, ni = ab_re - 1.0, ab_im
    f_re = (nr * a_re + ni * a_im) / den
    f_im = (ni * a_re - nr * a_im) / den
    bb_re = f_re[..., None] * b_re - f_im[..., None] * b_im
    bb_im = f_re[..., None] * b_im + f_im[..., None] * b_re
    bu_re = jnp.einsum('btgi,gpi->btgp', u, bb_re)
    bu_im = jnp.einsum('btgi,gpi->btgp', u, bb_im)
    s_re, s_im = s_re.astype(f32), s_im.astype(f32)
    bu_re = bu_re.at[:, 0].add(ab_re * s_re - ab_im * s_im)
    bu_im = bu_im.at[:, 0].add(ab_re * s_im + ab_im * s_re)
    a_re_t = jnp.broadcast_to(ab_re, bu_re.shape)
    a_im_t = jnp.broadcast_to(ab_im, bu_im.shape)

    def combine(e1, e2):
        a1r, a1i, b1r, b1i = e1
        a2r, a2i, b2r, b2i = e2
        return (a1r * a2r - a1i * a2i, a1r * a2i + a1i * a2r,
                a2r * b1r - a2i * b1i + b2r, a2r * b1i + a2i * b1r + b2i)

    _, _, x_re, x_im = lax.associative_scan(combine, (a_re_t, a_im_t, bu_re, bu_im), axis=1)
    y = (jnp.einsum('gip,btgp->btgi', c_re, x_re) - jnp.einsum('gip,btgp->btgi', c_im, x_im)
         + d_skip.astype(f32) * u).reshape(bsz, t, S5_WIDTH)
    za, zg = jnp.split(jax.nn.gelu(y).astype(h.dtype) @ w_glu, 2, axis=-1)
    return za * jax.nn.sigmoid(zg), x_re[:, -1], x_im[:, -1]

def swiglu(h, w_gate, w_up, w_down):
    return (jax.nn.silu(h @ w_gate) * (h @ w_up)) @ w_down

def moe_swiglu(h, w_router, w_gate, w_up, w_down):
    f32 = jnp.float32
    bsz, t, d = h.shape
    xt = h.reshape(-1, d)
    logits = (xt @ w_router).astype(f32)
    top_v, top_i = lax.top_k(logits, TOP_K)
    wts = jax.nn.softmax(top_v, axis=-1)
    comb = jnp.einsum('tk,tke->te', wts, jax.nn.one_hot(top_i, N_EXPERTS, dtype=f32))
    y = jnp.zeros(xt.shape, f32)
    for e in range(N_EXPERTS):
        he = jax.nn.silu(xt @ w_gate[e]) * (xt @ w_up[e])
        y = y + comb[:, e:e + 1] * (he @ w_down[e])
    return y.astype(h.dtype).reshape(bsz, t, d)

def trunk(x, c, s_gla, s_conv, s_re, s_im, params):
    (w_ada, b_ada, g_norm, w_in0, w_gate_up, b_gate_up, g_head_norm, w_conv, w_out0,
     w_ffn_gate, w_ffn_up, w_ffn_down, w_in1, s5_a_re, s5_a_im, s5_log_dt, s5_b_re, s5_b_im,
     s5_c_re, s5_c_im, s5_d, w_glu, w_router, w_exp_gate, w_exp_up, w_exp_down) = params
    cs = jax.nn.silu(c)
    new_gla, new_conv, new_re, new_im = [], [], [], []
    for layer in range(DEPTH):
        i = layer // 2
        mod = (cs @ w_ada[layer] + b_ada[layer])[:, None, :]
        sh_m, sc_m, gt_m, sh_f, sc_f, gt_f = jnp.split(mod, 6, axis=-1)
        h = rmsnorm(x, g_norm[layer, 0]) * (1 + sc_m) + sh_m
        if layer % 2 == 0:
            o, st_g, st_c = gla_conv_mixer(h, w_in0[i], w_gate_up[i], b_gate_up[i], g_head_norm[i],
                                           w_conv[i], w_out0[i], s_gla[:, i], s_conv[:, i])
            new_gla.append(st_g)
            new_conv.append(st_c)
        else:
            o, st_r, st_i = s5_mixer(h, w_in1[i], s5_a_re[i], s5_a_im[i], s5_log_dt[i], s5_b_re[i],
                                     s5_b_im[i], s5_c_re[i], s5_c_im[i], s5_d[i], w_glu[i],
                                     s_re[:, i], s_im[:, i])
            new_re.append(st_r)
            new_im.append(st_i)
        x = x + gt_m * rmsnorm(o, g_norm[layer, 1])
        h = rmsnorm(x, g_norm[layer, 2]) * (1 + sc_f) + sh_f
        if layer % 2 == 0:
            f = swiglu(h, w_ffn_gate[i], w_ffn_up[i], w_ffn_down[i])
        else:
            f = moe_swiglu(h, w_router[i], w_exp_gate[i], w_exp_up[i], w_exp_down[i])
        x = x + gt_f * rmsnorm(f, g_norm[layer, 3])
    return (x, jnp.stack(new_gla, 1), jnp.stack(new_conv, 1),
            jnp.stack(new_re, 1), jnp.stack(new_im, 1))

def setup_inputs(seed: int = 0) -> dict:
    f32 = jnp.float32
    key = jax.random.key(seed)
    ks = iter(jax.random.split(key, 48))
    nrm = lambda shape, scale: jax.random.normal(next(ks), shape, f32) * scale
    D, G, P = D_MODEL, S5_GROUPS, S5_STATE
    a_im_base = jnp.pi * jnp.arange(P, dtype=f32)[None, None, :]
    return {
        "x_prompt": nrm((BATCH, SEQ, D), 1.0),
        "x_sample": nrm((DEC_BATCH, DEC_SEQ, D), 1.0),
        "c_prompt": nrm((BATCH, D), 1.0),
        "c_sample": nrm((DEC_BATCH, D), 1.0),
        "state_gla": nrm((DEC_BATCH, N_EVEN, GLA_HEADS, GLA_DK, GLA_DV), 1.0),
        "state_conv": nrm((DEC_BATCH, N_EVEN, CONV_K - 1, CONV_CH), 1.0),
        "state_s5_re": nrm((DEC_BATCH, N_ODD, G, P), 0.1),
        "state_s5_im": nrm((DEC_BATCH, N_ODD, G, P), 0.1),
        "w_ada": nrm((DEPTH, D, 6 * D), 0.5 * D ** -0.5),
        "b_ada": nrm((DEPTH, 6 * D), 0.02),
        "g_norm": 1.0 + nrm((DEPTH, 4, D), 0.05),
        "w_in0": nrm((N_EVEN, D, IN0_DIM), D ** -0.5),
        "w_gate_up": nrm((N_EVEN, GLA_LOWRANK, GLA_HEADS * GLA_DK), GLA_LOWRANK ** -0.5),
        "b_gate_up": nrm((N_EVEN, GLA_HEADS * GLA_DK), 0.1),
        "g_head_norm": 1.0 + nrm((N_EVEN, GLA_DV), 0.05),
        "w_conv": nrm((N_EVEN, CONV_K, CONV_CH), CONV_K ** -0.5),
        "w_out0": nrm((N_EVEN, MIX_WIDTH, D), MIX_WIDTH ** -0.5),
        "w_ffn_gate": nrm((N_EVEN, D, D_FF), D ** -0.5),
        "w_ffn_up": nrm((N_EVEN, D, D_FF), D ** -0.5),
        "w_ffn_down": nrm((N_EVEN, D_FF, D), D_FF ** -0.5),
        "w_in1": nrm((N_ODD, D, S5_WIDTH), D ** -0.5),
        "s5_a_re": -0.5 + nrm((N_ODD, G, P), 0.01),
        "s5_a_im": a_im_base + nrm((N_ODD, G, P), 0.01),
        "s5_log_dt": jax.random.uniform(next(ks), (N_ODD, G), f32, math.log(1e-3), math.log(1e-1)),
        "s5_b_re": nrm((N_ODD, G, P, S5_GROUP), (2 * S5_GROUP) ** -0.5),
        "s5_b_im": nrm((N_ODD, G, P, S5_GROUP), (2 * S5_GROUP) ** -0.5),
        "s5_c_re": nrm((N_ODD, G, S5_GROUP, P), (2 * P) ** -0.5),
        "s5_c_im": nrm((N_ODD, G, S5_GROUP, P), (2 * P) ** -0.5),
        "s5_d": nrm((N_ODD, G, S5_GROUP), 1.0),
        "w_glu": nrm((N_ODD, S5_WIDTH, 2 * D), S5_WIDTH ** -0.5),
        "w_router": nrm((N_ODD, D, N_EXPERTS), D ** -0.5),
        "w_exp_gate": nrm((N_ODD, N_EXPERTS, D, D_FF_EXPERT), D ** -0.5),
        "w_exp_up": nrm((N_ODD, N_EXPERTS, D, D_FF_EXPERT), D ** -0.5),
        "w_exp_down": nrm((N_ODD, N_EXPERTS, D_FF_EXPERT, D), D_FF_EXPERT ** -0.5),
    }

def reference(x_prompt, x_sample, c_prompt, c_sample, state_gla, state_conv, state_s5_re,
              state_s5_im, w_ada, b_ada, g_norm, w_in0, w_gate_up, b_gate_up, g_head_norm,
              w_conv, w_out0, w_ffn_gate, w_ffn_up, w_ffn_down, w_in1, s5_a_re, s5_a_im,
              s5_log_dt, s5_b_re, s5_b_im, s5_c_re, s5_c_im, s5_d, w_glu, w_router,
              w_exp_gate, w_exp_up, w_exp_down):
    f32 = jnp.float32
    params = (w_ada, b_ada, g_norm, w_in0, w_gate_up, b_gate_up, g_head_norm, w_conv, w_out0,
              w_ffn_gate, w_ffn_up, w_ffn_down, w_in1, s5_a_re, s5_a_im, s5_log_dt, s5_b_re,
              s5_b_im, s5_c_re, s5_c_im, s5_d, w_glu, w_router, w_exp_gate, w_exp_up, w_exp_down)
    z_gla = jnp.zeros((BATCH, N_EVEN, GLA_HEADS, GLA_DK, GLA_DV), f32)
    z_conv = jnp.zeros((BATCH, N_EVEN, CONV_K - 1, CONV_CH), x_prompt.dtype)
    z_s5 = jnp.zeros((BATCH, N_ODD, S5_GROUPS, S5_STATE), f32)
    y_p, gla_p, conv_p, re_p, im_p = trunk(x_prompt, c_prompt, z_gla, z_conv, z_s5, z_s5, params)
    y_s, gla_s, conv_s, re_s, im_s = trunk(x_sample, c_sample, state_gla, state_conv,
                                           state_s5_re, state_s5_im, params)
    return (y_p, y_s, gla_p, conv_p, re_p, im_p, gla_s, conv_s, re_s, im_s)


_drawn_inputs = setup_inputs


def setup_inputs(seed=0):
    import zlib

    import numpy as np

    out = dict(_drawn_inputs(seed))
    spreads = {}
    factors = {'g_head_norm': 12.291, 's5_a_re': 51.415, 's5_c_im': 3.296, 's5_c_re': 3.779}
    for name, (base, spread) in spreads.items():
        noise = np.random.default_rng([zlib.crc32(name.encode()), seed]).standard_normal(out[name].shape)
        drawn = base * np.exp(spread * noise) if base else spread * noise
        out[name] = __import__('jax').numpy.asarray(drawn.astype(out[name].dtype))
    for name, factor in factors.items():
        out[name] = (out[name] * factor).astype(out[name].dtype)
    return out
```

```python
from contextlib import ExitStack

import numpy as np

import concourse.bass as bass
from concourse import mybir

ALU = mybir.AluOpType
ACT = mybir.ActivationFunctionType
AX = mybir.AxisListType
F32 = mybir.dt.float32
F32R = mybir.dt.float32r
I32 = mybir.dt.int32

P = 128
D = 1024
KT = D // P
TP = 256
NS = 8
T = TP + NS
NC = 1 + NS
H = 4
CH = 64
NCH = TP // CH
LOWRANK = 16
FF = 2816
FT = FF // P
EXPERTS = 8
FFE = 3584
W = 512
NCHK = FFE // W
S5T = 32
EPS = 1e-6
PIECE = KT * W
RING = 3
HALF = PIECE // 2
MAGIC = 12582912.0
TWO_PI = 6.283185
INV_TWO_PI = 0.15915494309189535
HALF_PI = 1.5707963
NO_SLOT = -1000.0
OVER = 4
JOBS = EXPERTS + OVER

Q, K_, V, OG, CH_H, CH_B, CH_C, GLR = 0, 2, 4, 8, 12, 16, 20, 24
N_IN0 = 24
IN0_COLS = [0, 512, 1024, 1552, 2064, 2576]
GLR_COL = 1536

TILES, _n = {}, 0
for _name, _count in (("ada0", 12), ("glr", 1), ("in0", N_IN0), ("ada1a", 4), ("gla", H), ("out0", KT),
                      ("ffn", 2 * FT), ("down", KT), ("in1", KT), ("ada1b", 8), ("glu", 2 * KT)):
    TILES[_name] = _n
    _n += _count
ROWS = ["are", "aim", "dr", "th", "turns", "hi", "lo", "mag", "sin", "cos", "abre", "abim", "den", "fre", "fim", "tmp"]
EXPERT_PIECES = 3 * NCHK


def hybrid_trunk(nc, x_prompt, x_sample, c_prompt, c_sample, state_gla, state_conv, state_s5_re, state_s5_im,
                 w_ada, b_ada, g_norm, w_in0, w_gate_up, b_gate_up, g_head_norm, w_conv, w_out0, w_ffn_gate,
                 w_ffn_up, w_ffn_down, w_in1, s5_a_re, s5_a_im, s5_log_dt, s5_b_re, s5_b_im, s5_c_re, s5_c_im,
                 s5_d, w_glu, w_router, w_exp_gate, w_exp_up, w_exp_down,
                 y_prompt, y_sample, gla_prompt, conv_prompt, s5_re_prompt, s5_im_prompt,
                 gla_sample, conv_sample, s5_re_sample, s5_im_sample):
    with ExitStack() as ctx:
        ctx.enter_context(nc.allow_non_contiguous_dma(reason="small vectors and states"))

        def sb(name, shape, dt=F32):
            return ctx.enter_context(nc.sbuf_tensor(name, shape, dt))

        def sem(name):
            return ctx.enter_context(nc.semaphore(name))

        ring = [sb(f"ring{i}", [P, PIECE]) for i in range(RING)]
        w_hi = [sb(f"w_hi{i}", [P, HALF], F32R) for i in range(3)]
        w_lo = [sb(f"w_lo{i}", [P, HALF], F32R) for i in range(3)]
        parts = sb("parts", [P, 2 * KT * T], F32R)
        xT = sb("xT", [P, KT, T])
        hT = sb("hT", [P, KT, T])
        fT = sb("fT", [P, KT, T])
        sq = sb("sq", [P, KT, T])
        rstd = sb("rstd", [P, T])
        modT = [sb(f"modT{i}", [P, 48, NC]) for i in range(2)]
        coefA = [sb(f"coefA{i}", [P, KT, NC]) for i in range(4)]
        coefG = [sb(f"coefG{i}", [P, KT, NC]) for i in range(4)]
        csT = sb("csT", [P, KT, NC])
        vecA = sb("vecA", [P, 96])
        vecB = sb("vecB", [P, 87])
        convT = sb("convT", [P, 4, 2 * NS])
        router_w = sb("router_w", [P, KT, EXPERTS])
        ident = sb("ident", [P, P])
        ones = sb("ones", [P, P])
        mean_d = sb("mean_d", [P, P])
        modrow = sb("modrow", [NC, W])
        half_rows = sb("half_rows", [P, 2])
        group_rows = sb("group_rows", [P, 8])
        minus_group_rows = sb("minus_group_rows", [P, 8])
        half_pi = sb("half_pi", [P, 1])
        magic = sb("magic", [P, 1])
        minus_magic = sb("minus_magic", [P, 1])
        tabi = sb("tabi", [P, 8], I32)
        ARENA = 12608
        arena = sb("arena", [P, ARENA])
        bank = [ctx.enter_context(nc.psum_tensor(f"bank{i}", [P, W], F32)) for i in range(8)]
        row_bank, ms_bank = bank[5], bank[6]

        def tile_bank(n):
            return bank[0 if TILES["ada1b"] <= n < TILES["glu"] else n % 4]

        def shaped(flat, shape):
            if len(shape) == 2:
                return flat.rearrange("p (a b) -> p a b", b=shape[1])
            if len(shape) == 3:
                return flat.rearrange("p (a b c) -> p a b c", b=shape[1], c=shape[2])
            return flat

        def view(at, *shape, rows=P):
            assert at + int(np.prod(shape)) <= ARENA
            return shaped(arena[0:rows, at:at + int(np.prod(shape))], shape)

        sq_flat = sq[:, :, :].rearrange("p a b -> p (a b)")
        fT_flat = fT[:, :, :].rearrange("p a b -> p (a b)")

        def bview(ap, shape, *dims):
            for d in dims:
                ap = ap.unsqueeze(d)
            return ap.broadcast_to(shape)

        xrow = view(0, 3, D)
        crow = view(3072, D, rows=NC)
        rawA = view(4096, P, rows=96)
        rawB = view(4224, P, rows=87)
        conv_rows = view(4352, 512, rows=2 * NS)
        pT = view(0, 25, T)
        v_tok = view(V * T, 2, W)
        kd_tok = view(8712, 2, TP)
        z_gate = view(6600, 2, T)
        b_cum = view(7128, 2, T)
        attn = view(6600, 2, W)
        head_rstd = view(6600, H, T)
        e_pos = view(8184 - 528, 2, T)
        e_neg = view(8712, 2, T)
        e_dec = view(9240, 2, TP)
        s_chunk = view(9752, NCH, 2, P)
        attn_mask = view(10776, P)
        scan_mask = view(10904, TP)
        ks_tok = view(11160, 256, rows=NS)
        glr_w = view(11416, KT, LOWRANK)
        gate_up_w = view(11544, 256, rows=LOWRANK)
        oT = view(11416, H, T)
        s0 = shaped(fT_flat[:, 0:2 * NS * P], (NS, 2, P))
        spread_v = shaped(sq_flat[0:NS, 0:2 * NS * P], (2, NS, P))
        vs_tok = hT[0:NS, 0:2, :].rearrange("p a b -> p (a b)")[:, 0:512]
        hid = view(0, FT, T)
        silu_g = view(FT * T, 4, T)
        up_c = view((FT + 4) * T, 4, T)

        uT = view(0, KT, T)
        ct = view(2112, 2, 8, P)
        bbt = view(4160, 2, 2, P)
        bb_pad = view(4672, 2, 4 * 32)
        c_pad = view(4928, 2, W)
        xri = [view(at, 2, T) for at in (5952, 6480, 12080)]
        c_raw = view(7920, 2, KT * 64)
        bb = view(8944, 2, W)
        b_raw = view(9968, 2, W)
        s_in = view(9968, 2, NS, S5T)
        s_out = view(9968 + W, 2, NS, S5T)
        cols = view(10992, 8, S5T)
        steps_t = view(11248, TP)
        s_last = view(11504, 2, S5T)
        s_rows = view(11568, 2, TP)
        s5_rows = view(7920, 16, P, rows=S5T)
        log_dt = view(12080, 4, rows=S5T)
        turn = [fT_flat[:, 1024 + TP * i:1024 + TP * i + TP] for i in range(2)]
        tables = [view(7008, 2, TP), shaped(fT_flat[:, 1536:2048], (2, TP)), view(11568, 2, TP)]
        work = [shaped(x, (4, TP)) for x in (sq_flat[:, 0:1024], sq_flat[:, 1024:2048], fT_flat[:, 0:1024])]
        zg_sig = view(5952, 4, T)
        out_rows = view(11568, 2, P, rows=S5T)
        s_out_rows = view(11824, 4, P)
        x_tok = view(0, 3, D)
        def two(at, *shape):
            n = int(np.prod(shape))
            return [shaped(parts[:, at + n * i:at + n * i + n], shape) for i in range(2)]

        xg = two(0, KT, P)
        g_act = view(4096, 2, W)
        h_act = view(5120, 2, W)
        h_t = [two(2048 + 2 * W * i, W) for i in range(2)]
        y_job = view(7168, 2, W)
        pick = view(8192, 3, P)
        pick_w = view(8576, 3, P)
        spread = view(8960, T)
        slots = view(9224, P)
        before = view(9352, P)
        logits_t = view(9480, T, rows=EXPERTS)
        lg = view(9744, 3, EXPERTS)
        sel = view(9768, 3, EXPERTS)
        ex = view(9792, 3, EXPERTS)
        comb = view(9816, 3, EXPERTS)
        slot_of = view(9840, 3, EXPERTS)
        valid = view(9864, 3)
        m_tok = view(9868, 3)
        d_tok = view(9872, 3)
        job_slot = view(9876, 3, JOBS + 1)
        job_w = view(9915, 3, JOBS + 1)
        cmp_a = view(9960, 24, EXPERTS)
        cmp_b = view(10152, 24, EXPERTS)
        earlier = view(10344, EXPERTS, EXPERTS)
        over = view(10408, EXPERTS, 2)
        over_at = view(10424, 16)
        over_pos = view(10440, 16)
        over_hot = view(10456, EXPERTS, 2)
        over_e = view(10472, EXPERTS)
        lot_base = view(10480, 16)
        lot_expert = view(10496, 16)
        over_tmp = view(10512, 16)
        over_base = view(10528, 1)
        tabf = view(10532, 8)
        tmp24 = view(10544, 3, EXPERTS)

        ring_loaded = [sem(f"ring_loaded{i}") for i in range(RING)]
        c_loaded, vec_loaded, x_loaded, small_loaded, s0_loaded = (
            sem(n) for n in ("c_loaded", "vec_loaded", "x_loaded", "small_loaded", "s0_loaded"))
        consts_ready, v_step, p_step, a_step, t_step = (
            sem(n) for n in ("consts_ready", "v_step", "p_step", "a_step", "t_step"))
        start_t, start_copied, cs_ready = (sem(n) for n in ("start_t", "start_copied", "cs_ready"))
        acc_full, acc_free, row_t, mod_ready = (sem(n) for n in ("acc_full", "acc_free", "row_t", "mod_ready"))
        sq_ready, ms_ready, inv_ready, rstd_ready, h_ready, x_ready = (
            sem(n) for n in ("sq_ready", "ms_ready", "inv_ready", "rstd_ready", "h_ready", "x_ready"))
        z_full, z_copied, gate_parts, b_ready, exps_ready, kd_ready, qk_ready = (
            sem(n) for n in ("z_full", "z_copied", "gate_parts", "b_ready", "exps_ready", "kd_ready", "qk_ready"))
        tok_full, tok_copied, att_full, att_masked, ds_full, s_ready = (
            sem(n) for n in ("tok_full", "tok_copied", "att_full", "att_masked", "ds_full", "s_ready"))
        spread_ready, kv_full, kv_added, mixed_o, mixed_y, conv_u = (
            sem(n) for n in ("spread_ready", "kv_full", "kv_added", "mixed_o", "mixed_y", "conv_u"))
        osq_ready, oms_ready, oinv_ready, orstd_ready = (
            sem(n) for n in ("osq_ready", "oms_ready", "oinv_ready", "orstd_ready"))
        s5_loaded, c_raw_loaded, s5_rows_ready, exp_ready, trig_ready, s5_cols_t, s5_cols = (
            sem(n) for n in ("s5_loaded", "c_raw_loaded", "s5_rows_ready", "exp_ready", "trig_ready", "s5_cols_t",
                             "s5_cols"))
        bb_ready, pads_ready, tr_full, tr_copied = (sem(n) for n in ("bb_ready", "pads_ready", "tr_full", "tr_copied"))
        whole_turns, turn_ready, table_ready, bu_full, bu_used, w_ready, z_ready, xre_ready, xim_ready, y_full, y_used = (
            sem(n) for n in ("whole_turns", "turn_ready", "table_ready", "bu_full", "bu_used", "w_ready", "z_ready",
                             "xre_ready", "xim_ready", "y_full", "y_used"))
        last_copied, gelu_ready, s5_t, s5_out, glu_ready, s5_stored = (
            sem(n) for n in ("last_copied", "gelu_ready", "s5_t", "s5_out", "glu_ready", "s5_stored"))
        logits_full, logits_copied, lg_full, xt_full, xt_copied, moe_consts, lg_ready, sel_ready, pos_full, jobs_ready = (
            sem(n) for n in ("logits_full", "logits_copied", "lg_full", "xt_full", "xt_copied", "moe_consts",
                             "lg_ready", "sel_ready", "pos_full", "jobs_ready"))
        first_half_used, hi_ready, lo_ready = (sem(n) for n in ("first_half_used", "hi_ready", "lo_ready"))
        gath_full, xg_hi_ready, xg_lo_ready, gate_full, up_full, g_ready, h_act_ready, ht_full, ht_hi_ready, ht_lo_ready, down_done = (
            sem(n) for n in ("gath_full", "xg_hi_ready", "xg_lo_ready", "gate_full", "up_full", "g_ready", "h_act_ready",
                             "ht_full", "ht_hi_ready", "ht_lo_ready", "down_done"))
        y_ready, pick_ready, pickw_ready, spread_full, spread_copied, back_full, back_added = (
            sem(n) for n in ("y_ready", "pick_ready", "pickw_ready", "spread_full", "spread_copied",
                             "back_full", "back_added"))
        outs_t, outs_copied, y_stored = sem("outs_t"), sem("outs_copied"), sem("y_stored")
        hid_ready, out_done = sem("hid_ready"), sem("out_done")

        def columns(w, c0, n=W):
            return w[:, c0:c0 + n].rearrange("(k p) n -> p k n", p=P), KT, n

        pieces = [columns(w_ada[0], W * i) for i in range(12)]
        pieces += [columns(w_in0[0], c) for c in IN0_COLS]
        pieces += [columns(w_ada[1], W * i) for i in range(4)]
        pieces += [columns(w_out0[0], W * i) for i in range(2)]
        for i in range(0, FF, W):
            n = min(W, FF - i)
            pieces += [columns(w_ffn_gate[0], i, n), columns(w_ffn_up[0], i, n)]
        for i in range(4):
            for half in range(2):
                rows = w_ffn_down[0][half * FF // 2:(half + 1) * FF // 2, 256 * i:256 * i + 256]
                pieces.append((rows.rearrange("(k p) n -> p k n", p=P), FT // 2, 256))
        pieces += [columns(w_in1[0], W * i) for i in range(2)]
        pieces += [columns(w_ada[1], W * i) for i in range(4, 12)]
        for i in range(2):
            pieces += [columns(w_glu[0], W * i), columns(w_glu[0], D + W * i)]

        used = [TILES["ada0"] + i + 1 for i in range(12)] + [TILES["in0"] + 4 * i + 4 for i in range(6)]
        used += [TILES["ada1a"] + i + 1 for i in range(4)] + [TILES["out0"] + 4 * i + 4 for i in range(2)]
        used += [TILES["ffn"] + min(8 * (i // 2) + 8, 2 * FT) for i in range(12)]
        used += [TILES["down"] + 2 * (i // 2) + 2 for i in range(8)] + [TILES["in1"] + 4 * i + 4 for i in range(2)]
        used += [TILES["ada1b"] + i + 1 for i in range(8)] + [TILES["glu"] + 8 * (i // 2) + 8 for i in range(4)]
        assert len(used) == len(pieces)

        def slot(i):
            _, k, n = pieces[i]
            return ring[i % RING][:, 0:k * n].rearrange("p (k n) -> p k n", n=n)

        NPIECES = len(pieces)
        DENSE_HALVES = 0

        kinds = [("gate", 0), ("up", 0)]
        for c in range(1, NCHK):
            kinds += [("gate", c), ("up", c), ("down", c - 1)]
        kinds.append(("down", NCHK - 1))
        released = {"gate": gate_full, "up": up_full, "down": down_done}
        NH = 2 * EXPERT_PIECES

        def expert_slot(m):
            n = D if kinds[m][0] == "down" else W
            return ring[(NPIECES + m) % RING][:, :].rearrange("p (k n) -> p k n", n=n)

        def expert_count(j, m):
            return 16 * (EXPERT_PIECES // RING) * j + 16 * ((NPIECES + m) // RING + 1)

        def half_slot(h):
            return (DENSE_HALVES + h) % 3

        def half_count(j, h):
            return NH * j + DENSE_HALVES + h + 1

        def half_free(eng, j, h):
            kind, c = kinds[h // 2]
            if h % 2 == 0:
                eng.wait_ge(first_half_used, EXPERT_PIECES * j + h // 2 + 1)
            else:
                eng.wait_ge(released[kind], NCHK * j + c + 1)

        def split_hi(act, j, h):
            act.wait_ge(ring_loaded[(NPIECES + h // 2) % RING], expert_count(j, h // 2))
            src = ring[(NPIECES + h // 2) % RING][:, HALF * (h % 2):HALF * (h % 2) + HALF]
            act.activation(w_hi[half_slot(h)][:, :], src, ACT.Copy).then_inc(hi_ready, 1)

        def split_lo(dve, j, h):
            dve.wait_ge(hi_ready, half_count(j, h))
            src = ring[(NPIECES + h // 2) % RING][:, HALF * (h % 2):HALF * (h % 2) + HALF]
            dve.tensor_tensor(w_lo[half_slot(h)][:, :], src, w_hi[half_slot(h)][:, :].bitcast(F32), ALU.subtract)\
                .then_inc(lo_ready, 1)

        def half_after(j, h):
            return (j, h + 3) if h + 3 < NH else (j + 1, h + 3 - NH)

        def for_jobs(eng, body):
            with eng.Fori(0, EXPERTS) as j:
                body(j)
            eng.wait_ge(jobs_ready, 2)
            more = eng.value_load(tabi[0:1, 0:1], min_val=0, max_val=OVER)
            with eng.If(more > 0):
                with eng.Fori(0, more) as k:
                    body(k + EXPERTS)
            return more + EXPERTS

        block = ctx.enter_context(nc.Block())

        @block.sync
        def _(sp):
            for i, (src, k, n) in enumerate(pieces):
                if i >= RING:
                    sp.wait_ge(acc_full, used[i - RING])
                sp.dma_start(slot(i), src).then_inc(ring_loaded[i % RING], 16)

            def load(j, m, e, first=False):
                if not first:
                    sp.wait_ge(lo_ready, half_count(j, 2 * (m - RING) + 1))
                else:
                    sp.wait_ge(acc_full, used[NPIECES - RING + m])
                kind, c = kinds[m]
                if kind == "down":
                    rows = w_exp_down[0].rearrange("e f n -> (e f) n")[bass.ds(e * FFE + W * c, W), :]
                    src = rows.rearrange("(k p) n -> p k n", p=P)
                else:
                    w = w_exp_gate if kind == "gate" else w_exp_up
                    src = w[0][bass.ds(e, 1), :, W * c:W * c + W].rearrange("e (k p) n -> p (e k) n", p=P)
                sp.dma_start(expert_slot(m), src).then_inc(ring_loaded[(NPIECES + m) % RING], 16)

            def job(j, e, after):
                for m in range(RING, EXPERT_PIECES):
                    load(j, m, e)
                for m in range(RING):
                    load(j + 1, m, after)

            def expert_of(n):
                return sp.value_load(tabi[0:1, bass.ds(n + 1, 1)], min_val=0, max_val=EXPERTS - 1)

            for m in range(RING):
                load(0, m, 0, first=True)
            with sp.Fori(0, EXPERTS - 1) as j:
                job(j, j, j + 1)
            sp.wait_ge(jobs_ready, 2)
            more = sp.value_load(tabi[0:1, 0:1], min_val=0, max_val=OVER)
            for m in range(RING, EXPERT_PIECES):
                load(EXPERTS - 1, m, EXPERTS - 1)
            after = expert_of(0)
            for m in range(RING):
                load(EXPERTS, m, after)
            with sp.If(more > 0):
                with sp.Fori(0, more) as k:
                    job(k + EXPERTS, expert_of(k), expert_of(k + 1))
            njobs = more + EXPERTS
            ends = [sp.snap(expert_count(njobs, m)) for m in range(RING)]
            for b in range(3):
                sp.wait_ge(ring_loaded[(NPIECES + b) % RING], ends[b])
                sp.wait_ge(outs_copied, 2 * b + 2)
                if b < 2:
                    sp.dma_start(y_prompt[0, P * b:P * b + P, :], x_tok[:, b, :]).then_inc(y_stored, 16)
                else:
                    sp.dma_start(y_sample[:, 0, :], x_tok[0:NS, b, :]).then_inc(y_stored, 16)
            sp.wait_ge(y_stored, 48)

        @block.gpsimd
        def _(pool):
            count = [0]

            def step(ins):
                count[0] += 1
                ins.then_inc(p_step, 1)
                pool.wait_ge(p_step, count[0])

            step(pool.memset(ident[:, :], 0.0))
            pool.affine_select(out=ident[:, :], in_=ident[:, :], compare_op=ALU.not_equal, fill=1.0, base=0,
                               pattern=[[-1, P]], channel_multiplier=1).then_inc(consts_ready, 1)
            pool.memset(ones[:, :], 1.0)
            pool.memset(mean_d[:, :], 1.0 / D)
            pool.memset(half_pi[:, :], HALF_PI)
            pool.memset(magic[:, :], MAGIC)
            pool.memset(minus_magic[:, :], -MAGIC).then_inc(consts_ready, 1)
            step(pool.memset(attn_mask, 1.0))
            step(pool.affine_select(out=attn_mask, in_=attn_mask, compare_op=ALU.is_ge, fill=0.0, base=0,
                                    pattern=[[1, P]], channel_multiplier=-1))
            step(pool.memset(attn_mask[0:CH, CH:P], 0.0))
            step(pool.memset(scan_mask, 1.0))
            pool.memset(scan_mask.rearrange("p (c t) -> p c t", t=CH)[:, :, 0:1], 0.0).then_inc(consts_ready, 1)
            step(pool.memset(half_rows[:, :], 0.0))
            step(pool.memset(half_rows[0:64, 0:1], 1.0))
            step(pool.memset(half_rows[64:P, 1:2], 1.0))
            for m, v in ((group_rows, 1.0), (minus_group_rows, -1.0)):
                step(pool.memset(m[:, :], v))
                step(pool.affine_select(out=m[:, :], in_=m[:, :], compare_op=ALU.is_ge, fill=0.0, base=0,
                                        pattern=[[-16, 8]], channel_multiplier=1))
                ins = pool.affine_select(out=m[:, :], in_=m[:, :], compare_op=ALU.is_ge, fill=0.0, base=15,
                                         pattern=[[16, 8]], channel_multiplier=-1)
            ins.then_inc(consts_ready, 1)
            pool.dma_start(glr_w, w_in0[0][:, GLR_COL:GLR_COL + LOWRANK].rearrange("(k p) n -> p k n", p=P))\
                .then_inc(small_loaded, 16)
            pool.dma_start(gate_up_w, w_gate_up[0]).then_inc(small_loaded, 16)
            pool.dma_start(router_w[:, :, :], w_router[0].rearrange("(k p) e -> p k e", p=P))\
                .then_inc(small_loaded, 16)
            pool.dma_start(s0, state_gla.rearrange("s n (a h) d v -> (h d) s (n a) v", h=2)).then_inc(s0_loaded, 16)
            pool.wait_ge(acc_free, TILES["in0"] + N_IN0)
            u = pT[:, CH_C:CH_C + 4, :]
            tmp = pT[:, CH_H:CH_H + 4, :]
            y = hT[:, 4:8, :]

            def wc(j, n):
                return bview(vecB[:, 66 + 4 * j:70 + 4 * j], [P, 4, n], 2)

            pool.tensor_tensor(u, u, tmp, ALU.mult).then_inc(conv_u, 1)
            pool.wait_ge(conv_u, 1)
            step(pool.tensor_tensor(y, u, wc(2, T), ALU.mult))
            for j, lag in ((1, 1), (0, 2)):
                step(pool.tensor_tensor(tmp[:, :, 0:TP - lag], u[:, :, 0:TP - lag], wc(j, TP - lag), ALU.mult))
                step(pool.tensor_tensor(y[:, :, lag:TP], y[:, :, lag:TP], tmp[:, :, 0:TP - lag], ALU.add))
                old = convT[:, :, :].rearrange("p k (s j) -> p k s j", j=2)[:, :, :, j]
                step(pool.tensor_tensor(tmp[:, :, TP:T], old, wc(j, NS), ALU.mult))
                step(pool.tensor_tensor(y[:, :, TP:T], y[:, :, TP:T], tmp[:, :, TP:T], ALU.add))
            pool.tensor_tensor(y, y, pT[:, CH_B:CH_B + 4, :], ALU.mult).then_inc(mixed_y, 1)
            n = 0
            for k in range(4):
                pool.dma_start(conv_prompt[0, 0, :, P * k:P * k + P].rearrange("j p -> p j"),
                               u[:, k, TP - 2:TP]).then_inc(out_done, 16)
                pool.dma_start(conv_sample[:, 0, 1, P * k:P * k + P].rearrange("s p -> p s"),
                               u[:, k, TP:T]).then_inc(out_done, 16)
            pool.dma_start(conv_sample[:, 0, 0, :], state_conv[:, 0, 1, :]).then_inc(out_done, 16)
            pool.wait_ge(s_ready, NCH)
            for h in range(2):
                rows = slice(64 * h, 64 * h + 64)
                pool.dma_start(gla_prompt[0, 0].rearrange("(a h) d v -> h d a v", h=2)[h],
                               s_chunk[rows, NCH - 1, :, :]).then_inc(out_done, 16)
            pool.wait_ge(kv_added, 2 * H)
            pool.dma_start(gla_sample.rearrange("s n (a h) d v -> (h d) s (n a) v", h=2), s0).then_inc(out_done, 16)
            pool.wait_ge(out_done, 16 * 12)
            pool.wait_ge(mixed_o, 1)
            for i, src in enumerate((s5_a_re, s5_a_im)):
                pool.dma_start(s5_rows[:, i, :], src[0].rearrange("(t g) p -> t (g p)", g=2)).then_inc(s5_loaded, 16)
            pool.dma_start(log_dt[:, 0:2], s5_log_dt[0].rearrange("(t g) -> t g", g=2)).then_inc(s5_loaded, 16)
            for i, src in enumerate((s5_b_re, s5_b_im)):
                pool.dma_start(b_raw[:, i, :].rearrange("q (t i) -> q t i", i=16),
                               src[0].rearrange("(t g) p i -> (g p) t i", g=2)).then_inc(s5_loaded, 16)
            for i, src in enumerate((state_s5_re, state_s5_im)):
                pool.dma_start(s_rows[:, i, :].rearrange("q (h n) -> q h n", h=2),
                               src.rearrange("(h s) n (t g) p -> (s n t) h (g p)", h=2, g=2)).then_inc(s5_loaded, 16)
            pool.iota(steps_t, pattern=[[1, TP]], base=1, channel_multiplier=0,
                      allow_small_or_imprecise_dtypes=True).then_inc(consts_ready, 1)
            pool.wait_ge(s5_cols, 1)
            for i, src in enumerate((s5_c_re, s5_c_im)):
                pool.dma_start(c_raw[:, i, :].rearrange("q (k p) -> q k p", p=64),
                               src[0].rearrange("(k g) i p -> (g i) k p", g=8)).then_inc(c_raw_loaded, 16)
            pool.wait_ge(c_raw_loaded, 32)
            pool.wait_ge(bb_ready, 1)
            pool.wait_ge(acc_full, TILES["down"] + KT)
            pool.wait_ge(consts_ready, 5)

            def pads(k):
                if k:
                    pool.wait_ge(tr_full, 3 * k)
                for i in range(2):
                    pool.tensor_tensor(bb_pad[:, i, :].rearrange("q (t g i) -> q t g i", g=2, i=16),
                                       bview(bb[:, i, 64 * k:64 * k + 64].rearrange("q (t i) -> q t i", i=16),
                                             [P, 4, 2, 16], 2),
                                       bview(half_rows[:, :], [P, 4, 2, 16], 1, 3), ALU.mult)
                    ins = pool.tensor_tensor(c_pad[:, i, :].rearrange("q (g p) -> q g p", p=64),
                                             bview(c_raw[:, i, 64 * k:64 * k + 64], [P, 8, 64], 1),
                                             bview((group_rows, minus_group_rows)[i][:, :], [P, 8, 64], 2), ALU.mult)
                ins.then_inc(pads_ready, 1)

            def rotate_re(j):
                wk, tb, x = work[j % 3], tables[j % 3], xri[j % 3]
                pool.wait_ge(z_ready, 2 * j + 2)
                pool.tensor_tensor(x[:, 0, 0:TP], tb[:, 0, :], wk[:, 0, :], ALU.mult)
                step(pool.tensor_tensor(wk[:, 1, :], tb[:, 1, :], wk[:, 2, :], ALU.mult))
                pool.tensor_tensor(x[:, 0, 0:TP], x[:, 0, 0:TP], wk[:, 1, :], ALU.subtract).then_inc(xre_ready, 1)

            pads(0)
            for j in range(S5T + 1):
                if j < S5T:
                    wk = work[j % 3]
                    pool.wait_ge(bu_used, j + 1)
                    pool.tensor_tensor(wk[:, 0, :], wk[:, 0, :], wk[:, 1, :], ALU.add)
                    pool.tensor_tensor(wk[:, 2, :], wk[:, 2, :], wk[:, 3, :], ALU.subtract).then_inc(w_ready, 1)
                if j:
                    rotate_re(j - 1)
                if j % 4 == 1 and j // 4 + 1 < KT:
                    pads(j // 4 + 1)
            pool.wait_ge(s5_out, 2)
            for i, (a, b) in enumerate(((s5_re_prompt, s5_re_sample), (s5_im_prompt, s5_im_sample))):
                pool.dma_start(a[0, 0].rearrange("(t g) p -> t (g p)", g=2), out_rows[:, i, :]).then_inc(s5_stored, 16)
                pool.dma_start(b.rearrange("(h s) n (t g) p -> (s n t) h (g p)", h=2, g=2),
                               s_out_rows[:, 2 * i:2 * i + 2, :]).then_inc(s5_stored, 16)
            pool.wait_ge(s5_stored, 64)
            pool.wait_ge(glu_ready, KT)
            pool.iota(slots, pattern=[[1, P]], base=0, channel_multiplier=0, allow_small_or_imprecise_dtypes=True)
            pool.iota(lot_base, pattern=[[0, EXPERTS], [P, 2]], base=P, channel_multiplier=0,
                      allow_small_or_imprecise_dtypes=True)
            pool.iota(lot_expert, pattern=[[1, EXPERTS], [0, 2]], base=0, channel_multiplier=0,
                      allow_small_or_imprecise_dtypes=True)
            pool.memset(y_job, 0.0)
            pool.memset(spread, 0.0)
            pool.memset(x_tok[:, 2, :], 0.0)
            pool.memset(lg[:, 2, :], 0.0)
            pool.memset(valid, 1.0)
            pool.memset(job_slot, NO_SLOT)
            pool.memset(job_w, 0.0)
            pool.memset(before, 1.0)
            step(pool.memset(earlier, 1.0))
            pool.affine_select(out=valid[:, 2:3], in_=valid[:, 2:3], compare_op=ALU.is_gt, fill=0.0, base=NS,
                               pattern=[[0, 1]], channel_multiplier=-1)
            pool.affine_select(out=before, in_=before, compare_op=ALU.is_gt, fill=0.0, base=0,
                               pattern=[[1, P]], channel_multiplier=-1)
            pool.affine_select(out=earlier, in_=earlier, compare_op=ALU.is_gt, fill=0.0, base=0,
                               pattern=[[1, EXPERTS], [-1, EXPERTS]], channel_multiplier=0).then_inc(moe_consts, 1)

        @block.scalar
        def _(act):
            count = [0]
            tile = [0]
            norms = [0]

            def step(ins):
                count[0] += 1
                ins.then_inc(a_step, 1)
                act.wait_ge(a_step, count[0])

            act.dma_start(crow[0:1, :], c_prompt).then_inc(c_loaded, 16)
            act.dma_start(crow[1:NC, :], c_sample).then_inc(c_loaded, 16)
            act.dma_start(rawA, b_ada.rearrange("l (t p) -> (l t) p", p=P)).then_inc(vec_loaded, 16)
            for at, src in ((0, g_norm.rearrange("l j (t p) -> (l j t) p", p=P)),
                            (64, b_gate_up.rearrange("l (t p) -> (l t) p", p=P)),
                            (66, w_conv.rearrange("l j (t p) -> (l j t) p", p=P)),
                            (78, g_head_norm),
                            (79, s5_d.rearrange("l (t g) i -> (l t) (g i)", g=8))):
                act.dma_start(rawB[at:at + src.shape[0], :], src).then_inc(vec_loaded, 16)
            act.dma_start(conv_rows, state_conv.rearrange("s n j c -> (s n j) c")).then_inc(vec_loaded, 16)
            act.dma_start(xrow[:, 0:2, :], x_prompt[0].rearrange("(b p) d -> p b d", p=P)).then_inc(x_loaded, 16)
            act.dma_start(xrow[0:NS, 2, :], x_sample[:, 0, :]).then_inc(x_loaded, 16)

            def evac(out, func=ACT.Copy, rows=P, n=T, **more):
                act.wait_ge(acc_full, tile[0] + 1)
                act.activation(out, tile_bank(tile[0])[0:rows, 0:n], func, **more).then_inc(acc_free, 1)
                tile[0] += 1

            def ada(i):
                if i:
                    act.wait_ge(row_t, i)
                evac(modrow[:, :], rows=NC, n=W)

            def norm(src):
                act.activation(sq[:, :, :], src[:, :, :], ACT.Square).then_inc(sq_ready, 1)
                norms[0] += 1
                act.wait_ge(inv_ready, norms[0])
                act.activation(rstd[:, :], rstd[:, :], ACT.Sqrt).then_inc(rstd_ready, 1)

            def R(name):
                return s5_rows[:, ROWS.index(name), :]

            def last_states(j):
                act.wait_ge(xre_ready, j + 1)
                act.wait_ge(xim_ready, j + 1)
                act.activation(s_last[:, :, j], xri[j % 3][:, :, TP - 1], ACT.Copy)
                act.activation(s_out[:, :, :, j], xri[j % 3][:, :, TP:T], ACT.Copy).then_inc(last_copied, 1)

            act.wait_ge(start_t, 1)
            act.activation(csT[:, :, :].rearrange("p k c -> p (k c)"), bank[4][:, 0:KT * NC], ACT.Silu)\
                .then_inc(cs_ready, 1)
            for i in range(12):
                ada(i)
            act.wait_ge(x_ready, 1)
            norm(xT)
            evac(pT[0:LOWRANK, GLR, :], rows=LOWRANK)
            for t in range(N_IN0):
                if t < K_:
                    evac(pT[:, t, :], scale=0.125)
                elif OG <= t < CH_H:
                    evac(pT[:, t, :], ACT.Silu)
                else:
                    evac(pT[:, t, :])
            for a in range(2):
                act.wait_ge(z_full, a + 1)
                act.activation(e_pos[:, a, :], bank[6 + a][:, 0:T], ACT.Identity, bias=vecB[:, 64 + a:65 + a])\
                    .then_inc(z_copied, 1)
            act.wait_ge(z_copied, 2)
            step(act.activation(e_neg, e_pos, ACT.Abs))
            step(act.activation(e_neg, e_neg, ACT.Exp, scale=-1.0))
            act.activation(e_neg, e_neg, ACT.Ln, bias=1.0).then_inc(gate_parts, 1)
            act.wait_ge(b_ready, 1)
            act.activation(e_pos, b_cum, ACT.Exp, scale=1.0 / 16)
            act.activation(e_neg, b_cum, ACT.Exp, scale=-1.0 / 16)
            act.wait_ge(b_ready, 2)
            act.activation(e_dec, e_dec, ACT.Exp, scale=1.0 / 16).then_inc(exps_ready, 1)
            for i in range(4):
                ada(12 + i)
            for h in range(H):
                evac(oT[:, h, :])
            act.wait_ge(acc_free, TILES["gla"] + H)
            act.activation(sq_flat[:, 0:H * T], oT.rearrange("p h t -> p (h t)"), ACT.Square).then_inc(osq_ready, 1)
            act.wait_ge(oinv_ready, 1)
            act.activation(head_rstd, head_rstd, ACT.Sqrt).then_inc(orstd_ready, 1)
            act.wait_ge(kv_added, 2 * H)
            act.wait_ge(out_done, 16 * 12)
            for t in range(KT):
                evac(fT[:, t, :])
            act.wait_ge(acc_free, TILES["out0"] + KT)
            norm(fT)
            act.wait_ge(x_ready, 2)
            norm(xT)
            for t in range(FT):
                if t >= 4:
                    act.wait_ge(hid_ready, t - 3)
                evac(silu_g[:, t % 4, :], ACT.Silu)
                evac(up_c[:, t % 4, :])
                if t == 8:
                    act.wait_ge(s5_loaded, 16 * 7)
                    act.activation(log_dt[:, 2:4], log_dt[:, 0:2], ACT.Exp).then_inc(exp_ready, 1)
                    act.wait_ge(s5_rows_ready, 1)
                    act.activation(R("mag"), R("dr"), ACT.Exp).then_inc(exp_ready, 1)
                    act.wait_ge(s5_rows_ready, 2)
                    act.activation(R("sin"), R("turns"), ACT.Sin, scale=TWO_PI)
                    step(act.activation(R("cos"), R("turns"), ACT.Abs))
                    act.activation(R("cos"), R("cos"), ACT.Sin, scale=-TWO_PI, bias=half_pi[0:S5T, :])\
                        .then_inc(trig_ready, 1)
            for t in range(KT):
                evac(fT[:, t, :])
            act.wait_ge(acc_free, TILES["down"] + KT)
            norm(fT)
            act.wait_ge(x_ready, 3)
            norm(xT)
            for t in range(KT):
                evac(uT[:, t, :])

            def copies(k):
                for n in range(3):
                    act.wait_ge(tr_full, 3 * k + n + 1)
                    if n == 0:
                        out = bbt[:, k % 2, :, :].rearrange("q a b -> q (a b)")
                    else:
                        out = ct[:, k % 2, 4 * n - 4:4 * n, :].rearrange("q a b -> q (a b)")
                    act.activation(out, bank[7][:, 0:out.shape[1]], ACT.Copy).then_inc(tr_copied, 1)

            def whole(j):
                if j >= 2:
                    act.wait_ge(table_ready, j - 1)
                step(act.activation(turn[j % 2], steps_t, ACT.Identity, scale=cols[:, 5, j:j + 1], bias=magic[:, :]))
                act.activation(turn[j % 2], turn[j % 2], ACT.Identity, bias=minus_magic[:, :])\
                    .then_inc(whole_turns, 1)

            def table(j):
                act.wait_ge(turn_ready, j + 1)
                if j >= 3:
                    act.wait_ge(xre_ready, j - 2)
                    act.wait_ge(xim_ready, j - 2)
                tb = tables[j % 3]
                step(act.activation(tb[:, 0, :], turn[j % 2], ACT.Abs))
                act.activation(tb[:, 0, :], tb[:, 0, :], ACT.Sin, scale=-TWO_PI, bias=half_pi[:, :])
                act.activation(tb[:, 1, :], turn[j % 2], ACT.Sin, scale=TWO_PI).then_inc(table_ready, 1)

            act.wait_ge(h_ready, 3)
            act.wait_ge(s5_cols, 1)
            act.wait_ge(consts_ready, 5)
            act.wait_ge(s5_cols, 2)
            copies(0)
            whole(0)
            whole(1)
            table(0)
            whole(2)
            for j in range(S5T):
                if j + 1 < S5T:
                    table(j + 1)
                if j + 3 < S5T:
                    whole(j + 3)
                if j >= 2:
                    last_states(j - 2)
                if j % 4 == 2 and j // 4 + 1 < KT:
                    copies(j // 4 + 1)
                if j % 4 == 3:
                    ada(16 + j // 4)
            last_states(S5T - 2)
            last_states(S5T - 1)
            act.wait_ge(y_used, KT)
            act.activation(hT[:, :, :], hT[:, :, :], ACT.Gelu_apprx_tanh).then_inc(gelu_ready, 1)
            for i in range(2):
                act.wait_ge(s5_t, i + 1)
                if i == 0:
                    act.activation(out_rows.rearrange("q a b -> q (a b)"), bank[1][0:S5T, 0:256], ACT.Copy)\
                        .then_inc(s5_out, 1)
                else:
                    act.activation(s_out_rows.rearrange("q a b -> q (a b)"), bank[2][:, :], ACT.Copy)\
                        .then_inc(s5_out, 1)
            for t in range(KT):
                evac(fT[:, t, :])
                if t >= 4:
                    act.wait_ge(glu_ready, t - 3)
                evac(zg_sig[:, t % 4, :], ACT.Sigmoid)
            act.wait_ge(glu_ready, KT)
            norm(fT)
            act.wait_ge(x_ready, 4)
            norm(xT)
            act.wait_ge(logits_full, 1)
            act.activation(logits_t, bank[7][0:EXPERTS, 0:T], ACT.Copy).then_inc(logits_copied, 1)
            for n in range(6):
                rows = P if n < 4 else NS
                act.wait_ge(xt_full, n + 1)
                if n >= 4:
                    act.wait_ge(moe_consts, 1)
                act.activation(x_tok[0:rows, n // 2, W * (n % 2):W * (n % 2) + W], bank[n % 4][0:rows, :], ACT.Copy)\
                    .then_inc(xt_copied, 1)
            act.wait_ge(lg_ready, 1)
            act.activation(ex, ex, ACT.Exp).then_inc(lg_ready, 1)

            def xg_hi(j):
                for half in range(2):
                    act.wait_ge(gath_full, 2 * j + half + 1)
                    act.activation(xg[0][:, 4 * half:4 * half + 4, :].rearrange("q a b -> q (a b)"),
                                   bank[7 if half == 0 else 2][:, :], ACT.Copy).then_inc(xg_hi_ready, 1)

            for h in range(3):
                split_hi(act, 0, h)
            xg_hi(0)

            def job(j):
                def ht_hi(c):
                    act.wait_ge(ht_full, NCHK * j + c + 1)
                    act.activation(h_t[c % 2][0], bank[6][:, :], ACT.Copy).then_inc(ht_hi_ready, 1)

                for m, (kind, c) in enumerate(kinds):
                    for h in (2 * m, 2 * m + 1):
                        half_free(act, j, h)
                        split_hi(act, *half_after(j, h))
                    if kind == "gate":
                        if c >= 2:
                            act.wait_ge(h_act_ready, NCHK * j + c - 1)
                        act.activation(g_act[:, c % 2, :], bank[2 * (c % 2)][:, :], ACT.Silu).then_inc(g_ready, 1)
                        if c:
                            ht_hi(c - 1)
                    if (kind, c) == ("down", NCHK - 2):
                        xg_hi(j + 1)
                        ht_hi(NCHK - 1)
                for half in range(2):
                    ins = act.activation(y_job[:, half, :], bank[4 + half][:, :], ACT.Copy)
                ins.then_inc(y_ready, 1)

            njobs = for_jobs(act, job)
            act.wait_ge(back_added, KT * njobs + KT)
            norm(fT)

        @block.vector
        def _(dve):
            count = [0]
            norms = [0]

            def step(ins):
                count[0] += 1
                ins.then_inc(v_step, 1)
                dve.wait_ge(v_step, count[0])

            def mod_rows(i):
                l, j = divmod(i, 12)
                dve.wait_ge(row_t, i + 1)
                rows = row_bank[:, 36 * (i % 2):36 * (i % 2) + 36].rearrange("p (t c) -> p t c", c=NC)
                b = vecA[:, 48 * l + 4 * j:48 * l + 4 * j + 4]
                dve.tensor_tensor(modT[l][:, 4 * j:4 * j + 4, :], rows, bview(b, [P, 4, NC], 2), ALU.add)\
                    .then_inc(mod_ready, 1)

            def coefs(l, part, which):
                g = [bview(vecB[:, (4 * l + 2 * part + j) * KT:(4 * l + 2 * part + j + 1) * KT], [P, KT, NC], 2)
                     for j in range(2)]
                at = 24 * part
                if which == "pre":
                    step(dve.scalar_tensor_tensor(out=coefA[2 * l + part][:, :, :], in0=modT[l][:, at + 8:at + 16, :],
                                                  scalar=1.0, in1=g[0], op0=ALU.add, op1=ALU.mult))
                else:
                    step(dve.tensor_tensor(coefG[2 * l + part][:, :, :], modT[l][:, at + 16:at + 24, :], g[1],
                                           ALU.mult))

            def inverse():
                norms[0] += 1
                dve.wait_ge(ms_ready, norms[0])
                step(dve.tensor_scalar(rstd[:, :], ms_bank[:, 0:T], EPS, None, ALU.add))
                dve.reciprocal(rstd[:, :], rstd[:, :]).then_inc(inv_ready, 1)
                dve.wait_ge(rstd_ready, norms[0])

            def pre(l, part):
                inverse()
                A, B = coefA[2 * l + part], modT[l][:, 24 * part:24 * part + 8, :]
                step(dve.tensor_tensor(sq[:, :, :], xT[:, :, :], bview(rstd[:, :], [P, KT, T], 1), ALU.mult))
                for k in range(KT):
                    dve.tensor_scalar(hT[:, k, 0:TP], sq[:, k, 0:TP], A[:, k, 0:1], B[:, k, 0:1], ALU.mult, ALU.add)
                step(dve.tensor_tensor(hT[:, :, TP:T], sq[:, :, TP:T], A[:, :, 1:NC], ALU.mult))
                dve.tensor_tensor(hT[:, :, TP:T], hT[:, :, TP:T], B[:, :, 1:NC], ALU.add).then_inc(h_ready, 1)

            def post(l, part):
                inverse()
                G = coefG[2 * l + part]
                step(dve.tensor_tensor(sq[:, :, :], fT[:, :, :], bview(rstd[:, :], [P, KT, T], 1), ALU.mult))
                for k in range(KT):
                    dve.scalar_tensor_tensor(out=xT[:, k, 0:TP], in0=sq[:, k, 0:TP], scalar=G[:, k, 0:1],
                                             in1=xT[:, k, 0:TP], op0=ALU.mult, op1=ALU.add)
                step(dve.tensor_tensor(sq[:, :, TP:T], sq[:, :, TP:T], G[:, :, 1:NC], ALU.mult))
                dve.tensor_tensor(xT[:, :, TP:T], xT[:, :, TP:T], sq[:, :, TP:T], ALU.add).then_inc(x_ready, 1)

            dve.wait_ge(start_t, 2)
            dve.tensor_copy(vecA[:, :], bank[7][:, 96:192])
            dve.tensor_copy(vecB[:, :], bank[7][:, 192:279])
            dve.tensor_copy(convT[:, :, :].rearrange("p k r -> p (k r)"), bank[7][:, 288:352]).then_inc(start_copied, 1)
            for k in range(KT):
                dve.wait_ge(start_t, 3 + k)
                ins = dve.tensor_copy(xT[:, k, :], bank[(6, 4)[k % 2]][:, 0:T])
                ins.then_inc(start_copied, 1)
            dve.wait_ge(start_copied, 1 + KT)
            dve.engine_nop().then_inc(x_ready, 1)
            for i in range(12):
                mod_rows(i)
            dve.wait_ge(mod_ready, 12)
            for part in range(2):
                coefs(0, part, "pre")
                coefs(0, part, "post")
            pre(0, 0)
            dve.wait_ge(gate_parts, 1)
            step(dve.scalar_tensor_tensor(out=z_gate, in0=e_pos, scalar=0.0, in1=e_neg, op0=ALU.min, op1=ALU.subtract))
            dve.wait_ge(consts_ready, 3)
            for a in range(2):
                dve.tensor_tensor_scan(b_cum[:, a, 0:TP], scan_mask, z_gate[:, a, 0:TP], 0.0, ALU.mult, ALU.add)
            dve.tensor_copy(b_cum[:, :, TP:T], z_gate[:, :, TP:T]).then_inc(b_ready, 1)
            dve.wait_ge(b_ready, 1)
            for a in range(2):
                b4 = b_cum[:, a, 0:TP].rearrange("p (c t) -> p c t", t=CH)
                ins = dve.tensor_tensor(e_dec[:, a, :].rearrange("p (c t) -> p c t", t=CH),
                                        b4[:, :, CH - 1:CH].broadcast_to([P, NCH, CH]), b4, ALU.subtract)
            ins.then_inc(b_ready, 1)
            dve.wait_ge(exps_ready, 1)
            dve.tensor_tensor(e_dec, pT[:, K_:K_ + 2, 0:TP], e_dec, ALU.mult).then_inc(kd_ready, 1)
            dve.tensor_tensor(pT[:, Q:Q + 2, 0:TP], pT[:, Q:Q + 2, 0:TP], e_pos[:, :, 0:TP], ALU.mult)
            dve.tensor_tensor(pT[:, K_:K_ + 2, 0:TP], pT[:, K_:K_ + 2, 0:TP], e_neg[:, :, 0:TP], ALU.mult)\
                .then_inc(qk_ready, 1)
            dve.wait_ge(tok_full, 3)
            dve.tensor_copy(v_tok[:, 0, :], bank[6][:, :]).then_inc(tok_copied, 1)
            dve.tensor_copy(v_tok[:, 1, :], bank[7][:, :]).then_inc(tok_copied, 1)
            dve.tensor_copy(vs_tok, bank[4][0:NS, :]).then_inc(tok_copied, 1)
            mod_rows(12)
            dve.wait_ge(tok_full, 4)
            dve.tensor_copy(ks_tok, bank[6][0:NS, 0:256]).then_inc(tok_copied, 1)
            dve.wait_ge(qk_ready, 1)
            dve.wait_ge(tok_full, 5)
            dve.tensor_copy(kd_tok.rearrange("p b n -> p (b n)"), bank[7][:, :]).then_inc(tok_copied, 1)
            for b in range(2):
                dve.wait_ge(att_full, b + 1)
                dve.tensor_tensor(attn[:, b, :].rearrange("p (h i) -> p h i", i=P),
                                  bank[6 + b][:, :].rearrange("p (h i) -> p h i", i=P),
                                  bview(attn_mask, [P, H, P], 1), ALU.mult).then_inc(att_masked, 1)
            for c in range(NCH):
                src = bank[(4, 6, 7, 4)[c]]
                dve.wait_ge(ds_full, c + 1)
                if c:
                    dve.wait_ge(s_ready, c)
                for h in range(H):
                    rows, a = slice(64 * (h % 2), 64 * (h % 2) + 64), h // 2
                    new, add = s_chunk[rows, c, a, :], src[rows, P * h:P * h + P]
                    if c == 0:
                        ins = dve.tensor_copy(new, add)
                    else:
                        last = CH * c + CH - 1
                        ins = dve.scalar_tensor_tensor(out=new, in0=s_chunk[rows, c - 1, a, :],
                                                       scalar=e_pos[rows, a, last:last + 1], in1=add,
                                                       op0=ALU.mult, op1=ALU.add)
                ins.then_inc(s_ready, 1)
            for i in range(1, 4):
                mod_rows(12 + i)
            dve.wait_ge(s0_loaded, 16)
            alpha = e_pos[:, :, TP:T].rearrange("p a s -> p s a")
            step(dve.tensor_tensor(s0, s0, bview(alpha, [P, NS, 2, P], 3), ALU.mult))
            for h in range(H):
                if h >= 2:
                    dve.wait_ge(kv_full, 2 * h - 2)
                dve.wait_ge(tok_copied, 3)
                dve.tensor_tensor(spread_v[:, h % 2, :, :], bview(vs_tok[:, P * h:P * h + P], [NS, NS, P], 1),
                                  bview(ident[0:NS, 0:NS], [NS, NS, P], 2), ALU.mult).then_inc(spread_ready, 1)
                for u in range(2):
                    n = 2 * h + u
                    dve.wait_ge(kv_full, n + 1)
                    rows = slice(64 * (h % 2), 64 * (h % 2) + 64)
                    part = s0[rows, 4 * u:4 * u + 4, h // 2, :]
                    dve.tensor_tensor(part, part, bank[(6, 7, 4)[n % 3]][rows, :].rearrange("p (s v) -> p s v", v=P),
                                      ALU.add).then_inc(kv_added, 1)
            dve.wait_ge(oms_ready, 1)
            for h in range(H):
                src = bank[5][:, 128:128 + T] if h == 3 else bank[(6, 7, 4)[h]][:, 0:T]
                ins = dve.tensor_scalar(head_rstd[:, h, :], src, 1.0 / P, EPS, ALU.mult, ALU.add)
            step(ins)
            dve.reciprocal(head_rstd, head_rstd).then_inc(oinv_ready, 1)
            dve.wait_ge(orstd_ready, 1)
            step(dve.tensor_tensor(oT, oT, head_rstd, ALU.mult))
            dve.scalar_tensor_tensor(out=hT[:, 0:H, :], in0=oT, scalar=vecB[:, 78:79], in1=pT[:, OG:OG + 4, :],
                                     op0=ALU.mult, op1=ALU.mult).then_inc(mixed_o, 1)
            post(0, 0)
            dve.wait_ge(x_ready, 2)
            pre(0, 1)

            def R(name):
                return s5_rows[:, ROWS.index(name), :]

            def prepare(part):
                V = dve
                if part == 0:
                    V.wait_ge(exp_ready, 1)
                    dt = bview(log_dt[:, 2:4], [S5T, 2, 64], 2)
                    wide = lambda name: R(name).rearrange("q (g p) -> q g p", p=64)
                    V.tensor_tensor(wide("dr"), wide("are"), dt, ALU.mult).then_inc(s5_rows_ready, 1)
                    step(V.tensor_tensor(wide("th"), wide("aim"), dt, ALU.mult))
                    step(V.tensor_scalar(R("th"), R("th"), INV_TWO_PI, None, ALU.mult))
                    step(V.tensor_scalar(R("tmp"), R("th"), MAGIC, MAGIC, ALU.add, ALU.subtract))
                    step(V.tensor_tensor(R("turns"), R("th"), R("tmp"), ALU.subtract))
                    step(V.tensor_scalar(R("hi"), R("turns"), 3072.0, 3072.0, ALU.add, ALU.subtract))
                    V.tensor_tensor(R("lo"), R("turns"), R("hi"), ALU.subtract).then_inc(s5_rows_ready, 1)
                    V.tensor_tensor(R("den"), R("are"), R("are"), ALU.mult)
                    step(V.tensor_tensor(R("tmp"), R("aim"), R("aim"), ALU.mult))
                    step(V.tensor_tensor(R("den"), R("den"), R("tmp"), ALU.add))
                    step(V.reciprocal(R("den"), R("den")))
                else:
                    V.wait_ge(trig_ready, 1)
                    V.wait_ge(exp_ready, 2)
                    V.tensor_tensor(R("abre"), R("mag"), R("cos"), ALU.mult)
                    step(V.tensor_tensor(R("abim"), R("mag"), R("sin"), ALU.mult))
                    step(V.tensor_scalar(R("cos"), R("abre"), -1.0, None, ALU.add))
                    V.tensor_tensor(R("fre"), R("cos"), R("are"), ALU.mult)
                    step(V.tensor_tensor(R("tmp"), R("abim"), R("aim"), ALU.mult))
                    step(V.tensor_tensor(R("fre"), R("fre"), R("tmp"), ALU.add))
                    V.tensor_tensor(R("fim"), R("abim"), R("are"), ALU.mult)
                    step(V.tensor_tensor(R("tmp"), R("cos"), R("aim"), ALU.mult))
                    step(V.tensor_tensor(R("fim"), R("fim"), R("tmp"), ALU.subtract))
                    V.tensor_tensor(R("fre"), R("fre"), R("den"), ALU.mult)
                    V.tensor_tensor(R("fim"), R("fim"), R("den"), ALU.mult).then_inc(s5_rows_ready, 1)

            for t in range(FT):
                dve.wait_ge(acc_free, TILES["ffn"] + 2 * t + 2)
                dve.tensor_tensor(hid[:, t, :], silu_g[:, t % 4, :], up_c[:, t % 4, :], ALU.mult).then_inc(hid_ready, 1)
                if t == 8:
                    prepare(0)
                if t == 12:
                    prepare(1)
            dve.wait_ge(s5_cols_t, 1)
            dve.tensor_copy(cols.rearrange("q a b -> q (a b)"), bank[7][:, 0:256]).then_inc(s5_cols, 1)
            dve.wait_ge(s5_cols, 1)
            f = [bview(cols[:, 3 + i, :], [P, S5T, 16], 2) for i in range(2)]
            raw = [b_raw[:, i, :].rearrange("q (t i) -> q t i", i=16) for i in range(2)]
            new = [bb[:, i, :].rearrange("q (t i) -> q t i", i=16) for i in range(2)]
            dve.tensor_tensor(new[0], f[0], raw[0], ALU.mult)
            step(dve.tensor_tensor(new[1], f[0], raw[1], ALU.mult))
            dve.tensor_tensor(raw[0], f[1], raw[0], ALU.mult)
            step(dve.tensor_tensor(raw[1], f[1], raw[1], ALU.mult))
            dve.tensor_tensor(new[0], new[0], raw[1], ALU.subtract)
            dve.tensor_tensor(new[1], new[1], raw[0], ALU.add).then_inc(bb_ready, 1)
            dve.wait_ge(bb_ready, 1)
            dve.wait_ge(s5_cols_t, 2)
            ab = [bview(cols[:, 1 + i, :], [P, NS, S5T], 1) for i in range(2)]
            st = [bank[4][:, 256 * i:256 * i + 256].rearrange("q (s t) -> q s t", t=S5T) for i in range(2)]
            dve.tensor_tensor(s_in[:, 0, :, :], ab[0], st[0], ALU.mult)
            dve.tensor_tensor(s_in[:, 1, :, :], ab[0], st[1], ALU.mult)
            dve.tensor_tensor(s_out[:, 0, :, :], ab[1], st[1], ALU.mult)
            step(dve.tensor_tensor(s_out[:, 1, :, :], ab[1], st[0], ALU.mult))
            dve.tensor_tensor(s_in[:, 0, :, :], s_in[:, 0, :, :], s_out[:, 0, :, :], ALU.subtract)
            dve.tensor_tensor(s_in[:, 1, :, :], s_in[:, 1, :, :], s_out[:, 1, :, :], ALU.add).then_inc(s5_cols, 1)
            post(0, 1)
            dve.wait_ge(mod_ready, 16)
            coefs(1, 0, "pre")
            dve.wait_ge(x_ready, 3)
            pre(1, 0)
            dve.wait_ge(s5_cols, 2)

            def rest(j):
                dve.wait_ge(whole_turns, j + 1)
                t = turn[j % 2]
                step(dve.scalar_tensor_tensor(out=t, in0=steps_t, scalar=cols[:, 6, j:j + 1], in1=t,
                                              op0=ALU.mult, op1=ALU.subtract))
                dve.scalar_tensor_tensor(out=t, in0=steps_t, scalar=cols[:, 7, j:j + 1], in1=t,
                                         op0=ALU.mult, op1=ALU.add).then_inc(turn_ready, 1)

            def turn_back(j):
                wk, tb = work[j % 3], tables[j % 3]
                re, im = bank[1 + 2 * (j % 2)], bank[2 + 2 * (j % 2)]
                dve.wait_ge(table_ready, j + 1)
                dve.wait_ge(bu_full, j + 1)
                if j >= 3:
                    dve.wait_ge(y_full, j - 2)
                    dve.wait_ge(last_copied, j - 2)
                    dve.wait_ge(xre_ready, j - 2)
                dve.tensor_tensor(wk[:, 0, :], tb[:, 0, :], re[:, 0:TP], ALU.mult)
                dve.tensor_tensor(wk[:, 1, :], tb[:, 1, :], im[:, 0:TP], ALU.mult)
                dve.tensor_tensor(wk[:, 2, :], tb[:, 0, :], im[:, 0:TP], ALU.mult)
                dve.tensor_tensor(wk[:, 3, :], tb[:, 1, :], re[:, 0:TP], ALU.mult)
                dve.tensor_tensor(xri[j % 3][:, 0, TP:T], s_in[:, 0, :, j], re[:, TP:T], ALU.add)
                dve.tensor_tensor(xri[j % 3][:, 1, TP:T], s_in[:, 1, :, j], im[:, TP:T], ALU.add).then_inc(bu_used, 1)

            def scans(j):
                wk = work[j % 3]
                dve.wait_ge(w_ready, j + 1)
                for i in (0, 2):
                    dve.tensor_tensor_scan(wk[:, i, :], cols[:, 0, j:j + 1].broadcast_to([P, TP]), wk[:, i, :], 0.0,
                                           ALU.mult, ALU.add).then_inc(z_ready, 1)

            def rotate_im(j):
                wk, tb, x = work[j % 3], tables[j % 3], xri[j % 3]
                dve.wait_ge(z_ready, 2 * j + 2)
                dve.tensor_tensor(x[:, 1, 0:TP], tb[:, 1, :], wk[:, 0, :], ALU.mult)
                step(dve.tensor_tensor(wk[:, 3, :], tb[:, 0, :], wk[:, 2, :], ALU.mult))
                dve.tensor_tensor(x[:, 1, 0:TP], x[:, 1, 0:TP], wk[:, 3, :], ALU.add).then_inc(xim_ready, 1)

            def s5_y(k):
                dve.wait_ge(y_full, 4 * k + 4)
                dve.scalar_tensor_tensor(out=hT[:, k, :], in0=uT[:, k, :], scalar=vecB[:, 79 + k:80 + k],
                                         in1=bank[6][:, 0:T], op0=ALU.mult, op1=ALU.add).then_inc(y_used, 1)

            rest(0)
            rest(1)
            for j in range(S5T + 1):
                if j < S5T:
                    turn_back(j)
                if j:
                    scans(j - 1)
                if j + 2 < S5T:
                    rest(j + 2)
                if j:
                    rotate_im(j - 1)
                if j >= 6 and j % 4 == 2:
                    s5_y(j // 4 - 1)
                if j % 4 == 1 and j >= 9:
                    mod_rows(14 + j // 4)
            s5_y(KT - 1)
            mod_rows(22)
            mod_rows(23)
            dve.wait_ge(mod_ready, 24)
            coefs(1, 0, "post")
            coefs(1, 1, "pre")
            coefs(1, 1, "post")
            for t in range(KT):
                dve.wait_ge(acc_free, TILES["glu"] + 2 * t + 2)
                dve.tensor_tensor(fT[:, t, :], fT[:, t, :], zg_sig[:, t % 4, :], ALU.mult).then_inc(glu_ready, 1)
            post(1, 0)
            dve.wait_ge(x_ready, 4)
            pre(1, 1)
            dve.memset(fT[:, :, :], 0.0)
            dve.wait_ge(moe_consts, 1)
            dve.wait_ge(lg_full, 1)
            dve.tensor_copy(lg[:, 0:2, :], bank[7][:, 0:16].rearrange("q (b e) -> q b e", e=EXPERTS))
            step(dve.tensor_copy(lg[0:NS, 2, :], bank[7][0:NS, 16:24]))
            by_e = lambda x: x.rearrange("q (b e) f -> q b e f", e=EXPERTS)
            mine, other = bview(lg, [P, 3, EXPERTS, EXPERTS], 3), bview(lg, [P, 3, EXPERTS, EXPERTS], 2)
            dve.tensor_reduce(m_tok, lg, AX.X, ALU.max)
            dve.tensor_tensor(by_e(cmp_a), other, mine, ALU.is_gt)
            step(dve.tensor_tensor(by_e(cmp_b), other, mine, ALU.is_equal))
            dve.tensor_tensor(ex, lg, bview(m_tok, [P, 3, EXPERTS], 2), ALU.subtract).then_inc(lg_ready, 1)
            step(dve.tensor_tensor(by_e(cmp_b), by_e(cmp_b), bview(earlier, [P, 3, EXPERTS, EXPERTS], 1), ALU.mult))
            step(dve.tensor_tensor(cmp_a, cmp_a, cmp_b, ALU.add))
            step(dve.tensor_reduce(slot_of.rearrange("q b e -> q (b e)"), cmp_a, AX.X, ALU.add))
            step(dve.tensor_scalar(sel, slot_of, 1.5, None, ALU.is_lt))
            dve.wait_ge(lg_ready, 2)
            step(dve.tensor_tensor(comb, ex, sel, ALU.mult))
            step(dve.tensor_tensor(sel, sel, bview(valid, [P, 3, EXPERTS], 2), ALU.mult))
            dve.tensor_reduce(d_tok, comb, AX.X, ALU.add).then_inc(sel_ready, 1)
            dve.wait_ge(sel_ready, 1)
            step(dve.reciprocal(d_tok, d_tok))
            step(dve.tensor_tensor(d_tok, d_tok, valid, ALU.mult))
            step(dve.tensor_tensor(comb, comb, bview(d_tok, [P, 3, EXPERTS], 2), ALU.mult))
            dve.tensor_copy(job_w[:, :, 0:EXPERTS], comb)
            dve.wait_ge(pos_full, 1)
            pos = bank[7][:, 0:24].rearrange("q (b e) -> q b e", e=EXPERTS)
            step(dve.scalar_tensor_tensor(out=slot_of, in0=pos, scalar=-NO_SLOT, in1=sel, op0=ALU.add, op1=ALU.mult))
            step(dve.tensor_scalar(slot_of, slot_of, NO_SLOT, None, ALU.add))
            step(dve.tensor_copy(job_slot[:, :, 0:EXPERTS], slot_of))

            def picks(j):
                for b in range(3):
                    ins = dve.tensor_scalar(pick[:, b, :], slots, job_slot[:, b, bass.ds(j, 1)], None, ALU.is_equal)
                ins.then_inc(pick_ready, 1)

            picks(0)
            for i in range(2):
                ins = dve.tensor_scalar(over[:, :, i], bank[7][:, 24:32], float(P * (i + 1)), None, ALU.is_gt)
            step(ins)
            over_f = over.rearrange("q e b -> q (e b)")
            hot_f = over_hot.rearrange("q e b -> q (e b)")
            step(dve.tensor_tensor_scan(over_pos, ones[:, 0:16], over_f, 0.0, ALU.mult, ALU.add))
            dve.tensor_copy(tabf[:, 0:1], over_pos[:, 15:16])
            step(dve.tensor_tensor(over_at, over_pos, over_f, ALU.subtract))
            for k in range(OVER):
                step(dve.scalar_tensor_tensor(out=hot_f, in0=over_at, scalar=float(k), in1=over_f,
                                              op0=ALU.is_equal, op1=ALU.mult))
                step(dve.tensor_reduce(over_e, over_hot, AX.X, ALU.add))
                step(dve.tensor_tensor(over_tmp, hot_f, lot_base, ALU.mult))
                step(dve.tensor_reduce(over_base, over_tmp, AX.X, ALU.add))
                step(dve.tensor_tensor(over_tmp, hot_f, lot_expert, ALU.mult))
                step(dve.tensor_reduce(tabf[:, 1 + k:2 + k], over_tmp, AX.X, ALU.add))
                wide_e = bview(over_e, [P, 3, EXPERTS], 1)
                step(dve.tensor_tensor(tmp24, slot_of, wide_e, ALU.mult))
                step(dve.tensor_reduce(m_tok, tmp24, AX.X, ALU.add))
                step(dve.tensor_scalar(job_slot[:, :, EXPERTS + k], m_tok, over_base, None, ALU.subtract))
                step(dve.tensor_tensor(tmp24, comb, wide_e, ALU.mult))
                step(dve.tensor_reduce(job_w[:, :, EXPERTS + k], tmp24, AX.X, ALU.add))
            dve.tensor_copy(tabi[:, 0:5], tabf[:, 0:5]).then_inc(jobs_ready, 2)
            dve.wait_ge(jobs_ready, 2)

            def xg_lo(j):
                for half in range(2):
                    dve.wait_ge(xg_hi_ready, 2 * j + half + 1)
                    hi, lo = (xg[i][:, 4 * half:4 * half + 4, :].rearrange("q a b -> q (a b)") for i in range(2))
                    dve.tensor_tensor(lo, bank[7 if half == 0 else 2][:, :], hi.bitcast(F32), ALU.subtract)\
                        .then_inc(xg_lo_ready, 1)

            for h in range(3):
                split_lo(dve, 0, h)
            xg_lo(0)

            def back(j):
                for k in range(KT):
                    dve.wait_ge(back_full, KT * j + k + 1)
                    dve.tensor_tensor(fT[:, k, :], fT[:, k, :], bank[7 - k % 2][:, 0:T], ALU.add).then_inc(back_added, 1)

            def job(j):
                def ht_lo(c):
                    dve.wait_ge(ht_hi_ready, NCHK * j + c + 1)
                    dve.tensor_tensor(h_t[c % 2][1], bank[6][:, :], h_t[c % 2][0].bitcast(F32), ALU.subtract)\
                        .then_inc(ht_lo_ready, 1)

                for m, (kind, c) in enumerate(kinds):
                    for h in (2 * m, 2 * m + 1):
                        half_free(dve, j, h)
                        split_lo(dve, *half_after(j, h))
                    if (kind, c) == ("gate", 0):
                        back(j)
                    if kind == "gate" and c:
                        ht_lo(c - 1)
                    if kind == "up":
                        dve.wait_ge(g_ready, NCHK * j + c + 1)
                        if c >= 2:
                            dve.wait_ge(ht_full, NCHK * j + c - 1)
                        dve.tensor_tensor(h_act[:, c % 2, :], g_act[:, c % 2, :], bank[2 * (c % 2) + 1][:, :],
                                          ALU.mult).then_inc(h_act_ready, 1)
                    if (kind, c) == ("up", 1):
                        for b in range(3):
                            ins = dve.tensor_scalar(pick_w[:, b, :], slots, job_slot[:, b, bass.ds(j, 1)],
                                                    job_w[:, b, bass.ds(j, 1)], ALU.is_equal, ALU.mult)
                        ins.then_inc(pickw_ready, 1)
                    if (kind, c) == ("down", 2):
                        dve.wait_ge(spread_full, j + 1)
                        dve.tensor_copy(spread, bank[7][:, 0:T]).then_inc(spread_copied, 1)
                    if (kind, c) == ("down", 3):
                        picks(j + 1)
                    if (kind, c) == ("down", NCHK - 2):
                        xg_lo(j + 1)
                        ht_lo(NCHK - 1)

            njobs = for_jobs(dve, job)
            back(njobs)
            post(1, 1)
            for n in range(6):
                rows = P if n < 4 else NS
                dve.wait_ge(outs_t, n + 1)
                dve.tensor_copy(x_tok[0:rows, n // 2, W * (n % 2):W * (n % 2) + W], bank[n % 4][0:rows, :])\
                    .then_inc(outs_copied, 1)

        @block.tensor
        def _(pe):
            tile = [0]
            piece = [0]
            norms = [0]

            def mm(out, lhsT, rhs, start, stop):
                return pe.matmul(out, lhsT, rhs, start=start, stop=stop, skip_group_check=True)

            count = [0]

            def step(ins):
                count[0] += 1
                ins.then_inc(t_step, 1)
                pe.wait_ge(t_step, count[0])

            def next_tile():
                n = tile[0]
                if TILES["ada1b"] <= n <= TILES["glu"]:
                    pe.wait_ge(acc_free, n)
                elif n >= 4:
                    pe.wait_ge(acc_free, n - 3)
                tile[0] += 1
                return tile_bank(n)

            def next_piece():
                i = piece[0]
                pe.wait_ge(ring_loaded[i % RING], 16 * (i // RING + 1))
                piece[0] += 1
                return slot(i)

            def product(out, w, c, src, kts, first, last):
                for j, k in enumerate(kts):
                    ins = mm(out, w[:, j, c:c + P], src[:, k, :], first and j == 0, last and j == len(kts) - 1)
                return ins

            def ada_part(w, out, ks):
                for k in ks:
                    ins = mm(out[0:NC, :], csT[:, k, :], w[:, k, :], k == 0, k == KT - 1)
                if k == KT - 1:
                    ins.then_inc(acc_full, 1)

            def ada(i):
                ada_part(next_piece(), next_tile(), range(KT))

            def ada_rows(i):
                l_tile = (TILES["ada0"] + i) if i < 12 else (TILES["ada1a"] + i - 12 if i < 16 else TILES["ada1b"] + i - 16)
                pe.wait_ge(acc_free, l_tile + 1)
                if i:
                    pe.wait_ge(mod_ready, i)
                for q in range(4):
                    at = 36 * (i % 2) + NC * q
                    ins = pe.transpose(row_bank[:, at:at + NC], modrow[:, P * q:P * q + P], ident[0:NC, 0:NC])
                ins.then_inc(row_t, 1)

            def mean_square():
                norms[0] += 1
                pe.wait_ge(sq_ready, norms[0])
                for k in range(KT):
                    ins = mm(ms_bank[:, 0:T], mean_d[:, :], sq[:, k, :], k == 0, k == KT - 1)
                ins.then_inc(ms_ready, 1)

            def dense(tiles, src, n_k=KT):
                for t in range(tiles):
                    if t % 4 == 0:
                        w = next_piece()
                    ins = product(next_tile()[:, 0:T], w, P * (t % 4), src, range(n_k), True, True)
                    ins.then_inc(acc_full, 1)

            pe.wait_ge(consts_ready, 2)
            pe.wait_ge(c_loaded, 32)
            for k in range(KT):
                ins = pe.transpose(bank[4][:, NC * k:NC * k + NC], crow[:, P * k:P * k + P], ident[0:NC, 0:NC])
            ins.then_inc(start_t, 1)
            pe.wait_ge(vec_loaded, 16 * 7)
            pe.transpose(bank[7][:, 96:192], rawA, ident[0:96, 0:96])
            pe.transpose(bank[7][:, 192:279], rawB, ident[0:87, 0:87])
            for k in range(4):
                ins = pe.transpose(bank[7][:, 288 + 16 * k:304 + 16 * k], conv_rows[:, P * k:P * k + P],
                                   ident[0:16, 0:16])
            ins.then_inc(start_t, 1)
            pe.wait_ge(x_loaded, 32)
            for k in range(KT):
                if k >= 2:
                    pe.wait_ge(start_copied, k)
                if k == 1:
                    pe.wait_ge(cs_ready, 1)
                out = bank[(6, 4)[k % 2]]
                for b in range(2):
                    pe.transpose(out[:, P * b:P * b + P], xrow[:, b, P * k:P * k + P], ident[:, :])
                pe.transpose(out[:, TP:T], xrow[0:NS, 2, P * k:P * k + P], ident[0:NS, 0:NS]).then_inc(start_t, 1)
            pe.wait_ge(cs_ready, 1)
            for i in range(12):
                ada(i)
                if i:
                    ada_rows(i - 1)
            ada_rows(11)
            pe.wait_ge(start_copied, 1 + KT)
            mean_square()
            pe.wait_ge(h_ready, 1)
            pe.wait_ge(small_loaded, 48)
            out = next_tile()
            for k in range(KT):
                ins = mm(out[0:LOWRANK, 0:T], glr_w[:, k, :], hT[:, k, :], k == 0, k == KT - 1)
            ins.then_inc(acc_full, 1)
            dense(N_IN0, hT)
            for a in range(2):
                mm(bank[6 + a][:, 0:T], gate_up_w[:, P * a:P * a + P], pT[0:LOWRANK, GLR, :], True, True)\
                    .then_inc(z_full, 1)
            pe.wait_ge(z_copied, 2)
            for b in range(2):
                for h in range(H):
                    ins = pe.transpose(bank[6 + b][:, P * h:P * h + P], pT[:, V + h, P * b:P * b + P], ident[:, :])
                ins.then_inc(tok_full, 1)
            for h in range(H):
                ins = pe.transpose(bank[4][0:NS, P * h:P * h + P], pT[:, V + h, TP:T], ident[:, :])
            ins.then_inc(tok_full, 1)
            for i in range(2):
                ada(12 + i)
            ada_rows(12)
            pe.wait_ge(tok_copied, 1)
            for a in range(2):
                ins = pe.transpose(bank[6][0:NS, P * a:P * a + P], pT[:, K_ + a, TP:T], ident[:, :])
            ins.then_inc(tok_full, 1)
            pe.wait_ge(kd_ready, 1)
            pe.wait_ge(tok_copied, 2)
            for b in range(2):
                for a in range(2):
                    at = TP * b + P * a
                    ins = pe.transpose(bank[7][:, at:at + P], e_dec[:, a, P * b:P * b + P], ident[:, :])
            ins.then_inc(tok_full, 1)
            pe.wait_ge(qk_ready, 1)
            for b in range(2):
                pe.wait_ge(tok_copied, 4 + b)
                for h in (0, 2, 1, 3):
                    rows, a = slice(64 * (h % 2), 64 * (h % 2) + 64), h // 2
                    cols_ = slice(P * b, P * b + P)
                    ins = mm(bank[6 + b][:, P * h:P * h + P], pT[rows, K_ + a, cols_], pT[rows, Q + a, cols_], True, True)
                    if h == 2:
                        step(ins)
                ins.then_inc(att_full, 1)
            for c in range(NCH):
                b, rows = c // 2, slice(64 * (c % 2), 64 * (c % 2) + 64)
                if c in (1, 2):
                    pe.wait_ge(att_masked, c)
                if c == 3:
                    pe.wait_ge(s_ready, 1)
                for a in range(2):
                    ins = mm(bank[(4, 6, 7, 4)[c]][:, 256 * a:256 * a + 256], kd_tok[rows, b, P * a:P * a + P],
                             v_tok[rows, b, 256 * a:256 * a + 256], True, True)
                ins.then_inc(ds_full, 1)
            for i in range(2, 4):
                ada(12 + i)
                ada_rows(11 + i)
            ada_rows(15)
            for n in range(2 * H):
                h, u = divmod(n, 2)
                if n < 3:
                    pe.wait_ge(s_ready, n + 2)
                else:
                    pe.wait_ge(kv_added, n - 2)
                pe.wait_ge(spread_ready, h + 1)
                mm(bank[(6, 7, 4)[n % 3]][:, :], ks_tok[:, P * (h // 2):P * (h // 2) + P],
                   spread_v[:, h % 2, 4 * u:4 * u + 4, :].rearrange("p s v -> p (s v)"), True, True).then_inc(kv_full, 1)
            pe.wait_ge(kv_added, 2 * H)
            for h in range(H):
                out = next_tile()
                rows, a = slice(64 * (h % 2), 64 * (h % 2) + 64), h // 2
                for b in range(2):
                    mm(out[:, P * b:P * b + P], v_tok[:, b, P * h:P * h + P], attn[:, b, P * h:P * h + P], b == 0, False)
                for c in range(1, NCH):
                    mm(out[:, CH * c:CH * c + CH], s_chunk[rows, c - 1, a, :], pT[rows, Q + a, CH * c:CH * c + CH],
                       False, False)
                for s in range(NS):
                    ins = mm(out[:, TP + s:TP + s + 1], s0[rows, s, a, :], pT[rows, Q + a, TP + s:TP + s + 1],
                             False, s == NS - 1)
                ins.then_inc(acc_full, 1)
            pe.wait_ge(osq_ready, 1)
            for h in range(H):
                out = bank[5][:, 128:128 + T] if h == 3 else bank[(6, 7, 4)[h]][:, 0:T]
                ins = mm(out, ones[:, :], sq_flat[:, T * h:T * h + T], True, True)
            ins.then_inc(oms_ready, 1)
            pe.wait_ge(mixed_o, 1)
            pe.wait_ge(mixed_y, 1)
            dense(KT, hT)
            mean_square()
            mean_square()
            pe.wait_ge(h_ready, 2)
            for t in range(FT):
                if t % 4 == 0:
                    w_gate, w_up = next_piece(), next_piece()
                product(next_tile()[:, 0:T], w_gate, P * (t % 4), hT, range(KT), True, True).then_inc(acc_full, 1)
                ins = product(next_tile()[:, 0:T], w_up, P * (t % 4), hT, range(KT), True, True)
                ins.then_inc(acc_full, 1)
                if t == 16:
                    pe.wait_ge(s5_rows_ready, 3)
                    for i, name in enumerate(("mag", "abre", "abim", "fre", "fim", "turns", "hi", "lo")):
                        ins = pe.transpose(bank[7][:, S5T * i:S5T * i + S5T], s5_rows[:, ROWS.index(name), :],
                                           ident[0:S5T, 0:S5T])
                    ins.then_inc(s5_cols_t, 1)
                    for i in range(2):
                        for h in range(2):
                            at = 256 * i + P * h
                            ins = pe.transpose(bank[4][:, at:at + P], s_rows[:, i, P * h:P * h + P], ident[:, :])
                    ins.then_inc(s5_cols_t, 1)
            for i in range(4):
                outs = [next_tile()[:, 0:T] for _ in range(2)]
                for half in range(2):
                    w = next_piece()
                    kts = range(half * FT // 2, (half + 1) * FT // 2)
                    if i == 0:
                        pe.wait_ge(hid_ready, kts[-1] + 1)
                    for j, out in enumerate(outs):
                        ins = product(out, w, P * j, hid, kts, half == 0, half == 1)
                        if half == 1:
                            ins.then_inc(acc_full, 1)
            mean_square()
            mean_square()
            pe.wait_ge(h_ready, 3)
            dense(KT, hT)

            def tr(k):
                pe.wait_ge(pads_ready, k + 1)
                for n in range(3):
                    if k or n:
                        pe.wait_ge(tr_copied, 3 * k + n)
                    src = bb_pad.rearrange("q a b -> q (a b)") if n == 0 else c_pad[:, n - 1, :]
                    for i in range(2 if n == 0 else 4):
                        ins = pe.transpose(bank[7][:, P * i:P * i + P], src[:, P * i:P * i + P], ident[:, :])
                    ins.then_inc(tr_full, 1)

            def bu(j):
                k, r = divmod(j, 4)
                rows = slice(32 * r, 32 * r + 32)
                if r == 0:
                    pe.wait_ge(tr_copied, 3 * k + 1)
                if j >= 2:
                    pe.wait_ge(bu_used, j - 1)
                for i in range(2):
                    ins = mm(bank[1 + 2 * (j % 2) + i][:, 0:T], bbt[rows, k % 2, i, :], uT[rows, k, :], True, True)
                ins.then_inc(bu_full, 1)

            def cx(j):
                k, r = divmod(j, 4)
                if r == 0:
                    pe.wait_ge(tr_copied, 3 * k + 3)
                    if k:
                        pe.wait_ge(y_used, k)
                pe.wait_ge(xre_ready, j + 1)
                pe.wait_ge(xim_ready, j + 1)
                for i in range(2):
                    ins = mm(bank[6][:, 0:T], ct[:, k % 2, 4 * i + r, :], xri[j % 3][:, i, :], r == 0 and i == 0,
                             r == 3 and i == 1)
                ins.then_inc(y_full, 1)

            pe.wait_ge(acc_free, TILES["in1"] + KT)
            tr(0)
            bu(0)
            for j in range(S5T + 2):
                if j + 1 < S5T:
                    bu(j + 1)
                if j >= 2:
                    cx(j - 2)
                if j % 4 == 1 and j // 4 + 1 < KT:
                    tr(j // 4 + 1)
                if j < S5T:
                    if j % 4 == 0:
                        ada_w, ada_out = next_piece(), next_tile()
                    ada_part(ada_w, ada_out, range(2 * (j % 4), 2 * (j % 4) + 2))
                    if j % 4 == 0 and j:
                        ada_rows(15 + j // 4)
            ada_rows(23)
            pe.wait_ge(last_copied, S5T)
            pe.wait_ge(bu_used, S5T)
            for i in range(2):
                ins = pe.transpose(bank[1][0:S5T, P * i:P * i + P], s_last[:, i, :], ident[:, :])
            ins.then_inc(s5_t, 1)
            flat = s_out.rearrange("q i s t -> q i (s t)")
            for i in range(2):
                for h in range(2):
                    ins = pe.transpose(bank[2][:, 256 * i + P * h:256 * i + P * h + P], flat[:, i, P * h:P * h + P],
                                       ident[:, :])
            ins.then_inc(s5_t, 1)
            pe.wait_ge(gelu_ready, 1)
            pe.wait_ge(s5_out, 2)
            for t in range(KT):
                if t % 4 == 0:
                    w_a, w_g = next_piece(), next_piece()
                for w in (w_a, w_g):
                    product(next_tile()[:, 0:T], w, P * (t % 4), hT, range(KT), True, True).then_inc(acc_full, 1)
            mean_square()
            mean_square()
            pe.wait_ge(h_ready, 4)
            for k in range(KT):
                ins = mm(bank[7][0:EXPERTS, 0:T], router_w[:, k, :], hT[:, k, :], k == 0, k == KT - 1)
            ins.then_inc(logits_full, 1)

            def token_rows(src, n, full):
                b, cols_ = n // 2, slice(P * (n // 2), min(P * (n // 2) + P, T))
                rows = cols_.stop - cols_.start
                for q in range(4):
                    ins = pe.transpose(bank[n % 4][0:rows, P * q:P * q + P], src[:, 4 * (n % 2) + q, cols_], ident[:, :])
                ins.then_inc(full, 1)

            for n in range(4):
                token_rows(hT, n, xt_full)
            pe.wait_ge(logits_copied, 1)
            for b in range(3):
                rows = P if b < 2 else NS
                ins = pe.transpose(bank[7][0:rows, EXPERTS * b:EXPERTS * b + EXPERTS],
                                   logits_t[:, P * b:P * b + rows], ident[0:EXPERTS, 0:EXPERTS])
            ins.then_inc(lg_full, 1)
            for n in range(4, 6):
                pe.wait_ge(xt_copied, n - 3)
                token_rows(hT, n, xt_full)
            pe.wait_ge(sel_ready, 1)
            for b in range(3):
                out = bank[7][:, EXPERTS * b:EXPERTS * b + EXPERTS]
                for a in range(b + 1):
                    mm(out, (before if a == b else ones[:, :]), sel[:, a, :], a == 0, a == b)
            for a in range(3):
                ins = mm(bank[7][:, 24:32], ones[:, :], sel[:, a, :], a == 0, a == 2)
            ins.then_inc(pos_full, 1)

            def gather(j):
                pe.wait_ge(pick_ready, j + 1)
                for half in range(2):
                    out = bank[7 if half == 0 else 2]
                    for q in range(4):
                        for b in range(3):
                            ins = mm(out[:, P * q:P * q + P], x_tok[:, b, P * (4 * half + q):P * (4 * half + q) + P],
                                     pick[:, b, :], b == 0, b == 2)
                    ins.then_inc(gath_full, 1)

            def back(j):
                pe.wait_ge(y_ready, j)
                pe.wait_ge(spread_copied, j)
                for k in range(KT):
                    if k >= 2:
                        pe.wait_ge(back_added, KT * j + k - 1)
                    mm(bank[7 - k % 2][:, 0:T], y_job[:, k // 4, P * (k % 4):P * (k % 4) + P], spread, True, True)\
                        .then_inc(back_full, 1)

            def job(j):
                def hidden(kind, c, full):
                    out = bank[2 * (c % 2) + (kind == "up")]
                    for h in range(2):
                        n = 2 * kinds.index((kind, c)) + h
                        w = [x[half_slot(n)][:, :].rearrange("p (k n) -> p k n", n=W) for x in (w_hi, w_lo)]
                        pe.wait_ge(lo_ready, half_count(j, n))
                        for k in range(4):
                            for a, b in ((0, 0), (1, 0), (0, 1)):
                                ins = mm(out[:, :], xg[a][:, 4 * h + k, :], w[b][:, k, :], n % 2 == k == a == b == 0,
                                         h == 1 and k == 3 and b == 1)
                        ins.then_inc(full if h else first_half_used, 1)

                def turn_h(c):
                    pe.wait_ge(h_act_ready, NCHK * j + c + 1)
                    if c:
                        pe.wait_ge(ht_lo_ready, NCHK * j + c)
                    for q in range(4):
                        ins = pe.transpose(bank[6][:, P * q:P * q + P], h_act[:, c % 2, P * q:P * q + P], ident[:, :])
                    ins.then_inc(ht_full, 1)

                def down(c):
                    pe.wait_ge(ht_lo_ready, NCHK * j + c + 1)
                    for h in range(2):
                        n = 2 * kinds.index(("down", c)) + h
                        w = [x[half_slot(n)][:, :].rearrange("p (k n) -> p k n", n=D) for x in (w_hi, w_lo)]
                        pe.wait_ge(lo_ready, half_count(j, n))
                        for k in range(2):
                            q = 2 * h + k
                            for a, b in ((0, 0), (1, 0), (0, 1)):
                                for half in range(2):
                                    ins = mm(bank[4 + half][:, :], h_t[c % 2][a][:, P * q:P * q + P],
                                             w[b][:, k, W * half:W * half + W], c == q == a == b == 0,
                                             c == NCHK - 1 and q == 3 and b == 1)
                        ins.then_inc(down_done if h else first_half_used, 1)

                pe.wait_ge(xg_lo_ready, 2 * j + 2)
                hidden("gate", 0, gate_full)
                back(j)
                hidden("up", 0, up_full)
                for c in range(1, NCHK):
                    if c >= 2:
                        pe.wait_ge(h_act_ready, NCHK * j + c - 1)
                    hidden("gate", c, gate_full)
                    if c == 1:
                        pe.wait_ge(back_added, KT * j + KT)
                    turn_h(c - 1)
                    hidden("up", c, up_full)
                    down(c - 1)
                    if c == 3:
                        pe.wait_ge(pickw_ready, j + 1)
                        for b in range(3):
                            rows = P if b < 2 else NS
                            ins = pe.transpose(bank[7][:, P * b:P * b + rows], pick_w[0:rows, b, :],
                                               ident[0:rows, 0:rows])
                        ins.then_inc(spread_full, 1)
                pe.wait_ge(spread_copied, j + 1)
                gather(j + 1)
                turn_h(NCHK - 1)
                down(NCHK - 1)

            pe.wait_ge(xt_copied, 6)
            pe.wait_ge(jobs_ready, 2)
            gather(0)
            njobs = for_jobs(pe, job)
            back(njobs)
            pe.wait_ge(back_added, KT * njobs + KT)
            mean_square()
            pe.wait_ge(x_ready, 5)
            for n in range(6):
                if n >= 4:
                    pe.wait_ge(outs_copied, n - 3)
                token_rows(xT, n, outs_t)


_INS = ["x_prompt", "x_sample", "c_prompt", "c_sample", "state_gla", "state_conv", "state_s5_re", "state_s5_im",
        "w_ada", "b_ada", "g_norm", "w_in0", "w_gate_up", "b_gate_up", "g_head_norm", "w_conv", "w_out0",
        "w_ffn_gate", "w_ffn_up", "w_ffn_down", "w_in1", "s5_a_re", "s5_a_im", "s5_log_dt", "s5_b_re", "s5_b_im",
        "s5_c_re", "s5_c_im", "s5_d", "w_glu", "w_router", "w_exp_gate", "w_exp_up", "w_exp_down"]
_OUTS = [((1, TP, D), "float32"), ((NS, 1, D), "float32"), ((1, 1, 4, 64, 128), "float32"),
         ((1, 1, 2, 512), "float32"), ((1, 1, 64, 64), "float32"), ((1, 1, 64, 64), "float32"),
         ((NS, 1, 4, 64, 128), "float32"), ((NS, 1, 2, 512), "float32"), ((NS, 1, 64, 64), "float32"),
         ((NS, 1, 64, 64), "float32")]


def kernel(**inputs):
    import numpy as _np
    import concourse.bacc as _bacc
    from concourse import mybir as _mybir
    from concourse.bass_utils import run_bass_kernel_spmd as _run

    nc = _bacc.Bacc("TRN2", target_bir_lowering=False, num_devices=1)
    arrays, args = {}, []
    for name in _INS:
        a = _np.ascontiguousarray(inputs[name])
        arrays[f"in_{name}_dram"] = a
        args.append(nc.dram_tensor(f"in_{name}_dram", a.shape, _mybir.dt.from_np(a.dtype), kind="ExternalInput").ap())
    for i, (shape, dtype) in enumerate(_OUTS):
        dt = _mybir.dt.from_np(_np.dtype(dtype))
        args.append(nc.dram_tensor(f"out_{i}_dram", shape, dt, kind="ExternalOutput").ap())
    hybrid_trunk(nc, *args)
    r = _run(nc, [arrays], core_ids=[0])
    return tuple(r.results[0][f"out_{i}_dram"] for i in range(len(_OUTS)))
```

```python
from contextlib import ExitStack

import numpy as np

import concourse.bass as bass
from concourse import mybir

ALU = mybir.AluOpType
ACT = mybir.ActivationFunctionType
AX = mybir.AxisListType
F32 = mybir.dt.float32
F32R = mybir.dt.float32r
I32 = mybir.dt.int32

P = 128
D = 1024
KT = D // P
TP = 256
NS = 8
T = TP + NS
NC = 1 + NS
H = 4
CH = 64
NCH = TP // CH
LOWRANK = 16
FF = 2816
FT = FF // P
EXPERTS = 8
FFE = 3584
W = 512
NCHK = FFE // W
S5T = 32
EPS = 1e-6
PIECE = KT * W
RING = 3
HALF = PIECE // 2
MAGIC = 12582912.0
TWO_PI = 6.283185
INV_TWO_PI = 0.15915494309189535
HALF_PI = 1.5707963
NO_SLOT = -1000.0
OVER = 4
JOBS = EXPERTS + OVER

Q, K_, V, OG, CH_H, CH_B, CH_C, GLR = 0, 2, 4, 8, 12, 16, 20, 24
N_IN0 = 24
IN0_COLS = [0, 512, 1024, 1552, 2064, 2576]
GLR_COL = 1536

TILES, _n = {}, 0
for _name, _count in (("ada0", 12), ("glr", 1), ("in0", N_IN0), ("ada1a", 4), ("gla", H), ("out0", KT),
                      ("ffn", 2 * FT), ("down", KT), ("in1", KT), ("ada1b", 8), ("glu", 2 * KT)):
    TILES[_name] = _n
    _n += _count
GROUPS = [range(i, min(i + 4, FT)) for i in range(0, FT, 4)]
ROWS = ["are", "aim", "dr", "th", "turns", "hi", "lo", "mag", "sin", "cos", "abre", "abim", "den", "fre", "fim", "tmp"]
EXPERT_PIECES = 3 * NCHK
HALVES = 7


def hybrid_trunk(nc, x_prompt, x_sample, c_prompt, c_sample, state_gla, state_conv, state_s5_re, state_s5_im,
                 w_ada, b_ada, g_norm, w_in0, w_gate_up, b_gate_up, g_head_norm, w_conv, w_out0, w_ffn_gate,
                 w_ffn_up, w_ffn_down, w_in1, s5_a_re, s5_a_im, s5_log_dt, s5_b_re, s5_b_im, s5_c_re, s5_c_im,
                 s5_d, w_glu, w_router, w_exp_gate, w_exp_up, w_exp_down,
                 y_prompt, y_sample, gla_prompt, conv_prompt, s5_re_prompt, s5_im_prompt,
                 gla_sample, conv_sample, s5_re_sample, s5_im_sample):
    with ExitStack() as ctx:
        ctx.enter_context(nc.allow_non_contiguous_dma(reason="small vectors and states"))

        def sb(name, shape, dt=F32):
            return ctx.enter_context(nc.sbuf_tensor(name, shape, dt))

        def sem(name):
            return ctx.enter_context(nc.semaphore(name))

        ring = [sb(f"ring{i}", [P, PIECE]) for i in range(RING)]
        w_hi = [sb(f"w_hi{i}", [P, HALF], F32R) for i in range(3)]
        w_lo = [sb(f"w_lo{i}", [P, HALF], F32R) for i in range(3)]
        parts = sb("parts", [P, 2 * KT * T], F32R)
        xT = sb("xT", [P, KT, T])
        hT = sb("hT", [P, KT, T])
        fT = sb("fT", [P, KT, T])
        sq = sb("sq", [P, KT, T])
        rstd = sb("rstd", [P, T])
        modT = [sb(f"modT{i}", [P, 48, NC]) for i in range(2)]
        coefA = [sb(f"coefA{i}", [P, KT, NC]) for i in range(4)]
        coefG = [sb(f"coefG{i}", [P, KT, NC]) for i in range(4)]
        csT = sb("csT", [P, KT, NC])
        vecA = sb("vecA", [P, 96])
        vecB = sb("vecB", [P, 87])
        convT = sb("convT", [P, 4, 2 * NS])
        router_w = sb("router_w", [P, KT, EXPERTS])
        ident = sb("ident", [P, P])
        ones = sb("ones", [P, P])
        mean_d = sb("mean_d", [P, P])
        modrow = sb("modrow", [NC, W])
        half_rows = sb("half_rows", [P, 2])
        group_rows = sb("group_rows", [P, 8])
        minus_group_rows = sb("minus_group_rows", [P, 8])
        half_pi = sb("half_pi", [P, 1])
        eps = sb("eps", [P, 1])
        act_table = sb("act_table", [P, 1])
        magic = sb("magic", [P, 1])
        minus_magic = sb("minus_magic", [P, 1])
        tabi = sb("tabi", [P, 8], I32)
        ARENA = 12608
        arena = sb("arena", [P, ARENA])
        bank = [ctx.enter_context(nc.psum_tensor(f"bank{i}", [P, W], F32)) for i in range(8)]
        row_bank, ms_bank = bank[5], bank[6]

        def tile_bank(n):
            return bank[0 if TILES["ada1b"] <= n < TILES["glu"] else n % 4]

        def shaped(flat, shape):
            if len(shape) == 2:
                return flat.rearrange("p (a b) -> p a b", b=shape[1])
            if len(shape) == 3:
                return flat.rearrange("p (a b c) -> p a b c", b=shape[1], c=shape[2])
            return flat

        def view(at, *shape, rows=P):
            assert at + int(np.prod(shape)) <= ARENA
            return shaped(arena[0:rows, at:at + int(np.prod(shape))], shape)

        sq_flat = sq[:, :, :].rearrange("p a b -> p (a b)")
        fT_flat = fT[:, :, :].rearrange("p a b -> p (a b)")

        def bview(ap, shape, *dims):
            for d in dims:
                ap = ap.unsqueeze(d)
            return ap.broadcast_to(shape)

        xrow = view(0, 3, D)
        crow = view(3072, D, rows=NC)
        rawA = view(4096, P, rows=96)
        rawB = view(4224, P, rows=87)
        conv_rows = view(4352, 512, rows=2 * NS)
        pT = view(0, 25, T)
        v_tok = view(V * T, 2, W)
        kd_tok = view(8712, 2, TP)
        z_gate = view(6600, 2, T)
        b_cum = view(7128, 2, T)
        attn = view(6600, 2, W)
        head_rstd = view(6600, H, T)
        e_pos = view(8184 - 528, 2, T)
        e_neg = view(8712, 2, T)
        e_dec = view(9240, 2, TP)
        s_chunk = view(9752, NCH, 2, P)
        attn_mask = view(10776, P)
        scan_mask = view(10904, TP)
        ks_tok = view(11160, 256, rows=NS)
        glr_w = view(11416, KT, LOWRANK)
        gate_up_w = view(11544, 256, rows=LOWRANK)
        oT = view(11416, H, T)
        s0 = shaped(fT_flat[:, 0:2 * NS * P], (NS, 2, P))
        spread_v = shaped(sq_flat[0:NS, 0:2 * NS * P], (2, NS, P))
        vs_tok = hT[0:NS, 0:2, :].rearrange("p a b -> p (a b)")[:, 0:512]
        hid = view(0, FT, T)
        silu_g = view(FT * T, 4, T)
        up_c = view((FT + 4) * T, 4, T)

        uT = view(0, KT, T)
        ct = view(2112, 2, 8, P)
        bbt = view(4160, 2, 2, P)
        bb_pad = view(4672, 2, 4 * 32)
        c_pad = view(4928, 2, W)
        xri = [view(at, 2, T) for at in (5952, 6480, 12080)]
        c_raw = view(7920, 2, KT * 64)
        bb = view(8944, 2, W)
        b_raw = view(9968, 2, W)
        s_in = view(9968, 2, NS, S5T)
        s_out = view(9968 + W, 2, NS, S5T)
        cols = view(10992, 8, S5T)
        steps_t = view(11248, TP)
        s_last = view(11504, 2, S5T)
        s_rows = view(11568, 2, TP)
        s5_rows = view(7920, 16, P, rows=S5T)
        log_dt = view(12080, 4, rows=S5T)
        turn = [fT_flat[:, 1024 + TP * i:1024 + TP * i + TP] for i in range(2)]
        tables = [view(7008, 2, TP), shaped(fT_flat[:, 1536:2048], (2, TP)), view(11568, 2, TP)]
        work = [shaped(x, (4, TP)) for x in (sq_flat[:, 0:1024], sq_flat[:, 1024:2048], fT_flat[:, 0:1024])]
        zg_sig = view(5952, 4, T)
        out_rows = view(11568, 2, P, rows=S5T)
        s_out_rows = view(11824, 4, P)
        x_tok = view(0, 3, D)
        def two(at, *shape):
            n = int(np.prod(shape))
            return [shaped(parts[:, at + n * i:at + n * i + n], shape) for i in range(2)]

        xg = two(0, KT, P)
        g_act = view(4096, 2, W)
        h_act = view(5120, 2, W)
        h_t = [two(2048 + 2 * W * i, W) for i in range(2)]
        y_job = view(7168, 2, W)
        pick = view(8192, 3, P)
        pick_w = view(8576, 3, P)
        spread = view(8960, T)
        slots = view(9224, P)
        before = view(9352, P)
        logits_t = view(9480, T, rows=EXPERTS)
        lg = view(9744, 3, EXPERTS)
        sel = view(9768, 3, EXPERTS)
        ex = view(9792, 3, EXPERTS)
        comb = view(9816, 3, EXPERTS)
        slot_of = view(9840, 3, EXPERTS)
        valid = view(9864, 3)
        m_tok = view(9868, 3)
        d_tok = view(9872, 3)
        job_slot = view(9876, 3, JOBS + 1)
        job_w = view(9915, 3, JOBS + 1)
        cmp_a = view(9960, 24, EXPERTS)
        cmp_b = view(10152, 24, EXPERTS)
        earlier = view(10344, EXPERTS, EXPERTS)
        over = view(10408, EXPERTS, 2)
        over_at = view(10424, 16)
        over_pos = view(10440, 16)
        over_hot = view(10456, EXPERTS, 2)
        over_e = view(10472, EXPERTS)
        lot_base = view(10480, 16)
        lot_expert = view(10496, 16)
        over_tmp = view(10512, 16)
        over_base = view(10528, 1)
        tabf = view(10532, 8)
        tmp24 = view(10544, 3, EXPERTS)

        ring_loaded = [sem(f"ring_loaded{i}") for i in range(RING)]
        half_loaded = [sem(f"half_loaded{i}") for i in range(HALVES)]
        c_loaded, vec_loaded, x_loaded, small_loaded, s0_loaded = (
            sem(n) for n in ("c_loaded", "vec_loaded", "x_loaded", "small_loaded", "s0_loaded"))
        consts_ready, v_step, p_step, a_step, t_step = (
            sem(n) for n in ("consts_ready", "v_step", "p_step", "a_step", "t_step"))
        start_t, start_copied, cs_ready = (sem(n) for n in ("start_t", "start_copied", "cs_ready"))
        acc_full, acc_free, row_t, mod_ready = (sem(n) for n in ("acc_full", "acc_free", "row_t", "mod_ready"))
        sq_ready, ms_ready, root_ready, scaled_ready, h_ready, x_ready = (
            sem(n) for n in ("sq_ready", "ms_ready", "root_ready", "scaled_ready", "h_ready", "x_ready"))
        z_full, z_copied, gate_parts, b_ready, exps_ready, kd_ready, qk_ready = (
            sem(n) for n in ("z_full", "z_copied", "gate_parts", "b_ready", "exps_ready", "kd_ready", "qk_ready"))
        tok_full, tok_copied, att_full, att_masked, ds_full, s_ready = (
            sem(n) for n in ("tok_full", "tok_copied", "att_full", "att_masked", "ds_full", "s_ready"))
        spread_ready, kv_full, kv_added, mixed_o, mixed_y, conv_u = (
            sem(n) for n in ("spread_ready", "kv_full", "kv_added", "mixed_o", "mixed_y", "conv_u"))
        osq_ready, oms_ready, oinv_ready, orstd_ready = (
            sem(n) for n in ("osq_ready", "oms_ready", "oinv_ready", "orstd_ready"))
        s5_loaded, c_raw_loaded, s5_rows_ready, exp_ready, trig_ready, s5_cols_t, s5_cols = (
            sem(n) for n in ("s5_loaded", "c_raw_loaded", "s5_rows_ready", "exp_ready", "trig_ready", "s5_cols_t",
                             "s5_cols"))
        bb_ready, pads_ready, tr_full, tr_copied = (sem(n) for n in ("bb_ready", "pads_ready", "tr_full", "tr_copied"))
        whole_turns, turn_ready, table_ready, bu_full, bu_used, w_ready, z_ready, xre_ready, xim_ready, y_full, y_used = (
            sem(n) for n in ("whole_turns", "turn_ready", "table_ready", "bu_full", "bu_used", "w_ready", "z_ready",
                             "xre_ready", "xim_ready", "y_full", "y_used"))
        last_copied, gelu_ready, s5_t, s5_out, glu_ready, s5_stored = (
            sem(n) for n in ("last_copied", "gelu_ready", "s5_t", "s5_out", "glu_ready", "s5_stored"))
        logits_full, logits_copied, lg_full, xt_full, xt_copied, moe_consts, lg_ready, sel_ready, pos_full, jobs_ready = (
            sem(n) for n in ("logits_full", "logits_copied", "lg_full", "xt_full", "xt_copied", "moe_consts",
                             "lg_ready", "sel_ready", "pos_full", "jobs_ready"))
        first_half_used, hi_ready, lo_ready = (sem(n) for n in ("first_half_used", "hi_ready", "lo_ready"))
        gath_full, xg_hi_ready, xg_lo_ready, gate_full, up_full, g_ready, h_act_ready, ht_full, ht_hi_ready, ht_lo_ready, down_done = (
            sem(n) for n in ("gath_full", "xg_hi_ready", "xg_lo_ready", "gate_full", "up_full", "g_ready", "h_act_ready",
                             "ht_full", "ht_hi_ready", "ht_lo_ready", "down_done"))
        y_ready, pick_ready, pickw_ready, spread_full, spread_copied, back_full, back_added = (
            sem(n) for n in ("y_ready", "pick_ready", "pickw_ready", "spread_full", "spread_copied",
                             "back_full", "back_added"))
        outs_t, outs_copied, y_stored = sem("outs_t"), sem("outs_copied"), sem("y_stored")
        hid_ready, out_done = sem("hid_ready"), sem("out_done")

        def columns(w, c0, n=W):
            return w[:, c0:c0 + n].rearrange("(k p) n -> p k n", p=P), KT, n

        pieces = [columns(w_ada[0], W * i) for i in range(12)]
        pieces += [columns(w_in0[0], c) for c in IN0_COLS]
        pieces += [columns(w_ada[1], W * i) for i in range(4)]
        pieces += [columns(w_out0[0], W * i) for i in range(2)]
        for i in range(0, FF, W):
            n = min(W, FF - i)
            pieces += [columns(w_ffn_gate[0], i, n), columns(w_ffn_up[0], i, n)]
        for i in range(4):
            for half in range(2):
                rows = w_ffn_down[0][half * FF // 2:(half + 1) * FF // 2, 256 * i:256 * i + 256]
                pieces.append((rows.rearrange("(k p) n -> p k n", p=P), FT // 2, 256))
        pieces += [columns(w_in1[0], W * i) for i in range(2)]
        pieces += [columns(w_ada[1], W * i) for i in range(4, 12)]
        for i in range(2):
            pieces += [columns(w_glu[0], W * i), columns(w_glu[0], D + W * i)]

        used = [TILES["ada0"] + i + 1 for i in range(12)] + [TILES["in0"] + 4 * i + 4 for i in range(6)]
        used += [TILES["ada1a"] + i + 1 for i in range(4)] + [TILES["out0"] + 4 * i + 4 for i in range(2)]
        used += [TILES["ffn"] + min(8 * (i // 2) + (4, 8)[i % 2], (42, 44)[i % 2]) for i in range(12)]
        used += [TILES["down"] + 2 * (i // 2) + 2 for i in range(8)] + [TILES["in1"] + 4 * i + 4 for i in range(2)]
        used += [TILES["ada1b"] + i + 1 for i in range(8)] + [TILES["glu"] + 4 * i + 4 for i in range(4)]
        assert len(used) == len(pieces)

        def slot(i):
            _, k, n = pieces[i]
            return ring[i % RING][:, 0:k * n].rearrange("p (k n) -> p k n", n=n)

        NPIECES = len(pieces)
        DENSE_HALVES = 0

        kinds = [("gate", 0), ("up", 0)]
        for c in range(1, NCHK):
            kinds += [("gate", c), ("up", c), ("down", c - 1)]
        kinds.append(("down", NCHK - 1))
        released = {"gate": gate_full, "up": up_full, "down": down_done}
        NH = 2 * EXPERT_PIECES

        half_ring = [ring[(NPIECES + i // 2) % RING][:, HALF * (i % 2):HALF * (i % 2) + HALF] for i in range(2 * RING)]
        half_ring.append(hT[:, :, :].rearrange("p a b -> p (a b)")[:, 0:HALF])

        def loaded_count(j, h):
            return 16 * (NH // HALVES) * j + 16 * (h // HALVES + 1)

        def half_slot(h):
            return (DENSE_HALVES + h) % 3

        def half_count(j, h):
            return NH * j + DENSE_HALVES + h + 1

        def half_free(eng, j, h):
            kind, c = kinds[h // 2]
            if h % 2 == 0:
                eng.wait_ge(first_half_used, EXPERT_PIECES * j + h // 2 + 1)
            else:
                eng.wait_ge(released[kind], NCHK * j + c + 1)

        def split_hi(act, j, h):
            act.wait_ge(half_loaded[h % HALVES], loaded_count(j, h))
            act.activation(w_hi[half_slot(h)][:, :], half_ring[h % HALVES], ACT.Copy).then_inc(hi_ready, 1)

        def split_lo(dve, j, h):
            dve.wait_ge(hi_ready, half_count(j, h))
            dve.tensor_tensor(w_lo[half_slot(h)][:, :], half_ring[h % HALVES], w_hi[half_slot(h)][:, :].bitcast(F32),
                              ALU.subtract).then_inc(lo_ready, 1)

        def half_after(j, h):
            return (j, h + 3) if h + 3 < NH else (j + 1, h + 3 - NH)

        def for_jobs(eng, body):
            with eng.Fori(0, EXPERTS) as j:
                body(j)
            eng.wait_ge(jobs_ready, 2)
            more = eng.value_load(tabi[0:1, 0:1], min_val=0, max_val=OVER)
            with eng.If(more > 0):
                with eng.Fori(0, more) as k:
                    body(k + EXPERTS)
            return more + EXPERTS

        block = ctx.enter_context(nc.Block())

        @block.sync
        def _(sp):
            sp.dma_start(crow[0:1, :], c_prompt).then_inc(c_loaded, 16)
            sp.dma_start(crow[1:NC, :], c_sample).then_inc(c_loaded, 16)
            for i, (src, k, n) in enumerate(pieces):
                if i >= RING:
                    sp.wait_ge(acc_full, used[i - RING])
                sp.dma_start(slot(i), src).then_inc(ring_loaded[i % RING], 16)

            def load(j, h, e, first=False):
                if not first:
                    sp.wait_ge(lo_ready, half_count(j, h - HALVES))
                elif h < 2 * RING:
                    sp.wait_ge(acc_full, used[NPIECES - RING + h // 2])
                else:
                    sp.wait_ge(xt_full, 6)
                kind, c = kinds[h // 2]
                if kind == "down":
                    at = W * c + W // 2 * (h % 2)
                    rows = w_exp_down[0].rearrange("e f n -> (e f) n")[bass.ds(e * FFE + at, W // 2), :]
                    src = rows.rearrange("(k p) n -> p k n", p=P)
                else:
                    w = w_exp_gate if kind == "gate" else w_exp_up
                    at = D // 2 * (h % 2)
                    rows = w[0].rearrange("e f n -> (e f) n")[bass.ds(e * D + at, D // 2), W * c:W * c + W]
                    src = rows.rearrange("(k p) n -> p k n", p=P)
                to = half_ring[h % HALVES].rearrange("p (k n) -> p k n", n=D if kind == "down" else W)
                sp.dma_start(to, src).then_inc(half_loaded[h % HALVES], 16)

            def job(j, e, after):
                for h in range(HALVES, NH):
                    load(j, h, e)
                for h in range(HALVES):
                    load(j + 1, h, after)

            def expert_of(n):
                return sp.value_load(tabi[0:1, bass.ds(n + 1, 1)], min_val=0, max_val=EXPERTS - 1)

            for h in range(HALVES):
                load(0, h, 0, first=True)
            with sp.Fori(0, EXPERTS - 1) as j:
                job(j, j, j + 1)
            sp.wait_ge(jobs_ready, 2)
            more = sp.value_load(tabi[0:1, 0:1], min_val=0, max_val=OVER)
            for h in range(HALVES, NH):
                load(EXPERTS - 1, h, EXPERTS - 1)
            after = expert_of(0)
            for h in range(HALVES):
                load(EXPERTS, h, after)
            with sp.If(more > 0):
                with sp.Fori(0, more) as k:
                    job(k + EXPERTS, expert_of(k), expert_of(k + 1))
            njobs = more + EXPERTS
            end = sp.snap(loaded_count(njobs, 0))
            for b in range(3):
                for h in range(3 * b, min(3 * b + 3, HALVES)):
                    sp.wait_ge(half_loaded[h], end)
                sp.wait_ge(outs_copied, 2 * b + 2)
                if b < 2:
                    sp.dma_start(y_prompt[0, P * b:P * b + P, :], x_tok[:, b, :]).then_inc(y_stored, 16)
                else:
                    sp.dma_start(y_sample[:, 0, :], x_tok[0:NS, b, :]).then_inc(y_stored, 16)
            sp.wait_ge(y_stored, 48)

        @block.gpsimd
        def _(pool):
            count = [0]

            def step(ins):
                count[0] += 1
                ins.then_inc(p_step, 1)
                pool.wait_ge(p_step, count[0])

            step(pool.memset(ident[:, :], 0.0))
            pool.affine_select(out=ident[:, :], in_=ident[:, :], compare_op=ALU.not_equal, fill=1.0, base=0,
                               pattern=[[-1, P]], channel_multiplier=1).then_inc(consts_ready, 1)
            pool.memset(ones[:, :], 1.0)
            pool.memset(mean_d[:, :], 1.0 / D)
            pool.memset(half_pi[:, :], HALF_PI)
            pool.memset(eps[:, :], EPS)
            pool.memset(magic[:, :], MAGIC)
            pool.memset(minus_magic[:, :], -MAGIC).then_inc(consts_ready, 1)
            step(pool.memset(attn_mask, 1.0))
            step(pool.affine_select(out=attn_mask, in_=attn_mask, compare_op=ALU.is_ge, fill=0.0, base=0,
                                    pattern=[[1, P]], channel_multiplier=-1))
            step(pool.memset(attn_mask[0:CH, CH:P], 0.0))
            step(pool.memset(scan_mask, 1.0))
            pool.memset(scan_mask.rearrange("p (c t) -> p c t", t=CH)[:, :, 0:1], 0.0).then_inc(consts_ready, 1)
            step(pool.memset(half_rows[:, :], 0.0))
            step(pool.memset(half_rows[0:64, 0:1], 1.0))
            step(pool.memset(half_rows[64:P, 1:2], 1.0))
            for m, v in ((group_rows, 1.0), (minus_group_rows, -1.0)):
                step(pool.memset(m[:, :], v))
                step(pool.affine_select(out=m[:, :], in_=m[:, :], compare_op=ALU.is_ge, fill=0.0, base=0,
                                        pattern=[[-16, 8]], channel_multiplier=1))
                ins = pool.affine_select(out=m[:, :], in_=m[:, :], compare_op=ALU.is_ge, fill=0.0, base=15,
                                         pattern=[[16, 8]], channel_multiplier=-1)
            ins.then_inc(consts_ready, 1)
            pool.dma_start(glr_w, w_in0[0][:, GLR_COL:GLR_COL + LOWRANK].rearrange("(k p) n -> p k n", p=P))\
                .then_inc(small_loaded, 16)
            pool.dma_start(gate_up_w, w_gate_up[0]).then_inc(small_loaded, 16)
            pool.dma_start(router_w[:, :, :], w_router[0].rearrange("(k p) e -> p k e", p=P))\
                .then_inc(small_loaded, 16)
            pool.dma_start(s0, state_gla.rearrange("s n (a h) d v -> (h d) s (n a) v", h=2)).then_inc(s0_loaded, 16)
            pool.wait_ge(acc_free, TILES["in0"] + N_IN0)
            u = pT[:, CH_C:CH_C + 4, :]
            tmp = pT[:, CH_H:CH_H + 4, :]
            y = hT[:, 4:8, :]

            def wc(j, n):
                return bview(vecB[:, 66 + 4 * j:70 + 4 * j], [P, 4, n], 2)

            pool.tensor_tensor(u, u, tmp, ALU.mult).then_inc(conv_u, 1)
            pool.wait_ge(conv_u, 1)
            step(pool.tensor_tensor(y, u, wc(2, T), ALU.mult))
            for j, lag in ((1, 1), (0, 2)):
                step(pool.tensor_tensor(tmp[:, :, 0:TP - lag], u[:, :, 0:TP - lag], wc(j, TP - lag), ALU.mult))
                step(pool.tensor_tensor(y[:, :, lag:TP], y[:, :, lag:TP], tmp[:, :, 0:TP - lag], ALU.add))
                old = convT[:, :, :].rearrange("p k (s j) -> p k s j", j=2)[:, :, :, j]
                step(pool.tensor_tensor(tmp[:, :, TP:T], old, wc(j, NS), ALU.mult))
                step(pool.tensor_tensor(y[:, :, TP:T], y[:, :, TP:T], tmp[:, :, TP:T], ALU.add))
            pool.tensor_tensor(y, y, pT[:, CH_B:CH_B + 4, :], ALU.mult).then_inc(mixed_y, 1)
            n = 0
            for k in range(4):
                pool.dma_start(conv_prompt[0, 0, :, P * k:P * k + P].rearrange("j p -> p j"),
                               u[:, k, TP - 2:TP]).then_inc(out_done, 16)
                pool.dma_start(conv_sample[:, 0, 1, P * k:P * k + P].rearrange("s p -> p s"),
                               u[:, k, TP:T]).then_inc(out_done, 16)
            pool.dma_start(conv_sample[:, 0, 0, :], state_conv[:, 0, 1, :]).then_inc(out_done, 16)
            pool.wait_ge(s_ready, NCH)
            for h in range(2):
                rows = slice(64 * h, 64 * h + 64)
                pool.dma_start(gla_prompt[0, 0].rearrange("(a h) d v -> h d a v", h=2)[h],
                               s_chunk[rows, NCH - 1, :, :]).then_inc(out_done, 16)
            pool.wait_ge(kv_added, 2 * H)
            pool.dma_start(gla_sample.rearrange("s n (a h) d v -> (h d) s (n a) v", h=2), s0).then_inc(out_done, 16)
            pool.wait_ge(out_done, 16 * 12)
            pool.wait_ge(mixed_o, 1)
            for i, src in enumerate((s5_a_re, s5_a_im)):
                pool.dma_start(s5_rows[:, i, :], src[0].rearrange("(t g) p -> t (g p)", g=2)).then_inc(s5_loaded, 16)
            pool.dma_start(log_dt[:, 0:2], s5_log_dt[0].rearrange("(t g) -> t g", g=2)).then_inc(s5_loaded, 16)
            for i, src in enumerate((s5_b_re, s5_b_im)):
                pool.dma_start(b_raw[:, i, :].rearrange("q (t i) -> q t i", i=16),
                               src[0].rearrange("(t g) p i -> (g p) t i", g=2)).then_inc(s5_loaded, 16)
            for i, src in enumerate((state_s5_re, state_s5_im)):
                pool.dma_start(s_rows[:, i, :].rearrange("q (h n) -> q h n", h=2),
                               src.rearrange("(h s) n (t g) p -> (s n t) h (g p)", h=2, g=2)).then_inc(s5_loaded, 16)
            pool.iota(steps_t, pattern=[[1, TP]], base=1, channel_multiplier=0,
                      allow_small_or_imprecise_dtypes=True).then_inc(consts_ready, 1)
            pool.wait_ge(s5_cols, 1)
            for i, src in enumerate((s5_c_re, s5_c_im)):
                pool.dma_start(c_raw[:, i, :].rearrange("q (k p) -> q k p", p=64),
                               src[0].rearrange("(k g) i p -> (g i) k p", g=8)).then_inc(c_raw_loaded, 16)
            pool.wait_ge(c_raw_loaded, 32)
            pool.wait_ge(bb_ready, 1)
            pool.wait_ge(acc_full, TILES["down"] + KT)
            pool.wait_ge(consts_ready, 5)

            def pads(k):
                if k:
                    pool.wait_ge(tr_full, 3 * k)
                for i in range(2):
                    pool.tensor_tensor(bb_pad[:, i, :].rearrange("q (t g i) -> q t g i", g=2, i=16),
                                       bview(bb[:, i, 64 * k:64 * k + 64].rearrange("q (t i) -> q t i", i=16),
                                             [P, 4, 2, 16], 2),
                                       bview(half_rows[:, :], [P, 4, 2, 16], 1, 3), ALU.mult)
                    ins = pool.tensor_tensor(c_pad[:, i, :].rearrange("q (g p) -> q g p", p=64),
                                             bview(c_raw[:, i, 64 * k:64 * k + 64], [P, 8, 64], 1),
                                             bview((group_rows, minus_group_rows)[i][:, :], [P, 8, 64], 2), ALU.mult)
                ins.then_inc(pads_ready, 1)

            def rotate_re(j):
                wk, tb, x = work[j % 3], tables[j % 3], xri[j % 3]
                pool.wait_ge(z_ready, 2 * j + 2)
                pool.tensor_tensor(x[:, 0, 0:TP], tb[:, 0, :], wk[:, 0, :], ALU.mult)
                step(pool.tensor_tensor(wk[:, 1, :], tb[:, 1, :], wk[:, 2, :], ALU.mult))
                pool.tensor_tensor(x[:, 0, 0:TP], x[:, 0, 0:TP], wk[:, 1, :], ALU.subtract).then_inc(xre_ready, 1)

            pads(0)
            for j in range(S5T + 1):
                if j < S5T:
                    wk = work[j % 3]
                    pool.wait_ge(bu_used, j + 1)
                    pool.tensor_tensor(wk[:, 0, :], wk[:, 0, :], wk[:, 1, :], ALU.add)
                    pool.tensor_tensor(wk[:, 2, :], wk[:, 2, :], wk[:, 3, :], ALU.subtract).then_inc(w_ready, 1)
                if j:
                    rotate_re(j - 1)
                if j % 4 == 1 and j // 4 + 1 < KT:
                    pads(j // 4 + 1)
            pool.wait_ge(s5_out, 2)
            for i, (a, b) in enumerate(((s5_re_prompt, s5_re_sample), (s5_im_prompt, s5_im_sample))):
                pool.dma_start(a[0, 0].rearrange("(t g) p -> t (g p)", g=2), out_rows[:, i, :]).then_inc(s5_stored, 16)
                pool.dma_start(b.rearrange("(h s) n (t g) p -> (s n t) h (g p)", h=2, g=2),
                               s_out_rows[:, 2 * i:2 * i + 2, :]).then_inc(s5_stored, 16)
            pool.wait_ge(s5_stored, 64)
            pool.wait_ge(glu_ready, KT)
            pool.iota(slots, pattern=[[1, P]], base=0, channel_multiplier=0, allow_small_or_imprecise_dtypes=True)
            pool.iota(lot_base, pattern=[[0, EXPERTS], [P, 2]], base=P, channel_multiplier=0,
                      allow_small_or_imprecise_dtypes=True)
            pool.iota(lot_expert, pattern=[[1, EXPERTS], [0, 2]], base=0, channel_multiplier=0,
                      allow_small_or_imprecise_dtypes=True)
            pool.memset(y_job, 0.0)
            pool.memset(spread, 0.0)
            pool.memset(x_tok[:, 2, :], 0.0)
            pool.memset(lg[:, 2, :], 0.0)
            pool.memset(valid, 1.0)
            pool.memset(job_slot, NO_SLOT)
            pool.memset(job_w, 0.0)
            pool.memset(before, 1.0)
            step(pool.memset(earlier, 1.0))
            pool.affine_select(out=valid[:, 2:3], in_=valid[:, 2:3], compare_op=ALU.is_gt, fill=0.0, base=NS,
                               pattern=[[0, 1]], channel_multiplier=-1)
            pool.affine_select(out=before, in_=before, compare_op=ALU.is_gt, fill=0.0, base=0,
                               pattern=[[1, P]], channel_multiplier=-1)
            pool.affine_select(out=earlier, in_=earlier, compare_op=ALU.is_gt, fill=0.0, base=0,
                               pattern=[[1, EXPERTS], [-1, EXPERTS]], channel_multiplier=0).then_inc(moe_consts, 1)

        @block.scalar
        def _(act):
            count = [0]
            tile = [0]
            norms = [0]

            def step(ins):
                count[0] += 1
                ins.then_inc(a_step, 1)
                act.wait_ge(a_step, count[0])

            act.dma_start(rawA, b_ada.rearrange("l (t p) -> (l t) p", p=P)).then_inc(vec_loaded, 16)
            for at, src in ((0, g_norm.rearrange("l j (t p) -> (l j t) p", p=P)),
                            (64, b_gate_up.rearrange("l (t p) -> (l t) p", p=P)),
                            (66, w_conv.rearrange("l j (t p) -> (l j t) p", p=P)),
                            (78, g_head_norm),
                            (79, s5_d.rearrange("l (t g) i -> (l t) (g i)", g=8))):
                act.dma_start(rawB[at:at + src.shape[0], :], src).then_inc(vec_loaded, 16)
            act.dma_start(conv_rows, state_conv.rearrange("s n j c -> (s n j) c")).then_inc(vec_loaded, 16)
            act.dma_start(xrow[:, 0:2, :], x_prompt[0].rearrange("(b p) d -> p b d", p=P)).then_inc(x_loaded, 16)
            act.dma_start(xrow[0:NS, 2, :], x_sample[:, 0, :]).then_inc(x_loaded, 16)

            def evac(out, func=ACT.Copy, rows=P, n=T, **more):
                act.wait_ge(acc_full, tile[0] + 1)
                act.activation(out, tile_bank(tile[0])[0:rows, 0:n], func, **more).then_inc(acc_free, 1)
                tile[0] += 1

            def ada(i):
                if i:
                    act.wait_ge(row_t, i)
                evac(modrow[:, :], rows=NC, n=W)

            def square(k, src):
                act.activation(sq[:, k, :], src, ACT.Square).then_inc(sq_ready, 1)

            def evac_f(k):
                act.wait_ge(acc_full, tile[0] + 1)
                square(k, tile_bank(tile[0])[:, 0:T])
                evac(fT[:, k, :])

            def root():
                act.activation(act_table[:, :], half_pi[:, :], ACT.Sqrt)
                act.wait_ge(ms_ready, norms[0] + 1)
                act.activation(rstd[:, :], ms_bank[:, 0:T], ACT.Sqrt, bias=eps[:, :]).then_inc(root_ready, 1)
                norms[0] += 1

            def squares_of_x(n):
                for k in range(KT):
                    act.wait_ge(x_ready, KT * n + k + 1)
                    square(k, xT[:, k, :])

            def affine(l, part, n):
                A, B = coefA[2 * l + part], modT[l][:, 24 * part:24 * part + 8, :]
                for k in range(KT):
                    act.wait_ge(scaled_ready, KT * n + k + 1)
                    act.activation(hT[:, k, 0:TP], sq[:, k, 0:TP], ACT.Identity, scale=A[:, k, 0:1],
                                   bias=B[:, k, 0:1]).then_inc(h_ready, 1)

            def R(name):
                return s5_rows[:, ROWS.index(name), :]

            def last_states(j):
                act.wait_ge(xre_ready, j + 1)
                act.wait_ge(xim_ready, j + 1)
                act.activation(s_last[:, :, j], xri[j % 3][:, :, TP - 1], ACT.Copy)
                act.activation(s_out[:, :, :, j], xri[j % 3][:, :, TP:T], ACT.Copy).then_inc(last_copied, 1)

            act.wait_ge(start_t, 1)
            act.activation(csT[:, :, :].rearrange("p k c -> p (k c)"), bank[4][:, 0:KT * NC], ACT.Silu)\
                .then_inc(cs_ready, 1)
            for i in range(12):
                ada(i)
                if i == 6:
                    for k in range(KT):
                        act.wait_ge(start_copied, k + 2)
                        square(k, xT[:, k, :])
            root()
            affine(0, 0, 0)
            evac(pT[0:LOWRANK, GLR, :], rows=LOWRANK)
            for t in range(N_IN0):
                if t < K_:
                    evac(pT[:, t, :], scale=0.125)
                elif OG <= t < CH_H:
                    evac(pT[:, t, :], ACT.Silu)
                else:
                    evac(pT[:, t, :])
            for a in range(2):
                act.wait_ge(z_full, a + 1)
                act.activation(e_pos[:, a, :], bank[6 + a][:, 0:T], ACT.Identity, bias=vecB[:, 64 + a:65 + a])\
                    .then_inc(z_copied, 1)
            act.wait_ge(z_copied, 2)
            step(act.activation(e_neg, e_pos, ACT.Abs))
            step(act.activation(e_neg, e_neg, ACT.Exp, scale=-1.0))
            act.activation(e_neg, e_neg, ACT.Ln, bias=1.0).then_inc(gate_parts, 1)
            act.wait_ge(b_ready, 1)
            act.activation(e_pos, b_cum, ACT.Exp, scale=1.0 / 16)
            act.activation(e_neg, b_cum, ACT.Exp, scale=-1.0 / 16)
            act.wait_ge(b_ready, 2)
            act.activation(e_dec, e_dec, ACT.Exp, scale=1.0 / 16).then_inc(exps_ready, 1)
            for i in range(4):
                ada(12 + i)
            for h in range(H):
                evac(oT[:, h, :])
            act.wait_ge(acc_free, TILES["gla"] + H)
            act.activation(sq_flat[:, 0:H * T], oT.rearrange("p h t -> p (h t)"), ACT.Square).then_inc(osq_ready, 1)
            act.wait_ge(oinv_ready, 1)
            act.activation(head_rstd, head_rstd, ACT.Sqrt).then_inc(orstd_ready, 1)
            act.wait_ge(kv_added, 2 * H)
            act.wait_ge(out_done, 16 * 12)
            for t in range(KT):
                evac_f(t)
            root()
            squares_of_x(0)
            root()
            affine(0, 1, 1)
            for group in GROUPS:
                for t in group:
                    if t >= 4:
                        act.wait_ge(hid_ready, t - 3)
                    evac(silu_g[:, t % 4, :], ACT.Silu)
                for t in group:
                    evac(up_c[:, t % 4, :])
                if 8 in group:
                    act.wait_ge(s5_loaded, 16 * 7)
                    act.activation(log_dt[:, 2:4], log_dt[:, 0:2], ACT.Exp).then_inc(exp_ready, 1)
                    act.wait_ge(s5_rows_ready, 1)
                    act.activation(R("mag"), R("dr"), ACT.Exp).then_inc(exp_ready, 1)
                    act.wait_ge(s5_rows_ready, 2)
                    act.activation(R("sin"), R("turns"), ACT.Sin, scale=TWO_PI)
                    step(act.activation(R("cos"), R("turns"), ACT.Abs))
                    act.activation(R("cos"), R("cos"), ACT.Sin, scale=-TWO_PI, bias=half_pi[0:S5T, :])\
                        .then_inc(trig_ready, 1)
            for t in range(KT):
                evac_f(t)
            root()
            squares_of_x(1)
            root()
            affine(1, 0, 2)
            for t in range(KT):
                evac(uT[:, t, :])

            def copy(k, n):
                act.wait_ge(tr_full, 3 * k + n + 1)
                if n == 0:
                    out = bbt[:, k % 2, :, :].rearrange("q a b -> q (a b)")
                else:
                    out = ct[:, k % 2, 4 * n - 4:4 * n, :].rearrange("q a b -> q (a b)")
                act.activation(out, bank[7][:, 0:out.shape[1]], ACT.Copy).then_inc(tr_copied, 1)

            def whole(j):
                if j >= 2:
                    act.wait_ge(table_ready, j - 1)
                step(act.activation(turn[j % 2], steps_t, ACT.Identity, scale=cols[:, 5, j:j + 1], bias=magic[:, :]))
                act.activation(turn[j % 2], turn[j % 2], ACT.Identity, bias=minus_magic[:, :])\
                    .then_inc(whole_turns, 1)

            def table(j):
                act.wait_ge(turn_ready, j + 1)
                if j >= 3:
                    act.wait_ge(xre_ready, j - 2)
                    act.wait_ge(xim_ready, j - 2)
                tb = tables[j % 3]
                step(act.activation(tb[:, 0, :], turn[j % 2], ACT.Abs))
                act.activation(tb[:, 0, :], tb[:, 0, :], ACT.Sin, scale=-TWO_PI, bias=half_pi[:, :])
                act.activation(tb[:, 1, :], turn[j % 2], ACT.Sin, scale=TWO_PI).then_inc(table_ready, 1)

            act.wait_ge(s5_cols, 1)
            act.wait_ge(consts_ready, 5)
            act.wait_ge(s5_cols, 2)
            for n in range(3):
                copy(0, n)
            whole(0)
            whole(1)
            table(0)
            whole(2)
            for j in range(S5T):
                if j + 1 < S5T:
                    table(j + 1)
                if j + 3 < S5T:
                    whole(j + 3)
                if j >= 2:
                    last_states(j - 2)
                if j >= 2 and j % 4 != 1 and (j + 2) // 4 < KT:
                    copy((j + 2) // 4, (j + 2) % 4)
                if j % 4 == 3:
                    ada(16 + j // 4)
            last_states(S5T - 2)
            last_states(S5T - 1)
            act.wait_ge(y_used, KT)
            act.activation(hT[:, :, :], hT[:, :, :], ACT.Gelu_apprx_tanh).then_inc(gelu_ready, 1)
            for i in range(2):
                act.wait_ge(s5_t, i + 1)
                if i == 0:
                    act.activation(out_rows.rearrange("q a b -> q (a b)"), bank[1][0:S5T, 0:256], ACT.Copy)\
                        .then_inc(s5_out, 1)
                else:
                    act.activation(s_out_rows.rearrange("q a b -> q (a b)"), bank[2][:, :], ACT.Copy)\
                        .then_inc(s5_out, 1)
            for group in (range(0, 4), range(4, 8)):
                for t in group:
                    evac(fT[:, t, :])
                for t in group:
                    if t >= 4:
                        act.wait_ge(glu_ready, t - 3)
                    evac(zg_sig[:, t % 4, :], ACT.Sigmoid)
                for t in group:
                    act.wait_ge(glu_ready, t + 1)
                    square(t, fT[:, t, :])
            root()
            squares_of_x(2)
            root()
            affine(1, 1, 3)
            act.wait_ge(logits_full, 1)
            act.activation(logits_t, bank[7][0:EXPERTS, 0:T], ACT.Copy).then_inc(logits_copied, 1)
            for n in range(6):
                rows = P if n < 4 else NS
                act.wait_ge(xt_full, n + 1)
                if n >= 4:
                    act.wait_ge(moe_consts, 1)
                act.activation(x_tok[0:rows, n // 2, W * (n % 2):W * (n % 2) + W], bank[n % 4][0:rows, :], ACT.Copy)\
                    .then_inc(xt_copied, 1)
            act.wait_ge(lg_ready, 1)
            act.activation(ex, ex, ACT.Exp).then_inc(lg_ready, 1)

            def xg_hi(j):
                for half in range(2):
                    act.wait_ge(gath_full, 2 * j + half + 1)
                    act.activation(xg[0][:, 4 * half:4 * half + 4, :].rearrange("q a b -> q (a b)"),
                                   bank[7 if half == 0 else 2][:, :], ACT.Copy).then_inc(xg_hi_ready, 1)

            for h in range(3):
                split_hi(act, 0, h)
            xg_hi(0)

            def job(j):
                act.activation(act_table[:, :], half_pi[:, :], ACT.Silu)

                def ht_hi(c):
                    act.wait_ge(ht_full, NCHK * j + c + 1)
                    act.activation(h_t[c % 2][0], bank[6][:, :], ACT.Copy).then_inc(ht_hi_ready, 1)

                for m, (kind, c) in enumerate(kinds):
                    for h in (2 * m, 2 * m + 1):
                        half_free(act, j, h)
                        if h == NH - 1:
                            for half in range(2):
                                ins = act.activation(y_job[:, half, :], bank[4 + half][:, :], ACT.Copy)
                            ins.then_inc(y_ready, 1)
                        split_hi(act, *half_after(j, h))
                    if kind == "gate":
                        if c >= 2:
                            act.wait_ge(h_act_ready, NCHK * j + c - 1)
                        act.activation(g_act[:, c % 2, :], bank[2 * (c % 2)][:, :], ACT.Silu).then_inc(g_ready, 1)
                        if c:
                            ht_hi(c - 1)
                    if (kind, c) == ("down", NCHK - 2):
                        ht_hi(NCHK - 1)
                        xg_hi(j + 1)

            njobs = for_jobs(act, job)
            for k in range(KT):
                act.wait_ge(back_added, KT * njobs + k + 1)
                square(k, fT[:, k, :])
            root()

        @block.vector
        def _(dve):
            count = [0]
            norms = [0]

            def step(ins):
                count[0] += 1
                ins.then_inc(v_step, 1)
                dve.wait_ge(v_step, count[0])

            def mod_rows(i):
                l, j = divmod(i, 12)
                dve.wait_ge(row_t, i + 1)
                rows = row_bank[:, 36 * (i % 2):36 * (i % 2) + 36].rearrange("p (t c) -> p t c", c=NC)
                b = vecA[:, 48 * l + 4 * j:48 * l + 4 * j + 4]
                dve.tensor_tensor(modT[l][:, 4 * j:4 * j + 4, :], rows, bview(b, [P, 4, NC], 2), ALU.add)\
                    .then_inc(mod_ready, 1)

            def coefs(l, part, which):
                g = [bview(vecB[:, (4 * l + 2 * part + j) * KT:(4 * l + 2 * part + j + 1) * KT], [P, KT, NC], 2)
                     for j in range(2)]
                at = 24 * part
                if which == "pre":
                    step(dve.scalar_tensor_tensor(out=coefA[2 * l + part][:, :, :], in0=modT[l][:, at + 8:at + 16, :],
                                                  scalar=1.0, in1=g[0], op0=ALU.add, op1=ALU.mult))
                else:
                    step(dve.tensor_tensor(coefG[2 * l + part][:, :, :], modT[l][:, at + 16:at + 24, :], g[1],
                                           ALU.mult))

            def inverse():
                norms[0] += 1
                dve.wait_ge(root_ready, norms[0])
                step(dve.reciprocal(rstd[:, :], rstd[:, :]))

            wide_rstd = bview(rstd[:, TP:T], [P, KT, NS], 1)

            def pre(l, part):
                inverse()
                A, B = coefA[2 * l + part], modT[l][:, 24 * part:24 * part + 8, :]
                step(dve.tensor_tensor(sq[:, :, TP:T], xT[:, :, TP:T], wide_rstd, ALU.mult))
                step(dve.tensor_tensor(sq[:, :, TP:T], sq[:, :, TP:T], A[:, :, 1:NC], ALU.mult))
                dve.tensor_tensor(hT[:, :, TP:T], sq[:, :, TP:T], B[:, :, 1:NC], ALU.add)
                for k in range(KT):
                    dve.tensor_tensor(sq[:, k, 0:TP], xT[:, k, 0:TP], rstd[:, 0:TP], ALU.mult).then_inc(scaled_ready, 1)

            def post(l, part):
                inverse()
                G = coefG[2 * l + part]
                step(dve.tensor_tensor(sq[:, :, TP:T], fT[:, :, TP:T], wide_rstd, ALU.mult))
                step(dve.tensor_tensor(sq[:, :, TP:T], sq[:, :, TP:T], G[:, :, 1:NC], ALU.mult))
                dve.tensor_tensor(xT[:, :, TP:T], xT[:, :, TP:T], sq[:, :, TP:T], ALU.add)

                def scaled(k):
                    count[0] += 1
                    dve.tensor_tensor(sq[:, k, 0:TP], fT[:, k, 0:TP], rstd[:, 0:TP], ALU.mult).then_inc(v_step, 1)
                    return count[0]

                done = scaled(0)
                for k in range(KT):
                    after = scaled(k + 1) if k + 1 < KT else None
                    dve.wait_ge(v_step, done)
                    dve.scalar_tensor_tensor(out=xT[:, k, 0:TP], in0=sq[:, k, 0:TP], scalar=G[:, k, 0:1],
                                             in1=xT[:, k, 0:TP], op0=ALU.mult, op1=ALU.add).then_inc(x_ready, 1)
                    done = after

            dve.wait_ge(start_t, 2)
            dve.tensor_copy(vecA[:, :], bank[7][:, 96:192])
            dve.tensor_copy(vecB[:, :], bank[7][:, 192:279])
            dve.tensor_copy(convT[:, :, :].rearrange("p k r -> p (k r)"), bank[7][:, 288:352]).then_inc(start_copied, 1)
            dve.wait_ge(start_copied, 1)
            for i in range(4):
                mod_rows(i)
            for k in range(KT):
                dve.wait_ge(start_t, 3 + k)
                ins = dve.tensor_copy(xT[:, k, :], bank[(6, 4)[k % 2]][:, 0:T])
                ins.then_inc(start_copied, 1)
            for i in range(4, 12):
                mod_rows(i)
            dve.wait_ge(mod_ready, 12)
            for part in range(2):
                coefs(0, part, "pre")
                coefs(0, part, "post")
            pre(0, 0)
            dve.wait_ge(gate_parts, 1)
            step(dve.scalar_tensor_tensor(out=z_gate, in0=e_pos, scalar=0.0, in1=e_neg, op0=ALU.min, op1=ALU.subtract))
            dve.wait_ge(consts_ready, 3)
            for a in range(2):
                dve.tensor_tensor_scan(b_cum[:, a, 0:TP], scan_mask, z_gate[:, a, 0:TP], 0.0, ALU.mult, ALU.add)
            dve.tensor_copy(b_cum[:, :, TP:T], z_gate[:, :, TP:T]).then_inc(b_ready, 1)
            dve.wait_ge(b_ready, 1)
            for a in range(2):
                b4 = b_cum[:, a, 0:TP].rearrange("p (c t) -> p c t", t=CH)
                ins = dve.tensor_tensor(e_dec[:, a, :].rearrange("p (c t) -> p c t", t=CH),
                                        b4[:, :, CH - 1:CH].broadcast_to([P, NCH, CH]), b4, ALU.subtract)
            ins.then_inc(b_ready, 1)
            dve.wait_ge(exps_ready, 1)
            dve.tensor_tensor(e_dec, pT[:, K_:K_ + 2, 0:TP], e_dec, ALU.mult).then_inc(kd_ready, 1)
            dve.tensor_tensor(pT[:, Q:Q + 2, 0:TP], pT[:, Q:Q + 2, 0:TP], e_pos[:, :, 0:TP], ALU.mult)
            dve.tensor_tensor(pT[:, K_:K_ + 2, 0:TP], pT[:, K_:K_ + 2, 0:TP], e_neg[:, :, 0:TP], ALU.mult)\
                .then_inc(qk_ready, 1)
            dve.wait_ge(tok_full, 3)
            dve.tensor_copy(v_tok[:, 0, :], bank[6][:, :]).then_inc(tok_copied, 1)
            dve.tensor_copy(v_tok[:, 1, :], bank[7][:, :]).then_inc(tok_copied, 1)
            dve.tensor_copy(vs_tok, bank[4][0:NS, :]).then_inc(tok_copied, 1)
            mod_rows(12)
            dve.wait_ge(tok_full, 4)
            dve.tensor_copy(ks_tok, bank[6][0:NS, 0:256]).then_inc(tok_copied, 1)
            dve.wait_ge(qk_ready, 1)
            dve.wait_ge(tok_full, 5)
            dve.tensor_copy(kd_tok.rearrange("p b n -> p (b n)"), bank[7][:, :]).then_inc(tok_copied, 1)
            for b in range(2):
                dve.wait_ge(att_full, b + 1)
                dve.tensor_tensor(attn[:, b, :].rearrange("p (h i) -> p h i", i=P),
                                  bank[6 + b][:, :].rearrange("p (h i) -> p h i", i=P),
                                  bview(attn_mask, [P, H, P], 1), ALU.mult).then_inc(att_masked, 1)
            for c in range(NCH):
                src = bank[(4, 6, 7, 4)[c]]
                dve.wait_ge(ds_full, c + 1)
                if c:
                    dve.wait_ge(s_ready, c)
                for h in range(H):
                    rows, a = slice(64 * (h % 2), 64 * (h % 2) + 64), h // 2
                    new, add = s_chunk[rows, c, a, :], src[rows, P * h:P * h + P]
                    if c == 0:
                        ins = dve.tensor_copy(new, add)
                    else:
                        last = CH * c + CH - 1
                        ins = dve.scalar_tensor_tensor(out=new, in0=s_chunk[rows, c - 1, a, :],
                                                       scalar=e_pos[rows, a, last:last + 1], in1=add,
                                                       op0=ALU.mult, op1=ALU.add)
                ins.then_inc(s_ready, 1)
            for i in range(1, 4):
                mod_rows(12 + i)
            dve.wait_ge(s0_loaded, 16)
            alpha = e_pos[:, :, TP:T].rearrange("p a s -> p s a")
            step(dve.tensor_tensor(s0, s0, bview(alpha, [P, NS, 2, P], 3), ALU.mult))
            for h in range(H):
                if h >= 2:
                    dve.wait_ge(kv_full, 2 * h - 2)
                dve.wait_ge(tok_copied, 3)
                dve.tensor_tensor(spread_v[:, h % 2, :, :], bview(vs_tok[:, P * h:P * h + P], [NS, NS, P], 1),
                                  bview(ident[0:NS, 0:NS], [NS, NS, P], 2), ALU.mult).then_inc(spread_ready, 1)
                for u in range(2):
                    n = 2 * h + u
                    dve.wait_ge(kv_full, n + 1)
                    rows = slice(64 * (h % 2), 64 * (h % 2) + 64)
                    part = s0[rows, 4 * u:4 * u + 4, h // 2, :]
                    dve.tensor_tensor(part, part, bank[(6, 7, 4)[n % 3]][rows, :].rearrange("p (s v) -> p s v", v=P),
                                      ALU.add).then_inc(kv_added, 1)
            dve.wait_ge(oms_ready, 1)
            for h in range(H):
                src = bank[5][:, 128:128 + T] if h == 3 else bank[(6, 7, 4)[h]][:, 0:T]
                ins = dve.tensor_scalar(head_rstd[:, h, :], src, 1.0 / P, EPS, ALU.mult, ALU.add)
            step(ins)
            dve.reciprocal(head_rstd, head_rstd).then_inc(oinv_ready, 1)
            dve.wait_ge(orstd_ready, 1)
            step(dve.tensor_tensor(oT, oT, head_rstd, ALU.mult))
            dve.scalar_tensor_tensor(out=hT[:, 0:H, :], in0=oT, scalar=vecB[:, 78:79], in1=pT[:, OG:OG + 4, :],
                                     op0=ALU.mult, op1=ALU.mult).then_inc(mixed_o, 1)
            post(0, 0)
            pre(0, 1)

            def R(name):
                return s5_rows[:, ROWS.index(name), :]

            def prepare(part):
                V = dve
                if part == 0:
                    V.wait_ge(exp_ready, 1)
                    dt = bview(log_dt[:, 2:4], [S5T, 2, 64], 2)
                    wide = lambda name: R(name).rearrange("q (g p) -> q g p", p=64)
                    V.tensor_tensor(wide("dr"), wide("are"), dt, ALU.mult).then_inc(s5_rows_ready, 1)
                    step(V.tensor_tensor(wide("th"), wide("aim"), dt, ALU.mult))
                    step(V.tensor_scalar(R("th"), R("th"), INV_TWO_PI, None, ALU.mult))
                    step(V.tensor_scalar(R("tmp"), R("th"), MAGIC, MAGIC, ALU.add, ALU.subtract))
                    step(V.tensor_tensor(R("turns"), R("th"), R("tmp"), ALU.subtract))
                    step(V.tensor_scalar(R("hi"), R("turns"), 3072.0, 3072.0, ALU.add, ALU.subtract))
                    V.tensor_tensor(R("lo"), R("turns"), R("hi"), ALU.subtract).then_inc(s5_rows_ready, 1)
                    V.tensor_tensor(R("den"), R("are"), R("are"), ALU.mult)
                    step(V.tensor_tensor(R("tmp"), R("aim"), R("aim"), ALU.mult))
                    step(V.tensor_tensor(R("den"), R("den"), R("tmp"), ALU.add))
                    step(V.reciprocal(R("den"), R("den")))
                else:
                    V.wait_ge(trig_ready, 1)
                    V.wait_ge(exp_ready, 2)
                    V.tensor_tensor(R("abre"), R("mag"), R("cos"), ALU.mult)
                    step(V.tensor_tensor(R("abim"), R("mag"), R("sin"), ALU.mult))
                    step(V.tensor_scalar(R("cos"), R("abre"), -1.0, None, ALU.add))
                    V.tensor_tensor(R("fre"), R("cos"), R("are"), ALU.mult)
                    step(V.tensor_tensor(R("tmp"), R("abim"), R("aim"), ALU.mult))
                    step(V.tensor_tensor(R("fre"), R("fre"), R("tmp"), ALU.add))
                    V.tensor_tensor(R("fim"), R("abim"), R("are"), ALU.mult)
                    step(V.tensor_tensor(R("tmp"), R("cos"), R("aim"), ALU.mult))
                    step(V.tensor_tensor(R("fim"), R("fim"), R("tmp"), ALU.subtract))
                    V.tensor_tensor(R("fre"), R("fre"), R("den"), ALU.mult)
                    V.tensor_tensor(R("fim"), R("fim"), R("den"), ALU.mult).then_inc(s5_rows_ready, 1)

            for t in range(FT):
                group = GROUPS[t // 4]
                dve.wait_ge(acc_free, TILES["ffn"] + group[0] + len(group) + t + 1)
                dve.tensor_tensor(hid[:, t, :], silu_g[:, t % 4, :], up_c[:, t % 4, :], ALU.mult).then_inc(hid_ready, 1)
                if t == 8:
                    prepare(0)
                if t == 12:
                    prepare(1)
            dve.wait_ge(s5_cols_t, 1)
            dve.tensor_copy(cols.rearrange("q a b -> q (a b)"), bank[7][:, 0:256]).then_inc(s5_cols, 1)
            dve.wait_ge(s5_cols, 1)
            f = [bview(cols[:, 3 + i, :], [P, S5T, 16], 2) for i in range(2)]
            raw = [b_raw[:, i, :].rearrange("q (t i) -> q t i", i=16) for i in range(2)]
            new = [bb[:, i, :].rearrange("q (t i) -> q t i", i=16) for i in range(2)]
            dve.tensor_tensor(new[0], f[0], raw[0], ALU.mult)
            step(dve.tensor_tensor(new[1], f[0], raw[1], ALU.mult))
            dve.tensor_tensor(raw[0], f[1], raw[0], ALU.mult)
            step(dve.tensor_tensor(raw[1], f[1], raw[1], ALU.mult))
            dve.tensor_tensor(new[0], new[0], raw[1], ALU.subtract)
            dve.tensor_tensor(new[1], new[1], raw[0], ALU.add).then_inc(bb_ready, 1)
            dve.wait_ge(bb_ready, 1)
            dve.wait_ge(s5_cols_t, 2)
            ab = [bview(cols[:, 1 + i, :], [P, NS, S5T], 1) for i in range(2)]
            st = [bank[4][:, 256 * i:256 * i + 256].rearrange("q (s t) -> q s t", t=S5T) for i in range(2)]
            dve.tensor_tensor(s_in[:, 0, :, :], ab[0], st[0], ALU.mult)
            dve.tensor_tensor(s_in[:, 1, :, :], ab[0], st[1], ALU.mult)
            dve.tensor_tensor(s_out[:, 0, :, :], ab[1], st[1], ALU.mult)
            step(dve.tensor_tensor(s_out[:, 1, :, :], ab[1], st[0], ALU.mult))
            dve.tensor_tensor(s_in[:, 0, :, :], s_in[:, 0, :, :], s_out[:, 0, :, :], ALU.subtract)
            dve.tensor_tensor(s_in[:, 1, :, :], s_in[:, 1, :, :], s_out[:, 1, :, :], ALU.add).then_inc(s5_cols, 1)
            post(0, 1)
            dve.wait_ge(mod_ready, 16)
            coefs(1, 0, "pre")
            pre(1, 0)
            dve.wait_ge(s5_cols, 2)

            def rest(j):
                dve.wait_ge(whole_turns, j + 1)
                t = turn[j % 2]
                step(dve.scalar_tensor_tensor(out=t, in0=steps_t, scalar=cols[:, 6, j:j + 1], in1=t,
                                              op0=ALU.mult, op1=ALU.subtract))
                dve.scalar_tensor_tensor(out=t, in0=steps_t, scalar=cols[:, 7, j:j + 1], in1=t,
                                         op0=ALU.mult, op1=ALU.add).then_inc(turn_ready, 1)

            def turn_back(j):
                wk, tb = work[j % 3], tables[j % 3]
                re, im = bank[1 + 2 * (j % 2)], bank[2 + 2 * (j % 2)]
                dve.wait_ge(table_ready, j + 1)
                dve.wait_ge(bu_full, j + 1)
                if j >= 3:
                    dve.wait_ge(y_full, j - 2)
                    dve.wait_ge(last_copied, j - 2)
                    dve.wait_ge(xre_ready, j - 2)
                dve.tensor_tensor(wk[:, 0, :], tb[:, 0, :], re[:, 0:TP], ALU.mult)
                dve.tensor_tensor(wk[:, 1, :], tb[:, 1, :], im[:, 0:TP], ALU.mult)
                dve.tensor_tensor(wk[:, 2, :], tb[:, 0, :], im[:, 0:TP], ALU.mult)
                dve.tensor_tensor(wk[:, 3, :], tb[:, 1, :], re[:, 0:TP], ALU.mult)
                dve.tensor_tensor(xri[j % 3][:, 0, TP:T], s_in[:, 0, :, j], re[:, TP:T], ALU.add)
                dve.tensor_tensor(xri[j % 3][:, 1, TP:T], s_in[:, 1, :, j], im[:, TP:T], ALU.add).then_inc(bu_used, 1)

            def scans(j):
                wk = work[j % 3]
                dve.wait_ge(w_ready, j + 1)
                for i in (0, 2):
                    dve.tensor_tensor_scan(wk[:, i, :], cols[:, 0, j:j + 1].broadcast_to([P, TP]), wk[:, i, :], 0.0,
                                           ALU.mult, ALU.add).then_inc(z_ready, 1)

            def rotate_im(j):
                wk, tb, x = work[j % 3], tables[j % 3], xri[j % 3]
                dve.wait_ge(z_ready, 2 * j + 2)
                dve.tensor_tensor(x[:, 1, 0:TP], tb[:, 1, :], wk[:, 0, :], ALU.mult)
                step(dve.tensor_tensor(wk[:, 3, :], tb[:, 0, :], wk[:, 2, :], ALU.mult))
                dve.tensor_tensor(x[:, 1, 0:TP], x[:, 1, 0:TP], wk[:, 3, :], ALU.add).then_inc(xim_ready, 1)

            def s5_y(k):
                dve.wait_ge(y_full, 4 * k + 4)
                dve.scalar_tensor_tensor(out=hT[:, k, :], in0=uT[:, k, :], scalar=vecB[:, 79 + k:80 + k],
                                         in1=bank[6][:, 0:T], op0=ALU.mult, op1=ALU.add).then_inc(y_used, 1)

            rest(0)
            rest(1)
            for j in range(S5T + 1):
                if j < S5T:
                    turn_back(j)
                if j >= 6 and j % 4 == 2:
                    s5_y(j // 4 - 1)
                if j:
                    scans(j - 1)
                if j + 2 < S5T:
                    rest(j + 2)
                if j:
                    rotate_im(j - 1)
                if j % 4 == 1 and j >= 9:
                    mod_rows(14 + j // 4)
            s5_y(KT - 1)
            mod_rows(22)
            mod_rows(23)
            dve.wait_ge(mod_ready, 24)
            coefs(1, 0, "post")
            coefs(1, 1, "pre")
            coefs(1, 1, "post")
            for t in range(KT):
                dve.wait_ge(acc_free, TILES["glu"] + 4 * (t // 4) + 4 + t + 1)
                dve.tensor_tensor(fT[:, t, :], fT[:, t, :], zg_sig[:, t % 4, :], ALU.mult).then_inc(glu_ready, 1)
            post(1, 0)
            pre(1, 1)
            dve.memset(fT[:, :, :], 0.0)
            dve.wait_ge(moe_consts, 1)
            dve.wait_ge(lg_full, 1)
            dve.tensor_copy(lg[:, 0:2, :], bank[7][:, 0:16].rearrange("q (b e) -> q b e", e=EXPERTS))
            step(dve.tensor_copy(lg[0:NS, 2, :], bank[7][0:NS, 16:24]))
            by_e = lambda x: x.rearrange("q (b e) f -> q b e f", e=EXPERTS)
            mine, other = bview(lg, [P, 3, EXPERTS, EXPERTS], 3), bview(lg, [P, 3, EXPERTS, EXPERTS], 2)
            dve.tensor_reduce(m_tok, lg, AX.X, ALU.max)
            dve.tensor_tensor(by_e(cmp_a), other, mine, ALU.is_gt)
            step(dve.tensor_tensor(by_e(cmp_b), other, mine, ALU.is_equal))
            dve.tensor_tensor(ex, lg, bview(m_tok, [P, 3, EXPERTS], 2), ALU.subtract).then_inc(lg_ready, 1)
            step(dve.tensor_tensor(by_e(cmp_b), by_e(cmp_b), bview(earlier, [P, 3, EXPERTS, EXPERTS], 1), ALU.mult))
            step(dve.tensor_tensor(cmp_a, cmp_a, cmp_b, ALU.add))
            step(dve.tensor_reduce(slot_of.rearrange("q b e -> q (b e)"), cmp_a, AX.X, ALU.add))
            step(dve.tensor_scalar(sel, slot_of, 1.5, None, ALU.is_lt))
            dve.wait_ge(lg_ready, 2)
            step(dve.tensor_tensor(comb, ex, sel, ALU.mult))
            step(dve.tensor_tensor(sel, sel, bview(valid, [P, 3, EXPERTS], 2), ALU.mult))
            dve.tensor_reduce(d_tok, comb, AX.X, ALU.add).then_inc(sel_ready, 1)
            dve.wait_ge(sel_ready, 1)
            step(dve.reciprocal(d_tok, d_tok))
            step(dve.tensor_tensor(d_tok, d_tok, valid, ALU.mult))
            step(dve.tensor_tensor(comb, comb, bview(d_tok, [P, 3, EXPERTS], 2), ALU.mult))
            dve.tensor_copy(job_w[:, :, 0:EXPERTS], comb)
            dve.wait_ge(pos_full, 1)
            pos = bank[7][:, 0:24].rearrange("q (b e) -> q b e", e=EXPERTS)
            step(dve.scalar_tensor_tensor(out=slot_of, in0=pos, scalar=-NO_SLOT, in1=sel, op0=ALU.add, op1=ALU.mult))
            step(dve.tensor_scalar(slot_of, slot_of, NO_SLOT, None, ALU.add))
            step(dve.tensor_copy(job_slot[:, :, 0:EXPERTS], slot_of))

            def picks(j):
                for b in range(3):
                    ins = dve.tensor_scalar(pick[:, b, :], slots, job_slot[:, b, bass.ds(j, 1)], None, ALU.is_equal)
                ins.then_inc(pick_ready, 1)

            picks(0)
            for i in range(2):
                ins = dve.tensor_scalar(over[:, :, i], bank[7][:, 24:32], float(P * (i + 1)), None, ALU.is_gt)
            step(ins)
            over_f = over.rearrange("q e b -> q (e b)")
            hot_f = over_hot.rearrange("q e b -> q (e b)")
            step(dve.tensor_tensor_scan(over_pos, ones[:, 0:16], over_f, 0.0, ALU.mult, ALU.add))
            dve.tensor_copy(tabf[:, 0:1], over_pos[:, 15:16])
            step(dve.tensor_tensor(over_at, over_pos, over_f, ALU.subtract))
            for k in range(OVER):
                step(dve.scalar_tensor_tensor(out=hot_f, in0=over_at, scalar=float(k), in1=over_f,
                                              op0=ALU.is_equal, op1=ALU.mult))
                step(dve.tensor_reduce(over_e, over_hot, AX.X, ALU.add))
                step(dve.tensor_tensor(over_tmp, hot_f, lot_base, ALU.mult))
                step(dve.tensor_reduce(over_base, over_tmp, AX.X, ALU.add))
                step(dve.tensor_tensor(over_tmp, hot_f, lot_expert, ALU.mult))
                step(dve.tensor_reduce(tabf[:, 1 + k:2 + k], over_tmp, AX.X, ALU.add))
                wide_e = bview(over_e, [P, 3, EXPERTS], 1)
                step(dve.tensor_tensor(tmp24, slot_of, wide_e, ALU.mult))
                step(dve.tensor_reduce(m_tok, tmp24, AX.X, ALU.add))
                step(dve.tensor_scalar(job_slot[:, :, EXPERTS + k], m_tok, over_base, None, ALU.subtract))
                step(dve.tensor_tensor(tmp24, comb, wide_e, ALU.mult))
                step(dve.tensor_reduce(job_w[:, :, EXPERTS + k], tmp24, AX.X, ALU.add))
            dve.tensor_copy(tabi[:, 0:5], tabf[:, 0:5]).then_inc(jobs_ready, 2)
            dve.wait_ge(jobs_ready, 2)

            def xg_lo(j):
                for half in range(2):
                    dve.wait_ge(xg_hi_ready, 2 * j + half + 1)
                    hi, lo = (xg[i][:, 4 * half:4 * half + 4, :].rearrange("q a b -> q (a b)") for i in range(2))
                    dve.tensor_tensor(lo, bank[7 if half == 0 else 2][:, :], hi.bitcast(F32), ALU.subtract)\
                        .then_inc(xg_lo_ready, 1)

            for h in range(3):
                split_lo(dve, 0, h)
            xg_lo(0)

            def back(j, pair):
                for k in range(2 * pair, 2 * pair + 2):
                    dve.wait_ge(back_full, KT * j + k + 1)
                    dve.tensor_tensor(fT[:, k, :], fT[:, k, :], bank[7 - k % 2][:, 0:T], ALU.add).then_inc(back_added, 1)

            def job(j):
                def ht_lo(c):
                    dve.wait_ge(ht_hi_ready, NCHK * j + c + 1)
                    dve.tensor_tensor(h_t[c % 2][1], bank[6][:, :], h_t[c % 2][0].bitcast(F32), ALU.subtract)\
                        .then_inc(ht_lo_ready, 1)

                for m, (kind, c) in enumerate(kinds):
                    for h in (2 * m, 2 * m + 1):
                        half_free(dve, j, h)
                        split_lo(dve, *half_after(j, h))
                        if c == 0 and kind != "down":
                            back(j, h)
                    if kind == "gate" and c:
                        ht_lo(c - 1)
                    if kind == "up":
                        dve.wait_ge(g_ready, NCHK * j + c + 1)
                        if c >= 2:
                            dve.wait_ge(ht_full, NCHK * j + c - 1)
                        dve.tensor_tensor(h_act[:, c % 2, :], g_act[:, c % 2, :], bank[2 * (c % 2) + 1][:, :],
                                          ALU.mult).then_inc(h_act_ready, 1)
                    if (kind, c) == ("up", 1):
                        for b in range(3):
                            ins = dve.tensor_scalar(pick_w[:, b, :], slots, job_slot[:, b, bass.ds(j, 1)],
                                                    job_w[:, b, bass.ds(j, 1)], ALU.is_equal, ALU.mult)
                        ins.then_inc(pickw_ready, 1)
                    if (kind, c) == ("down", 2):
                        dve.wait_ge(spread_full, j + 1)
                        dve.tensor_copy(spread, bank[7][:, 0:T]).then_inc(spread_copied, 1)
                    if (kind, c) == ("down", 3):
                        picks(j + 1)
                    if (kind, c) == ("down", NCHK - 2):
                        ht_lo(NCHK - 1)
                        xg_lo(j + 1)

            njobs = for_jobs(dve, job)
            for pair in range(KT // 2):
                back(njobs, pair)
            post(1, 1)
            for n in range(6):
                rows = P if n < 4 else NS
                dve.wait_ge(outs_t, n + 1)
                dve.tensor_copy(x_tok[0:rows, n // 2, W * (n % 2):W * (n % 2) + W], bank[n % 4][0:rows, :])\
                    .then_inc(outs_copied, 1)

        @block.tensor
        def _(pe):
            tile = [0]
            piece = [0]
            norms = [0]

            def mm(out, lhsT, rhs, start, stop):
                return pe.matmul(out, lhsT, rhs, start=start, stop=stop, skip_group_check=True)

            count = [0]

            def step(ins):
                count[0] += 1
                ins.then_inc(t_step, 1)
                pe.wait_ge(t_step, count[0])

            def next_tile():
                n = tile[0]
                if TILES["ada1b"] <= n <= TILES["glu"]:
                    pe.wait_ge(acc_free, n)
                elif n >= 4:
                    pe.wait_ge(acc_free, n - 3)
                tile[0] += 1
                return tile_bank(n)

            def next_piece():
                i = piece[0]
                pe.wait_ge(ring_loaded[i % RING], 16 * (i // RING + 1))
                piece[0] += 1
                return slot(i)

            def product(out, w, c, src, kts, first, last):
                for j, k in enumerate(kts):
                    ins = mm(out, w[:, j, c:c + P], src[:, k, :], first and j == 0, last and j == len(kts) - 1)
                return ins

            def ada_part(w, out, ks):
                for k in ks:
                    ins = mm(out[0:NC, :], csT[:, k, :], w[:, k, :], k == 0, k == KT - 1)
                if k == KT - 1:
                    ins.then_inc(acc_full, 1)

            def ada(i):
                ada_part(next_piece(), next_tile(), range(KT))

            def ada_rows(i):
                l_tile = (TILES["ada0"] + i) if i < 12 else (TILES["ada1a"] + i - 12 if i < 16 else TILES["ada1b"] + i - 16)
                pe.wait_ge(acc_free, l_tile + 1)
                if i:
                    pe.wait_ge(mod_ready, i)
                for q in range(4):
                    at = 36 * (i % 2) + NC * q
                    ins = pe.transpose(row_bank[:, at:at + NC], modrow[:, P * q:P * q + P], ident[0:NC, 0:NC])
                ins.then_inc(row_t, 1)

            def mean_square(ks=range(KT)):
                for k in ks:
                    pe.wait_ge(sq_ready, KT * norms[0] + k + 1)
                    ins = mm(ms_bank[:, 0:T], mean_d[:, :], sq[:, k, :], k == 0, k == KT - 1)
                if KT - 1 in ks:
                    ins.then_inc(ms_ready, 1)
                    norms[0] += 1

            def dense(tiles, src, sublayer=None, squares=False):
                for t in range(tiles):
                    if t % 4 == 0:
                        w = next_piece()
                    out = next_tile()[:, 0:T]
                    for k in range(KT):
                        if t == 0 and sublayer is not None:
                            pe.wait_ge(h_ready, KT * sublayer + k + 1)
                        ins = mm(out, w[:, k, P * (t % 4):P * (t % 4) + P], src[:, k, :], k == 0, k == KT - 1)
                    ins.then_inc(acc_full, 1)
                    if squares and t:
                        mean_square([t - 1])

            pe.wait_ge(consts_ready, 2)
            pe.wait_ge(c_loaded, 32)
            for k in range(KT):
                ins = pe.transpose(bank[4][:, NC * k:NC * k + NC], crow[:, P * k:P * k + P], ident[0:NC, 0:NC])
            ins.then_inc(start_t, 1)
            pe.wait_ge(cs_ready, 1)
            ada(0)
            ada(1)
            pe.wait_ge(vec_loaded, 16 * 7)
            pe.transpose(bank[7][:, 96:192], rawA, ident[0:96, 0:96])
            pe.transpose(bank[7][:, 192:279], rawB, ident[0:87, 0:87])
            for k in range(4):
                ins = pe.transpose(bank[7][:, 288 + 16 * k:304 + 16 * k], conv_rows[:, P * k:P * k + P],
                                   ident[0:16, 0:16])
            ins.then_inc(start_t, 1)
            ada_rows(0)
            for i in range(2, 5):
                ada(i)
                ada_rows(i - 1)
            pe.wait_ge(x_loaded, 32)
            for k in range(KT):
                if k >= 2:
                    pe.wait_ge(start_copied, k)
                out = bank[(6, 4)[k % 2]]
                for b in range(2):
                    pe.transpose(out[:, P * b:P * b + P], xrow[:, b, P * k:P * k + P], ident[:, :])
                pe.transpose(out[:, TP:T], xrow[0:NS, 2, P * k:P * k + P], ident[0:NS, 0:NS]).then_inc(start_t, 1)
            for i in range(5, 12):
                ada(i)
                ada_rows(i - 1)
                if i == 9:
                    pe.wait_ge(start_copied, 1 + KT)
                    mean_square()
            ada_rows(11)
            pe.wait_ge(small_loaded, 48)
            out = next_tile()
            for k in range(KT):
                pe.wait_ge(h_ready, k + 1)
                ins = mm(out[0:LOWRANK, 0:T], glr_w[:, k, :], hT[:, k, :], k == 0, k == KT - 1)
            ins.then_inc(acc_full, 1)
            dense(N_IN0, hT)
            for a in range(2):
                mm(bank[6 + a][:, 0:T], gate_up_w[:, P * a:P * a + P], pT[0:LOWRANK, GLR, :], True, True)\
                    .then_inc(z_full, 1)
            pe.wait_ge(z_copied, 2)
            for b in range(2):
                for h in range(H):
                    ins = pe.transpose(bank[6 + b][:, P * h:P * h + P], pT[:, V + h, P * b:P * b + P], ident[:, :])
                ins.then_inc(tok_full, 1)
            for h in range(H):
                ins = pe.transpose(bank[4][0:NS, P * h:P * h + P], pT[:, V + h, TP:T], ident[:, :])
            ins.then_inc(tok_full, 1)
            for i in range(2):
                ada(12 + i)
            ada_rows(12)
            pe.wait_ge(tok_copied, 1)
            for a in range(2):
                ins = pe.transpose(bank[6][0:NS, P * a:P * a + P], pT[:, K_ + a, TP:T], ident[:, :])
            ins.then_inc(tok_full, 1)
            pe.wait_ge(kd_ready, 1)
            pe.wait_ge(tok_copied, 2)
            for b in range(2):
                for a in range(2):
                    at = TP * b + P * a
                    ins = pe.transpose(bank[7][:, at:at + P], e_dec[:, a, P * b:P * b + P], ident[:, :])
            ins.then_inc(tok_full, 1)
            pe.wait_ge(qk_ready, 1)
            for b in range(2):
                pe.wait_ge(tok_copied, 4 + b)
                for h in (0, 2, 1, 3):
                    rows, a = slice(64 * (h % 2), 64 * (h % 2) + 64), h // 2
                    cols_ = slice(P * b, P * b + P)
                    ins = mm(bank[6 + b][:, P * h:P * h + P], pT[rows, K_ + a, cols_], pT[rows, Q + a, cols_], True, True)
                    if h == 2:
                        step(ins)
                ins.then_inc(att_full, 1)
            for c in range(NCH):
                b, rows = c // 2, slice(64 * (c % 2), 64 * (c % 2) + 64)
                if c in (1, 2):
                    pe.wait_ge(att_masked, c)
                if c == 3:
                    pe.wait_ge(s_ready, 1)
                for a in range(2):
                    ins = mm(bank[(4, 6, 7, 4)[c]][:, 256 * a:256 * a + 256], kd_tok[rows, b, P * a:P * a + P],
                             v_tok[rows, b, 256 * a:256 * a + 256], True, True)
                ins.then_inc(ds_full, 1)
            for i in range(2, 4):
                ada(12 + i)
                ada_rows(11 + i)
            ada_rows(15)
            for n in range(2 * H):
                h, u = divmod(n, 2)
                if n < 3:
                    pe.wait_ge(s_ready, n + 2)
                else:
                    pe.wait_ge(kv_added, n - 2)
                pe.wait_ge(spread_ready, h + 1)
                mm(bank[(6, 7, 4)[n % 3]][:, :], ks_tok[:, P * (h // 2):P * (h // 2) + P],
                   spread_v[:, h % 2, 4 * u:4 * u + 4, :].rearrange("p s v -> p (s v)"), True, True).then_inc(kv_full, 1)
            pe.wait_ge(kv_added, 2 * H)
            for h in range(H):
                out = next_tile()
                rows, a = slice(64 * (h % 2), 64 * (h % 2) + 64), h // 2
                for b in range(2):
                    mm(out[:, P * b:P * b + P], v_tok[:, b, P * h:P * h + P], attn[:, b, P * h:P * h + P], b == 0, False)
                for c in range(1, NCH):
                    mm(out[:, CH * c:CH * c + CH], s_chunk[rows, c - 1, a, :], pT[rows, Q + a, CH * c:CH * c + CH],
                       False, False)
                for s in range(NS):
                    ins = mm(out[:, TP + s:TP + s + 1], s0[rows, s, a, :], pT[rows, Q + a, TP + s:TP + s + 1],
                             False, s == NS - 1)
                ins.then_inc(acc_full, 1)
            pe.wait_ge(osq_ready, 1)
            for h in range(H):
                out = bank[5][:, 128:128 + T] if h == 3 else bank[(6, 7, 4)[h]][:, 0:T]
                ins = mm(out, ones[:, :], sq_flat[:, T * h:T * h + T], True, True)
            ins.then_inc(oms_ready, 1)
            pe.wait_ge(mixed_o, 1)
            pe.wait_ge(mixed_y, 1)
            dense(KT, hT, squares=True)
            mean_square([KT - 1])
            mean_square()
            for group in GROUPS:
                for _ in ("gate", "up"):
                    w = next_piece()
                    for t in group:
                        out = next_tile()[:, 0:T]
                        for k in range(KT):
                            if t == 0:
                                pe.wait_ge(h_ready, KT + k + 1)
                            ins = mm(out, w[:, k, P * (t % 4):P * (t % 4) + P], hT[:, k, :], k == 0, k == KT - 1)
                        ins.then_inc(acc_full, 1)
                if 16 in group:
                    pe.wait_ge(s5_rows_ready, 3)
                    for i, name in enumerate(("mag", "abre", "abim", "fre", "fim", "turns", "hi", "lo")):
                        ins = pe.transpose(bank[7][:, S5T * i:S5T * i + S5T], s5_rows[:, ROWS.index(name), :],
                                           ident[0:S5T, 0:S5T])
                    ins.then_inc(s5_cols_t, 1)
                    for i in range(2):
                        for h in range(2):
                            at = 256 * i + P * h
                            ins = pe.transpose(bank[4][:, at:at + P], s_rows[:, i, P * h:P * h + P], ident[:, :])
                    ins.then_inc(s5_cols_t, 1)
            for i in range(4):
                outs = [next_tile()[:, 0:T] for _ in range(2)]
                for half in range(2):
                    w = next_piece()
                    kts = range(half * FT // 2, (half + 1) * FT // 2)
                    if i == 0:
                        pe.wait_ge(hid_ready, kts[-1] + 1)
                    for j, out in enumerate(outs):
                        ins = product(out, w, P * j, hid, kts, half == 0, half == 1)
                        if half == 1:
                            ins.then_inc(acc_full, 1)
                if i:
                    mean_square([2 * i - 2, 2 * i - 1])
            mean_square([KT - 2, KT - 1])
            mean_square()
            dense(KT, hT, sublayer=2)

            def tr(k, n):
                pe.wait_ge(pads_ready, k + 1)
                if k or n:
                    pe.wait_ge(tr_copied, 3 * k + n)
                src = bb_pad.rearrange("q a b -> q (a b)") if n == 0 else c_pad[:, n - 1, :]
                for i in range(2 if n == 0 else 4):
                    ins = pe.transpose(bank[7][:, P * i:P * i + P], src[:, P * i:P * i + P], ident[:, :])
                ins.then_inc(tr_full, 1)

            def bu(j):
                k, r = divmod(j, 4)
                rows = slice(32 * r, 32 * r + 32)
                if r == 0:
                    pe.wait_ge(tr_copied, 3 * k + 1)
                if j >= 2:
                    pe.wait_ge(bu_used, j - 1)
                for i in range(2):
                    ins = mm(bank[1 + 2 * (j % 2) + i][:, 0:T], bbt[rows, k % 2, i, :], uT[rows, k, :], True, True)
                ins.then_inc(bu_full, 1)

            def cx(j):
                k, r = divmod(j, 4)
                if r == 0:
                    pe.wait_ge(tr_copied, 3 * k + 3)
                    if k:
                        pe.wait_ge(y_used, k)
                pe.wait_ge(xre_ready, j + 1)
                pe.wait_ge(xim_ready, j + 1)
                for i in range(2):
                    ins = mm(bank[6][:, 0:T], ct[:, k % 2, 4 * i + r, :], xri[j % 3][:, i, :], r == 0 and i == 0,
                             r == 3 and i == 1)
                ins.then_inc(y_full, 1)

            pe.wait_ge(acc_free, TILES["in1"] + KT)
            for n in range(3):
                tr(0, n)
            bu(0)
            for j in range(S5T + 2):
                if j + 1 < S5T:
                    bu(j + 1)
                if j >= 2:
                    cx(j - 2)
                if 2 <= j < S5T and j % 4 != 1 and (j + 2) // 4 < KT:
                    tr((j + 2) // 4, (j + 2) % 4)
                if j < S5T:
                    if j % 4 == 0:
                        ada_w, ada_out = next_piece(), next_tile()
                    ada_part(ada_w, ada_out, range(2 * (j % 4), 2 * (j % 4) + 2))
                    if j % 4 == 2 and j > 4:
                        ada_rows(15 + j // 4)
            ada_rows(23)
            pe.wait_ge(last_copied, S5T)
            pe.wait_ge(bu_used, S5T)
            for i in range(2):
                ins = pe.transpose(bank[1][0:S5T, P * i:P * i + P], s_last[:, i, :], ident[:, :])
            ins.then_inc(s5_t, 1)
            flat = s_out.rearrange("q i s t -> q i (s t)")
            for i in range(2):
                for h in range(2):
                    ins = pe.transpose(bank[2][:, 256 * i + P * h:256 * i + P * h + P], flat[:, i, P * h:P * h + P],
                                       ident[:, :])
            ins.then_inc(s5_t, 1)
            pe.wait_ge(gelu_ready, 1)
            pe.wait_ge(s5_out, 2)
            dense(2 * KT, hT)
            mean_square()
            mean_square()
            for k in range(KT):
                pe.wait_ge(h_ready, 3 * KT + k + 1)
                ins = mm(bank[7][0:EXPERTS, 0:T], router_w[:, k, :], hT[:, k, :], k == 0, k == KT - 1)
            ins.then_inc(logits_full, 1)

            def token_rows(src, n, full):
                b, cols_ = n // 2, slice(P * (n // 2), min(P * (n // 2) + P, T))
                rows = cols_.stop - cols_.start
                for q in range(4):
                    ins = pe.transpose(bank[n % 4][0:rows, P * q:P * q + P], src[:, 4 * (n % 2) + q, cols_], ident[:, :])
                ins.then_inc(full, 1)

            for n in range(4):
                token_rows(hT, n, xt_full)
            pe.wait_ge(logits_copied, 1)
            for b in range(3):
                rows = P if b < 2 else NS
                ins = pe.transpose(bank[7][0:rows, EXPERTS * b:EXPERTS * b + EXPERTS],
                                   logits_t[:, P * b:P * b + rows], ident[0:EXPERTS, 0:EXPERTS])
            ins.then_inc(lg_full, 1)
            for n in range(4, 6):
                pe.wait_ge(xt_copied, n - 3)
                token_rows(hT, n, xt_full)
            pe.wait_ge(sel_ready, 1)
            for b in range(3):
                out = bank[7][:, EXPERTS * b:EXPERTS * b + EXPERTS]
                for a in range(b + 1):
                    mm(out, (before if a == b else ones[:, :]), sel[:, a, :], a == 0, a == b)
            for a in range(3):
                ins = mm(bank[7][:, 24:32], ones[:, :], sel[:, a, :], a == 0, a == 2)
            ins.then_inc(pos_full, 1)

            def gather(j):
                pe.wait_ge(pick_ready, j + 1)
                for half in range(2):
                    out = bank[7 if half == 0 else 2]
                    for q in range(4):
                        for b in range(3):
                            ins = mm(out[:, P * q:P * q + P], x_tok[:, b, P * (4 * half + q):P * (4 * half + q) + P],
                                     pick[:, b, :], b == 0, b == 2)
                    ins.then_inc(gath_full, 1)

            def back(j, pair):
                for k in range(2 * pair, 2 * pair + 2):
                    if k >= 2:
                        pe.wait_ge(back_added, KT * j + k - 1)
                    mm(bank[7 - k % 2][:, 0:T], y_job[:, k // 4, P * (k % 4):P * (k % 4) + P], spread, True, True)\
                        .then_inc(back_full, 1)

            def job(j):
                def hidden(kind, c, full):
                    out = bank[2 * (c % 2) + (kind == "up")]
                    for h in range(2):
                        n = 2 * kinds.index((kind, c)) + h
                        w = [x[half_slot(n)][:, :].rearrange("p (k n) -> p k n", n=W) for x in (w_hi, w_lo)]
                        pe.wait_ge(lo_ready, half_count(j, n))
                        for k in range(4):
                            for a, b in ((0, 0), (1, 0), (0, 1)):
                                ins = mm(out[:, :], xg[a][:, 4 * h + k, :], w[b][:, k, :], n % 2 == k == a == b == 0,
                                         h == 1 and k == 3 and b == 1)
                        ins.then_inc(full if h else first_half_used, 1)
                        if c == 0:
                            if kind == "gate" and h == 0:
                                pe.wait_ge(y_ready, j)
                            back(j, 2 * (kind == "up") + h)

                def turn_h(c):
                    pe.wait_ge(h_act_ready, NCHK * j + c + 1)
                    if c:
                        pe.wait_ge(ht_lo_ready, NCHK * j + c)
                    for q in range(4):
                        ins = pe.transpose(bank[6][:, P * q:P * q + P], h_act[:, c % 2, P * q:P * q + P], ident[:, :])
                    ins.then_inc(ht_full, 1)

                def down(c):
                    pe.wait_ge(ht_lo_ready, NCHK * j + c + 1)
                    for h in range(2):
                        n = 2 * kinds.index(("down", c)) + h
                        w = [x[half_slot(n)][:, :].rearrange("p (k n) -> p k n", n=D) for x in (w_hi, w_lo)]
                        pe.wait_ge(lo_ready, half_count(j, n))
                        for k in range(2):
                            q = 2 * h + k
                            for a, b in ((0, 0), (1, 0), (0, 1)):
                                for half in range(2):
                                    ins = mm(bank[4 + half][:, :], h_t[c % 2][a][:, P * q:P * q + P],
                                             w[b][:, k, W * half:W * half + W], c == q == a == b == 0,
                                             c == NCHK - 1 and q == 3 and b == 1)
                        ins.then_inc(down_done if h else first_half_used, 1)

                pe.wait_ge(xg_lo_ready, 2 * j + 2)
                hidden("gate", 0, gate_full)
                hidden("up", 0, up_full)
                for c in range(1, NCHK):
                    if c >= 2:
                        pe.wait_ge(h_act_ready, NCHK * j + c - 1)
                    hidden("gate", c, gate_full)
                    if c == 1:
                        pe.wait_ge(back_added, KT * j + KT)
                    turn_h(c - 1)
                    hidden("up", c, up_full)
                    down(c - 1)
                    if c == 3:
                        pe.wait_ge(pickw_ready, j + 1)
                        for b in range(3):
                            rows = P if b < 2 else NS
                            ins = pe.transpose(bank[7][:, P * b:P * b + rows], pick_w[0:rows, b, :],
                                               ident[0:rows, 0:rows])
                        ins.then_inc(spread_full, 1)
                turn_h(NCHK - 1)
                pe.wait_ge(spread_copied, j + 1)
                gather(j + 1)
                down(NCHK - 1)

            pe.wait_ge(xt_copied, 6)
            pe.wait_ge(jobs_ready, 2)
            gather(0)
            njobs = for_jobs(pe, job)
            pe.wait_ge(xg_lo_ready, 2 * njobs + 2)
            pe.wait_ge(y_ready, njobs)
            for pair in range(KT // 2):
                back(njobs, pair)
            pe.wait_ge(back_added, KT * njobs + KT)
            mean_square()
            for n in range(6):
                pe.wait_ge(x_ready, 3 * KT + 4 * (n % 2) + 4)
                if n >= 4:
                    pe.wait_ge(outs_copied, n - 3)
                token_rows(xT, n, outs_t)


_INS = ["x_prompt", "x_sample", "c_prompt", "c_sample", "state_gla", "state_conv", "state_s5_re", "state_s5_im",
        "w_ada", "b_ada", "g_norm", "w_in0", "w_gate_up", "b_gate_up", "g_head_norm", "w_conv", "w_out0",
        "w_ffn_gate", "w_ffn_up", "w_ffn_down", "w_in1", "s5_a_re", "s5_a_im", "s5_log_dt", "s5_b_re", "s5_b_im",
        "s5_c_re", "s5_c_im", "s5_d", "w_glu", "w_router", "w_exp_gate", "w_exp_up", "w_exp_down"]
_OUTS = [((1, TP, D), "float32"), ((NS, 1, D), "float32"), ((1, 1, 4, 64, 128), "float32"),
         ((1, 1, 2, 512), "float32"), ((1, 1, 64, 64), "float32"), ((1, 1, 64, 64), "float32"),
         ((NS, 1, 4, 64, 128), "float32"), ((NS, 1, 2, 512), "float32"), ((NS, 1, 64, 64), "float32"),
         ((NS, 1, 64, 64), "float32")]


def kernel(**inputs):
    import numpy as _np
    import concourse.bacc as _bacc
    from concourse import mybir as _mybir
    from concourse.bass_utils import run_bass_kernel_spmd as _run

    nc = _bacc.Bacc("TRN2", target_bir_lowering=False, num_devices=1)
    arrays, args = {}, []
    for name in _INS:
        a = _np.ascontiguousarray(inputs[name])
        arrays[f"in_{name}_dram"] = a
        args.append(nc.dram_tensor(f"in_{name}_dram", a.shape, _mybir.dt.from_np(a.dtype), kind="ExternalInput").ap())
    for i, (shape, dtype) in enumerate(_OUTS):
        dt = _mybir.dt.from_np(_np.dtype(dtype))
        args.append(nc.dram_tensor(f"out_{i}_dram", shape, dt, kind="ExternalOutput").ap())
    hybrid_trunk(nc, *args)
    r = _run(nc, [arrays], core_ids=[0])
    return tuple(r.results[0][f"out_{i}_dram"] for i in range(len(_OUTS)))
```

```python
from contextlib import ExitStack

import numpy as np

import concourse.bass as bass
from concourse import mybir

ALU = mybir.AluOpType
ACT = mybir.ActivationFunctionType
AX = mybir.AxisListType
F32 = mybir.dt.float32
F32R = mybir.dt.float32r
I32 = mybir.dt.int32

P = 128
D = 1024
KT = D // P
TP = 256
NS = 8
T = TP + NS
NC = 1 + NS
H = 4
CH = 64
NCH = TP // CH
LOWRANK = 16
FF = 2816
FT = FF // P
EXPERTS = 8
FFE = 3584
W = 512
NCHK = FFE // W
S5T = 32
EPS = 1e-6
PIECE = KT * W
RING = 3
HALF = PIECE // 2
MAGIC = 12582912.0
TWO_PI = 6.283185
INV_TWO_PI = 0.15915494309189535
HALF_PI = 1.5707963
NO_SLOT = -1000.0
OVER = 4
JOBS = EXPERTS + OVER

Q, K_, V, OG, CH_H, CH_B, CH_C, GLR = 0, 2, 4, 8, 12, 16, 20, 24
N_IN0 = 24
IN0_COLS = [0, 512, 1024, 1552, 2064, 2576]
GLR_COL = 1536

TILES, _n = {}, 0
for _name, _count in (("ada0", 12), ("glr", 1), ("in0", N_IN0), ("ada1a", 4), ("gla", H), ("out0", KT),
                      ("ffn", 2 * FT), ("down", KT), ("in1", KT), ("ada1b", 8), ("glu", 2 * KT)):
    TILES[_name] = _n
    _n += _count
GROUPS = [range(i, min(i + 4, FT)) for i in range(0, FT, 4)]
EARLY = (0, 1, 2, 12, 13, 14, 18, 38, 39, 40, 42, 43, 44)
OUT_ORDER = (0, 2, 4, 1, 3, 5)
ROWS = ["are", "aim", "dr", "th", "turns", "hi", "lo", "mag", "sin", "cos", "abre", "abim", "den", "fre", "fim", "tmp"]
EXPERT_PIECES = 3 * NCHK
HALVES = 7


def hybrid_trunk(nc, x_prompt, x_sample, c_prompt, c_sample, state_gla, state_conv, state_s5_re, state_s5_im,
                 w_ada, b_ada, g_norm, w_in0, w_gate_up, b_gate_up, g_head_norm, w_conv, w_out0, w_ffn_gate,
                 w_ffn_up, w_ffn_down, w_in1, s5_a_re, s5_a_im, s5_log_dt, s5_b_re, s5_b_im, s5_c_re, s5_c_im,
                 s5_d, w_glu, w_router, w_exp_gate, w_exp_up, w_exp_down,
                 y_prompt, y_sample, gla_prompt, conv_prompt, s5_re_prompt, s5_im_prompt,
                 gla_sample, conv_sample, s5_re_sample, s5_im_sample):
    with ExitStack() as ctx:
        ctx.enter_context(nc.allow_non_contiguous_dma(reason="small vectors and states"))

        def sb(name, shape, dt=F32):
            return ctx.enter_context(nc.sbuf_tensor(name, shape, dt))

        def sem(name):
            return ctx.enter_context(nc.semaphore(name))

        ring = [sb(f"ring{i}", [P, PIECE]) for i in range(RING)]
        w_hi = [sb(f"w_hi{i}", [P, HALF], F32R) for i in range(3)]
        w_lo = [sb(f"w_lo{i}", [P, HALF], F32R) for i in range(3)]
        parts = sb("parts", [P, 2 * KT * T], F32R)
        xT = sb("xT", [P, KT, T])
        hT = sb("hT", [P, KT, T])
        fT = sb("fT", [P, KT, T])
        sq = sb("sq", [P, KT, T])
        rstd = sb("rstd", [P, T])
        modT = [sb(f"modT{i}", [P, 48, NC]) for i in range(2)]
        coefA = [sb(f"coefA{i}", [P, KT, NC]) for i in range(4)]
        coefG = [sb(f"coefG{i}", [P, KT, NC]) for i in range(4)]
        csT = sb("csT", [P, KT, NC])
        vecA = sb("vecA", [P, 96])
        vecB = sb("vecB", [P, 87])
        convT = sb("convT", [P, 4, 2 * NS])
        router_w = sb("router_w", [P, KT, EXPERTS])
        ident = sb("ident", [P, P])
        ones = sb("ones", [P, P])
        mean_d = sb("mean_d", [P, P])
        modrow = sb("modrow", [NC, W])
        half_rows = sb("half_rows", [P, 2])
        group_rows = sb("group_rows", [P, 8])
        minus_group_rows = sb("minus_group_rows", [P, 8])
        half_pi = sb("half_pi", [P, 1])
        eps = sb("eps", [P, 1])
        act_table = sb("act_table", [P, 1])
        magic = sb("magic", [P, 1])
        minus_magic = sb("minus_magic", [P, 1])
        tabi = sb("tabi", [P, 8], I32)
        ARENA = 12608
        arena = sb("arena", [P, ARENA])
        bank = [ctx.enter_context(nc.psum_tensor(f"bank{i}", [P, W], F32)) for i in range(8)]
        row_bank, ms_bank = bank[5], bank[6]

        def tile_bank(n):
            return bank[0 if TILES["ada1b"] <= n < TILES["glu"] else n % 4]

        def shaped(flat, shape):
            if len(shape) == 2:
                return flat.rearrange("p (a b) -> p a b", b=shape[1])
            if len(shape) == 3:
                return flat.rearrange("p (a b c) -> p a b c", b=shape[1], c=shape[2])
            return flat

        def view(at, *shape, rows=P):
            assert at + int(np.prod(shape)) <= ARENA
            return shaped(arena[0:rows, at:at + int(np.prod(shape))], shape)

        sq_flat = sq[:, :, :].rearrange("p a b -> p (a b)")
        fT_flat = fT[:, :, :].rearrange("p a b -> p (a b)")

        def bview(ap, shape, *dims):
            for d in dims:
                ap = ap.unsqueeze(d)
            return ap.broadcast_to(shape)

        xrow = view(0, 3, D)
        crow = view(3072, D, rows=NC)
        rawA = view(4096, P, rows=96)
        rawB = view(4224, P, rows=87)
        conv_rows = view(4352, 512, rows=2 * NS)
        pT = view(0, 25, T)
        v_tok = view(V * T, 2, W)
        kd_tok = view(8712, 2, TP)
        z_gate = view(6600, 2, T)
        b_cum = view(7128, 2, T)
        attn = view(6600, 2, W)
        e_pos = view(8184 - 528, 2, T)
        e_neg = view(8712, 2, T)
        e_dec = view(9240, 2, TP)
        s_chunk = view(9752, NCH, 2, P)
        attn_mask = view(10776, P)
        scan_mask = view(10904, TP)
        ks_tok = view(11160, 256, rows=NS)
        glr_w = view(11416, KT, LOWRANK)
        gate_up_w = view(11544, 256, rows=LOWRANK)
        oT = view(11416, H, T)
        s0 = shaped(fT_flat[:, 0:2 * NS * P], (NS, 2, P))
        spread_v = shaped(sq_flat[0:NS, 0:2 * NS * P], (2, NS, P))
        head_rstd = shaped(sq_flat[:, H * T:2 * H * T], (H, T))
        vs_tok = hT[0:NS, 0:2, :].rearrange("p a b -> p (a b)")[:, 0:512]
        hid = view(0, FT, T)
        silu_g = view(FT * T, 4, T)
        up_c = view((FT + 4) * T, 4, T)

        uT = view(0, KT, T)
        ct = view(2112, 2, 8, P)
        bbt = view(4160, 2, 2, P)
        bb_pad = view(4672, 2, 4 * 32)
        c_pad = view(4928, 2, W)
        xri = [view(at, 2, T) for at in (5952, 6480, 12080)]
        c_raw = view(7920, 2, KT * 64)
        bb = view(8944, 2, W)
        b_raw = view(9968, 2, W)
        s_in = view(9968, 2, NS, S5T)
        s_out = view(9968 + W, 2, NS, S5T)
        cols = view(10992, 8, S5T)
        steps_t = view(11248, TP)
        s_last = view(11504, 2, S5T)
        s_rows = view(11568, 2, TP)
        s5_rows = view(7920, 16, P, rows=S5T)
        log_dt = view(12080, 4, rows=S5T)
        turn = [fT_flat[:, 1024 + TP * i:1024 + TP * i + TP] for i in range(2)]
        tables = [view(7008, 2, TP), shaped(fT_flat[:, 1536:2048], (2, TP)), view(11568, 2, TP)]
        work = [shaped(x, (4, TP)) for x in (sq_flat[:, 0:1024], sq_flat[:, 1024:2048], fT_flat[:, 0:1024])]
        zg_sig = view(5952, 4, T)
        out_rows = view(11568, 2, P, rows=S5T)
        s_out_rows = view(11824, 4, P)
        x_tok = view(0, 3, D)
        def two(at, *shape):
            n = int(np.prod(shape))
            return [shaped(parts[:, at + n * i:at + n * i + n], shape) for i in range(2)]

        xg = two(0, KT, P)
        g_act = view(4096, 2, W)
        h_act = view(5120, 2, W)
        h_t = [two(2048 + 2 * W * i, W) for i in range(2)]
        y_job = view(7168, 2, W)
        pick = view(8192, 3, P)
        pick_w = view(8576, 3, P)
        spread = view(8960, T)
        slots = view(9224, P)
        before = view(9352, P)
        logits_t = view(9480, T, rows=EXPERTS)
        lg = view(9744, 3, EXPERTS)
        sel = view(9768, 3, EXPERTS)
        ex = view(9792, 3, EXPERTS)
        comb = view(9816, 3, EXPERTS)
        slot_of = view(9840, 3, EXPERTS)
        valid = view(9864, 3)
        m_tok = view(9868, 3)
        d_tok = view(9872, 3)
        job_slot = view(9876, 3, JOBS + 1)
        job_w = view(9915, 3, JOBS + 1)
        cmp_a = view(9960, 24, EXPERTS)
        cmp_b = view(10152, 24, EXPERTS)
        earlier = view(10344, EXPERTS, EXPERTS)
        over = view(10408, EXPERTS, 2)
        over_at = view(10424, 16)
        over_pos = view(10440, 16)
        over_hot = view(10456, EXPERTS, 2)
        over_e = view(10472, EXPERTS)
        lot_base = view(10480, 16)
        lot_expert = view(10496, 16)
        over_tmp = view(10512, 16)
        over_base = view(10528, 1)
        tabf = view(10532, 8)
        tmp24 = view(10544, 3, EXPERTS)
        lot_tok = view(10568, 3, 1)

        ring_loaded = [sem(f"ring_loaded{i}") for i in range(RING)]
        half_loaded = [sem(f"half_loaded{i}") for i in range(HALVES)]
        c_loaded, vec_loaded, x_loaded, small_loaded, s0_loaded = (
            sem(n) for n in ("c_loaded", "vec_loaded", "x_loaded", "small_loaded", "s0_loaded"))
        consts_ready, v_step, p_step, a_step, t_step = (
            sem(n) for n in ("consts_ready", "v_step", "p_step", "a_step", "t_step"))
        start_t, start_copied, cs_ready = (sem(n) for n in ("start_t", "start_copied", "cs_ready"))
        acc_full, acc_free, row_t, mod_ready = (sem(n) for n in ("acc_full", "acc_free", "row_t", "mod_ready"))
        sq_ready, ms_ready, root_ready, scaled_ready, h_ready, x_ready = (
            sem(n) for n in ("sq_ready", "ms_ready", "root_ready", "scaled_ready", "h_ready", "x_ready"))
        z_full, z_copied, gate_parts, b_ready, exps_ready, kd_ready, qk_ready = (
            sem(n) for n in ("z_full", "z_copied", "gate_parts", "b_ready", "exps_ready", "kd_ready", "qk_ready"))
        tok_full, tok_copied, att_full, att_masked, ds_full, s_ready = (
            sem(n) for n in ("tok_full", "tok_copied", "att_full", "att_masked", "ds_full", "s_ready"))
        spread_ready, kv_full, kv_added, mixed_o, mixed_y, conv_u = (
            sem(n) for n in ("spread_ready", "kv_full", "kv_added", "mixed_o", "mixed_y", "conv_u"))
        osq_ready, oms_ready, oroot_ready = (sem(n) for n in ("osq_ready", "oms_ready", "oroot_ready"))
        s5_loaded, c_raw_loaded, s5_rows_ready, exp_ready, trig_ready, s5_cols_t, s5_cols = (
            sem(n) for n in ("s5_loaded", "c_raw_loaded", "s5_rows_ready", "exp_ready", "trig_ready", "s5_cols_t",
                             "s5_cols"))
        bb_ready, pads_ready, tr_full, tr_copied = (sem(n) for n in ("bb_ready", "pads_ready", "tr_full", "tr_copied"))
        whole_turns, turn_ready, table_ready, bu_full, bu_used, w_ready, z_ready, xre_ready, xim_ready, y_full, y_used = (
            sem(n) for n in ("whole_turns", "turn_ready", "table_ready", "bu_full", "bu_used", "w_ready", "z_ready",
                             "xre_ready", "xim_ready", "y_full", "y_used"))
        last_copied, gelu_ready, s5_t, s5_out, glu_ready, s5_stored = (
            sem(n) for n in ("last_copied", "gelu_ready", "s5_t", "s5_out", "glu_ready", "s5_stored"))
        logits_full, logits_copied, lg_full, xt_full, xt_copied, moe_consts, lg_ready, sel_ready, pos_full, jobs_ready = (
            sem(n) for n in ("logits_full", "logits_copied", "lg_full", "xt_full", "xt_copied", "moe_consts",
                             "lg_ready", "sel_ready", "pos_full", "jobs_ready"))
        part_hi, part_lo = sem("part_hi"), sem("part_lo")
        over_ready = sem("over_ready")
        first_half_used, hi_ready, lo_ready = (sem(n) for n in ("first_half_used", "hi_ready", "lo_ready"))
        gath_full, xg_hi_ready, xg_lo_ready, gate_full, up_full, g_ready, h_act_ready, ht_full, ht_hi_ready, ht_lo_ready, down_done = (
            sem(n) for n in ("gath_full", "xg_hi_ready", "xg_lo_ready", "gate_full", "up_full", "g_ready", "h_act_ready",
                             "ht_full", "ht_hi_ready", "ht_lo_ready", "down_done"))
        y_ready, pick_ready, pickw_ready, spread_full, spread_copied, back_full, back_added = (
            sem(n) for n in ("y_ready", "pick_ready", "pickw_ready", "spread_full", "spread_copied",
                             "back_full", "back_added"))
        outs_t, outs_copied_act, outs_copied_dve, y_stored = (
            sem(n) for n in ("outs_t", "outs_copied_act", "outs_copied_dve", "y_stored"))
        hid_ready, out_done = sem("hid_ready"), sem("out_done")

        def columns(w, c0, n=W):
            return w[:, c0:c0 + n].rearrange("(k p) n -> p k n", p=P), KT, n

        pieces = [columns(w_ada[0], W * i) for i in range(12)]
        pieces += [columns(w_in0[0], c) for c in IN0_COLS]
        pieces += [columns(w_ada[1], W * i) for i in range(4)]
        pieces += [columns(w_out0[0], W * i) for i in range(2)]
        for i in range(0, FF, W):
            n = min(W, FF - i)
            pieces += [columns(w_ffn_gate[0], i, n), columns(w_ffn_up[0], i, n)]
        for i in range(4):
            for half in range(2):
                rows = w_ffn_down[0][half * FF // 2:(half + 1) * FF // 2, 256 * i:256 * i + 256]
                pieces.append((rows.rearrange("(k p) n -> p k n", p=P), FT // 2, 256))
        pieces += [columns(w_in1[0], W * i) for i in range(2)]
        pieces += [columns(w_ada[1], W * i) for i in range(4, 12)]
        for i in range(2):
            pieces += [columns(w_glu[0], W * i), columns(w_glu[0], D + W * i)]

        dense_halves = []
        first_tile = {12: TILES["in0"], 22: TILES["out0"], 24: TILES["ffn"], 44: TILES["in1"], 54: TILES["glu"]}
        for i in [*range(12, 18), 22, 23, *range(24, 36), 44, 45, *range(54, 58)]:
            n = first_tile.get(i, dense_halves[-1][2] if dense_halves else None)
            dense_halves += [(i, q, n + 2 * q + 2) for q in range(pieces[i][2] // 256)]
        DENSE_HALVES = len(dense_halves)
        used = [(acc_full, TILES["ada0"] + i + 1) for i in range(12)] + [None] * 6
        used += [(acc_full, TILES["ada1a"] + i + 1) for i in range(4)] + [None] * 14
        used += [(acc_full, TILES["down"] + 2 * (i // 2) + 2) for i in range(8)] + [None] * 2
        used += [(acc_full, TILES["ada1b"] + i + 1) for i in range(8)] + [None] * 4
        for n, (i, _, _) in enumerate(dense_halves):
            used[i] = (lo_ready, n + 1)
        assert len(used) == len(pieces)
        PARTS_OF = {"in0": 0, "out0": KT, "ffn": KT + 5, "in1": 2 * KT + 5, "glu": 3 * KT + 5}
        h_parts = two(0, KT, T)

        def slot(i):
            _, k, n = pieces[i]
            return ring[i % RING][:, 0:k * n].rearrange("p (k n) -> p k n", n=n)

        NPIECES = len(pieces)

        def dense_half(n):
            i, q, _ = dense_halves[n]
            return slot(i)[:, :, 256 * q:256 * q + 256], [x[n % 3][:, :].rearrange("p (k n) -> p k n", n=256)
                                                         for x in (w_hi, w_lo)]

        def split_dense_hi(act, n):
            i, _, _ = dense_halves[n]
            act.wait_ge(ring_loaded[i % RING], 16 * (i // RING + 1))
            if n >= 3:
                act.wait_ge(acc_full, dense_halves[n - 3][2])
            raw, (hi, _) = dense_half(n)
            act.activation(hi, raw, ACT.Copy).then_inc(hi_ready, 1)

        def split_dense_lo(dve, n):
            dve.wait_ge(hi_ready, n + 1)
            raw, (hi, lo) = dense_half(n)
            dve.tensor_tensor(lo, raw, hi.bitcast(F32), ALU.subtract).then_inc(lo_ready, 1)


        kinds = [("gate", 0), ("up", 0)]
        for c in range(1, NCHK):
            kinds += [("gate", c), ("up", c), ("down", c - 1)]
        kinds.append(("down", NCHK - 1))
        released = {"gate": gate_full, "up": up_full, "down": down_done}
        NH = 2 * EXPERT_PIECES

        half_ring = [ring[(NPIECES + i // 2) % RING][:, HALF * (i % 2):HALF * (i % 2) + HALF] for i in range(2 * RING)]
        half_ring.append(hT[:, :, :].rearrange("p a b -> p (a b)")[:, 0:HALF])

        def loaded_count(j, h):
            return 16 * (NH // HALVES) * j + 16 * (h // HALVES + 1)

        def half_slot(h):
            return (DENSE_HALVES + h) % 3

        def half_count(j, h):
            return NH * j + DENSE_HALVES + h + 1

        def half_free(eng, j, h):
            kind, c = kinds[h // 2]
            if h % 2 == 0:
                eng.wait_ge(first_half_used, EXPERT_PIECES * j + h // 2 + 1)
            else:
                eng.wait_ge(released[kind], NCHK * j + c + 1)

        def split_hi(act, j, h):
            act.wait_ge(half_loaded[h % HALVES], loaded_count(j, h))
            act.activation(w_hi[half_slot(h)][:, :], half_ring[h % HALVES], ACT.Copy).then_inc(hi_ready, 1)

        def split_lo(dve, j, h):
            dve.wait_ge(hi_ready, half_count(j, h))
            dve.tensor_tensor(w_lo[half_slot(h)][:, :], half_ring[h % HALVES], w_hi[half_slot(h)][:, :].bitcast(F32),
                              ALU.subtract).then_inc(lo_ready, 1)

        def half_after(j, h):
            return (j, h + 3) if h + 3 < NH else (j + 1, h + 3 - NH)

        def for_jobs(eng, body):
            with eng.Fori(0, EXPERTS) as j:
                body(j)
            eng.wait_ge(jobs_ready, 2)
            more = eng.value_load(tabi[0:1, 0:1], min_val=0, max_val=OVER)
            with eng.If(more > 0):
                with eng.Fori(0, more) as k:
                    body(k + EXPERTS)
            return more + EXPERTS

        block = ctx.enter_context(nc.Block())

        @block.sync
        def _(sp):
            sp.dma_start(crow[0:1, :], c_prompt).then_inc(c_loaded, 16)
            sp.dma_start(crow[1:NC, :], c_sample).then_inc(c_loaded, 16)
            for i, (src, k, n) in enumerate(pieces):
                if i >= RING:
                    sp.wait_ge(*used[i - RING])
                sp.dma_start(slot(i), src).then_inc(ring_loaded[i % RING], 16)

            def load(j, h, e, first=False):
                if not first:
                    sp.wait_ge(lo_ready, half_count(j, h - HALVES))
                elif h < 2 * RING:
                    sp.wait_ge(*used[NPIECES - RING + h // 2])
                else:
                    sp.wait_ge(xt_full, 6)
                kind, c = kinds[h // 2]
                if kind == "down":
                    at = W * c + W // 2 * (h % 2)
                    rows = w_exp_down[0].rearrange("e f n -> (e f) n")[bass.ds(e * FFE + at, W // 2), :]
                    src = rows.rearrange("(k p) n -> p k n", p=P)
                else:
                    w = w_exp_gate if kind == "gate" else w_exp_up
                    at = D // 2 * (h % 2)
                    rows = w[0].rearrange("e f n -> (e f) n")[bass.ds(e * D + at, D // 2), W * c:W * c + W]
                    src = rows.rearrange("(k p) n -> p k n", p=P)
                to = half_ring[h % HALVES].rearrange("p (k n) -> p k n", n=D if kind == "down" else W)
                sp.dma_start(to, src).then_inc(half_loaded[h % HALVES], 16)

            def job(j, e, after):
                for h in range(HALVES, NH):
                    load(j, h, e)
                for h in range(HALVES):
                    load(j + 1, h, after)

            def expert_of(n):
                return sp.value_load(tabi[0:1, bass.ds(n + 1, 1)], min_val=0, max_val=EXPERTS - 1)

            for h in range(HALVES):
                load(0, h, 0, first=True)
            with sp.Fori(0, EXPERTS - 1) as j:
                job(j, j, j + 1)
            sp.wait_ge(jobs_ready, 2)
            more = sp.value_load(tabi[0:1, 0:1], min_val=0, max_val=OVER)
            for h in range(HALVES, NH):
                load(EXPERTS - 1, h, EXPERTS - 1)
            after = expert_of(0)
            for h in range(HALVES):
                load(EXPERTS, h, after)
            with sp.If(more > 0):
                with sp.Fori(0, more) as k:
                    job(k + EXPERTS, expert_of(k), expert_of(k + 1))
            njobs = more + EXPERTS
            end = sp.snap(loaded_count(njobs, 0))
            for b in range(3):
                for h in range(3 * b, min(3 * b + 3, HALVES)):
                    sp.wait_ge(half_loaded[h], end)
                sp.wait_ge(outs_copied_act, (1, 4, 3)[b])
                sp.wait_ge(outs_copied_dve, (1, 1, 2)[b])
                if b < 2:
                    sp.dma_start(y_prompt[0, P * b:P * b + P, :], x_tok[:, b, :]).then_inc(y_stored, 16)
                else:
                    sp.dma_start(y_sample[:, 0, :], x_tok[0:NS, b, :]).then_inc(y_stored, 16)
            sp.wait_ge(y_stored, 48)

        @block.gpsimd
        def _(pool):
            count = [0]

            def step(ins):
                count[0] += 1
                ins.then_inc(p_step, 1)
                pool.wait_ge(p_step, count[0])

            step(pool.memset(ident[:, :], 0.0))
            pool.affine_select(out=ident[:, :], in_=ident[:, :], compare_op=ALU.not_equal, fill=1.0, base=0,
                               pattern=[[-1, P]], channel_multiplier=1).then_inc(consts_ready, 1)
            pool.memset(ones[:, :], 1.0)
            pool.memset(mean_d[:, :], 1.0 / D)
            pool.memset(half_pi[:, :], HALF_PI)
            pool.memset(eps[:, :], EPS)
            pool.memset(magic[:, :], MAGIC)
            pool.memset(minus_magic[:, :], -MAGIC).then_inc(consts_ready, 1)
            step(pool.memset(attn_mask, 1.0))
            step(pool.affine_select(out=attn_mask, in_=attn_mask, compare_op=ALU.is_ge, fill=0.0, base=0,
                                    pattern=[[1, P]], channel_multiplier=-1))
            step(pool.memset(attn_mask[0:CH, CH:P], 0.0))
            step(pool.memset(scan_mask, 1.0))
            pool.memset(scan_mask.rearrange("p (c t) -> p c t", t=CH)[:, :, 0:1], 0.0).then_inc(consts_ready, 1)
            step(pool.memset(half_rows[:, :], 0.0))
            step(pool.memset(half_rows[0:64, 0:1], 1.0))
            step(pool.memset(half_rows[64:P, 1:2], 1.0))
            for m, v in ((group_rows, 1.0), (minus_group_rows, -1.0)):
                step(pool.memset(m[:, :], v))
                step(pool.affine_select(out=m[:, :], in_=m[:, :], compare_op=ALU.is_ge, fill=0.0, base=0,
                                        pattern=[[-16, 8]], channel_multiplier=1))
                ins = pool.affine_select(out=m[:, :], in_=m[:, :], compare_op=ALU.is_ge, fill=0.0, base=15,
                                         pattern=[[16, 8]], channel_multiplier=-1)
            ins.then_inc(consts_ready, 1)
            pool.dma_start(glr_w, w_in0[0][:, GLR_COL:GLR_COL + LOWRANK].rearrange("(k p) n -> p k n", p=P))\
                .then_inc(small_loaded, 16)
            pool.dma_start(gate_up_w, w_gate_up[0]).then_inc(small_loaded, 16)
            pool.dma_start(router_w[:, :, :], w_router[0].rearrange("(k p) e -> p k e", p=P))\
                .then_inc(small_loaded, 16)
            pool.dma_start(s0, state_gla.rearrange("s n (a h) d v -> (h d) s (n a) v", h=2)).then_inc(s0_loaded, 16)
            pool.wait_ge(acc_free, TILES["in0"] + N_IN0)
            u = pT[:, CH_C:CH_C + 4, :]
            tmp = pT[:, CH_H:CH_H + 4, :]
            y = hT[:, 4:8, :]

            def wc(j, n):
                return bview(vecB[:, 66 + 4 * j:70 + 4 * j], [P, 4, n], 2)

            pool.tensor_tensor(u, u, tmp, ALU.mult).then_inc(conv_u, 1)
            pool.wait_ge(conv_u, 1)
            step(pool.tensor_tensor(y, u, wc(2, T), ALU.mult))
            for j, lag in ((1, 1), (0, 2)):
                step(pool.tensor_tensor(tmp[:, :, 0:TP - lag], u[:, :, 0:TP - lag], wc(j, TP - lag), ALU.mult))
                step(pool.tensor_tensor(y[:, :, lag:TP], y[:, :, lag:TP], tmp[:, :, 0:TP - lag], ALU.add))
                old = convT[:, :, :].rearrange("p k (s j) -> p k s j", j=2)[:, :, :, j]
                step(pool.tensor_tensor(tmp[:, :, TP:T], old, wc(j, NS), ALU.mult))
                step(pool.tensor_tensor(y[:, :, TP:T], y[:, :, TP:T], tmp[:, :, TP:T], ALU.add))
            pool.tensor_tensor(y, y, pT[:, CH_B:CH_B + 4, :], ALU.mult).then_inc(mixed_y, 1)
            n = 0
            for k in range(4):
                pool.dma_start(conv_prompt[0, 0, :, P * k:P * k + P].rearrange("j p -> p j"),
                               u[:, k, TP - 2:TP]).then_inc(out_done, 16)
                pool.dma_start(conv_sample[:, 0, 1, P * k:P * k + P].rearrange("s p -> p s"),
                               u[:, k, TP:T]).then_inc(out_done, 16)
            pool.dma_start(conv_sample[:, 0, 0, :], state_conv[:, 0, 1, :]).then_inc(out_done, 16)
            pool.wait_ge(s_ready, NCH)
            for h in range(2):
                rows = slice(64 * h, 64 * h + 64)
                pool.dma_start(gla_prompt[0, 0].rearrange("(a h) d v -> h d a v", h=2)[h],
                               s_chunk[rows, NCH - 1, :, :]).then_inc(out_done, 16)
            pool.wait_ge(kv_added, 2 * H)
            pool.dma_start(gla_sample.rearrange("s n (a h) d v -> (h d) s (n a) v", h=2), s0).then_inc(out_done, 16)
            pool.wait_ge(out_done, 16 * 12)
            pool.wait_ge(mixed_o, H)
            for i, src in enumerate((s5_a_re, s5_a_im)):
                pool.dma_start(s5_rows[:, i, :], src[0].rearrange("(t g) p -> t (g p)", g=2)).then_inc(s5_loaded, 16)
            pool.dma_start(log_dt[:, 0:2], s5_log_dt[0].rearrange("(t g) -> t g", g=2)).then_inc(s5_loaded, 16)
            for i, src in enumerate((s5_b_re, s5_b_im)):
                pool.dma_start(b_raw[:, i, :].rearrange("q (t i) -> q t i", i=16),
                               src[0].rearrange("(t g) p i -> (g p) t i", g=2)).then_inc(s5_loaded, 16)
            for i, src in enumerate((state_s5_re, state_s5_im)):
                pool.dma_start(s_rows[:, i, :].rearrange("q (h n) -> q h n", h=2),
                               src.rearrange("(h s) n (t g) p -> (s n t) h (g p)", h=2, g=2)).then_inc(s5_loaded, 16)
            pool.iota(steps_t, pattern=[[1, TP]], base=1, channel_multiplier=0,
                      allow_small_or_imprecise_dtypes=True).then_inc(consts_ready, 1)
            pool.wait_ge(s5_cols, 1)
            for i, src in enumerate((s5_c_re, s5_c_im)):
                pool.dma_start(c_raw[:, i, :].rearrange("q (k p) -> q k p", p=64),
                               src[0].rearrange("(k g) i p -> (g i) k p", g=8)).then_inc(c_raw_loaded, 16)
            pool.wait_ge(c_raw_loaded, 32)
            pool.wait_ge(bb_ready, 1)
            pool.wait_ge(acc_full, TILES["down"] + KT)
            pool.wait_ge(consts_ready, 5)

            def pads(k):
                if k:
                    pool.wait_ge(tr_full, 3 * k)
                for i in range(2):
                    pool.tensor_tensor(bb_pad[:, i, :].rearrange("q (t g i) -> q t g i", g=2, i=16),
                                       bview(bb[:, i, 64 * k:64 * k + 64].rearrange("q (t i) -> q t i", i=16),
                                             [P, 4, 2, 16], 2),
                                       bview(half_rows[:, :], [P, 4, 2, 16], 1, 3), ALU.mult)
                    ins = pool.tensor_tensor(c_pad[:, i, :].rearrange("q (g p) -> q g p", p=64),
                                             bview(c_raw[:, i, 64 * k:64 * k + 64], [P, 8, 64], 1),
                                             bview((group_rows, minus_group_rows)[i][:, :], [P, 8, 64], 2), ALU.mult)
                ins.then_inc(pads_ready, 1)

            def rotate_re(j):
                wk, tb, x = work[j % 3], tables[j % 3], xri[j % 3]
                pool.wait_ge(z_ready, 2 * j + 2)
                pool.tensor_tensor(x[:, 0, 0:TP], tb[:, 0, :], wk[:, 0, :], ALU.mult)
                step(pool.tensor_tensor(wk[:, 1, :], tb[:, 1, :], wk[:, 2, :], ALU.mult))
                pool.tensor_tensor(x[:, 0, 0:TP], x[:, 0, 0:TP], wk[:, 1, :], ALU.subtract).then_inc(xre_ready, 1)

            pads(0)
            for j in range(S5T + 1):
                if j < S5T:
                    wk = work[j % 3]
                    pool.wait_ge(bu_used, j + 1)
                    pool.tensor_tensor(wk[:, 0, :], wk[:, 0, :], wk[:, 1, :], ALU.add)
                    pool.tensor_tensor(wk[:, 2, :], wk[:, 2, :], wk[:, 3, :], ALU.subtract).then_inc(w_ready, 1)
                if j:
                    rotate_re(j - 1)
                if j % 4 == 1 and j // 4 + 1 < KT:
                    pads(j // 4 + 1)
            pool.wait_ge(s5_out, 2)
            for i, (a, b) in enumerate(((s5_re_prompt, s5_re_sample), (s5_im_prompt, s5_im_sample))):
                pool.dma_start(a[0, 0].rearrange("(t g) p -> t (g p)", g=2), out_rows[:, i, :]).then_inc(s5_stored, 16)
                pool.dma_start(b.rearrange("(h s) n (t g) p -> (s n t) h (g p)", h=2, g=2),
                               s_out_rows[:, 2 * i:2 * i + 2, :]).then_inc(s5_stored, 16)
            pool.wait_ge(s5_stored, 64)
            pool.wait_ge(glu_ready, KT)
            pool.iota(slots, pattern=[[1, P]], base=0, channel_multiplier=0, allow_small_or_imprecise_dtypes=True)
            pool.iota(lot_base, pattern=[[0, EXPERTS], [P, 2]], base=P, channel_multiplier=0,
                      allow_small_or_imprecise_dtypes=True)
            pool.iota(lot_expert, pattern=[[1, EXPERTS], [0, 2]], base=0, channel_multiplier=0,
                      allow_small_or_imprecise_dtypes=True)
            pool.memset(y_job, 0.0).then_inc(y_ready, 2)
            pool.memset(spread, 0.0)
            pool.memset(x_tok[:, 2, :], 0.0)
            pool.memset(lg[:, 2, :], 0.0)
            pool.memset(valid, 1.0)
            pool.memset(job_slot, NO_SLOT)
            pool.memset(job_w, 0.0)
            pool.memset(tabf, 0.0)
            pool.memset(before, 1.0)
            pool.wait_ge(x_ready, 3 * KT)
            pool.memset(fT[:, :, :], 0.0).then_inc(moe_consts, 1)
            step(pool.memset(earlier, 1.0))
            pool.affine_select(out=valid[:, 2:3], in_=valid[:, 2:3], compare_op=ALU.is_gt, fill=0.0, base=NS,
                               pattern=[[0, 1]], channel_multiplier=-1)
            pool.affine_select(out=before, in_=before, compare_op=ALU.is_gt, fill=0.0, base=0,
                               pattern=[[1, P]], channel_multiplier=-1)
            pool.affine_select(out=earlier, in_=earlier, compare_op=ALU.is_gt, fill=0.0, base=0,
                               pattern=[[1, EXPERTS], [-1, EXPERTS]], channel_multiplier=0).then_inc(moe_consts, 1)
            over_f = over.rearrange("q e b -> q (e b)")
            hot_f = over_hot.rearrange("q e b -> q (e b)")

            def total(out, x, n):
                at = (slice(None),) * (len(x.shape) - 1)
                while n > 2:
                    n //= 2
                    low = x[at + (slice(0, n),)]
                    step(pool.tensor_tensor(low, low, x[at + (slice(n, 2 * n),)], ALU.add))
                step(pool.tensor_tensor(out, x[at + (slice(0, 1),)], x[at + (slice(1, 2),)], ALU.add))

            pool.wait_ge(over_ready, 1)
            pool.tensor_copy(tabf[:, 0:1], over_pos[:, 15:16])
            step(pool.tensor_tensor(over_at, over_pos, over_f, ALU.subtract))
            for k in range(OVER):
                step(pool.tensor_scalar(hot_f, over_at, float(k), None, ALU.is_equal))
                step(pool.tensor_tensor(hot_f, hot_f, over_f, ALU.mult))
                step(pool.tensor_tensor(over_e, over_hot[:, :, 0], over_hot[:, :, 1], ALU.add))
                step(pool.tensor_tensor(over_tmp, hot_f, lot_base, ALU.mult))
                total(over_base, over_tmp, 2 * EXPERTS)
                step(pool.tensor_tensor(over_tmp, hot_f, lot_expert, ALU.mult))
                total(tabf[:, 1 + k:2 + k], over_tmp, 2 * EXPERTS)
                wide_e = bview(over_e, [P, 3, EXPERTS], 1)
                step(pool.tensor_tensor(tmp24, slot_of, wide_e, ALU.mult))
                total(lot_tok, tmp24, EXPERTS)
                step(pool.tensor_scalar(job_slot[:, :, EXPERTS + k:EXPERTS + k + 1], lot_tok, over_base, None, ALU.subtract))
                step(pool.tensor_tensor(tmp24, comb, wide_e, ALU.mult))
                total(job_w[:, :, EXPERTS + k:EXPERTS + k + 1], tmp24, EXPERTS)
            pool.tensor_copy(tabi[:, :], tabf).then_inc(jobs_ready, 2)

        @block.scalar
        def _(act):
            count = [0]
            tile = [0]
            norms = [0]

            def step(ins):
                count[0] += 1
                ins.then_inc(a_step, 1)
                act.wait_ge(a_step, count[0])

            act.dma_start(rawA, b_ada.rearrange("l (t p) -> (l t) p", p=P)).then_inc(vec_loaded, 16)
            for at, src in ((0, g_norm.rearrange("l j (t p) -> (l j t) p", p=P)),
                            (64, b_gate_up.rearrange("l (t p) -> (l t) p", p=P)),
                            (66, w_conv.rearrange("l j (t p) -> (l j t) p", p=P)),
                            (78, g_head_norm),
                            (79, s5_d.rearrange("l (t g) i -> (l t) (g i)", g=8))):
                act.dma_start(rawB[at:at + src.shape[0], :], src).then_inc(vec_loaded, 16)
            act.dma_start(conv_rows, state_conv.rearrange("s n j c -> (s n j) c")).then_inc(vec_loaded, 16)
            act.dma_start(xrow[:, 0:2, :], x_prompt[0].rearrange("(b p) d -> p b d", p=P)).then_inc(x_loaded, 16)
            act.dma_start(xrow[0:NS, 2, :], x_sample[:, 0, :]).then_inc(x_loaded, 16)

            def evac(out, func=ACT.Copy, rows=P, n=T, **more):
                act.wait_ge(acc_full, tile[0] + 1)
                act.activation(out, tile_bank(tile[0])[0:rows, 0:n], func, **more).then_inc(acc_free, 1)
                tile[0] += 1
                for m, (_, _, full) in enumerate(dense_halves):
                    if full == tile[0] and m + 3 < DENSE_HALVES and m + 3 not in EARLY:
                        split_dense_hi(act, m + 3)

            def ada(i):
                if i:
                    act.wait_ge(row_t, i)
                evac(modrow[:, :], rows=NC, n=W)

            def square(k, src):
                act.activation(sq[:, k, :], src, ACT.Square).then_inc(sq_ready, 1)

            def evac_f(k):
                act.wait_ge(acc_full, tile[0] + 1)
                square(k, tile_bank(tile[0])[:, 0:T])
                evac(fT[:, k, :])

            def root():
                act.activation(act_table[:, :], half_pi[:, :], ACT.Sqrt)
                act.wait_ge(ms_ready, norms[0] + 1)
                act.activation(rstd[:, :], ms_bank[:, 0:T], ACT.Sqrt, bias=eps[:, :]).then_inc(root_ready, 1)
                norms[0] += 1

            def squares_of_x(n):
                for k in range(KT):
                    act.wait_ge(x_ready, KT * n + k + 1)
                    square(k, xT[:, k, :])

            def token_parts(ks):
                act.activation(h_parts[0][:, ks, :], hT[:, ks, :], ACT.Copy).then_inc(part_hi, 1)

            def affine(l, part, n, parts=True):
                A, B = coefA[2 * l + part], modT[l][:, 24 * part:24 * part + 8, :]
                for k in range(KT + 1):
                    if k < KT:
                        act.wait_ge(scaled_ready, KT * n + k + 1)
                        act.activation(hT[:, k, 0:TP], sq[:, k, 0:TP], ACT.Identity, scale=A[:, k, 0:1],
                                       bias=B[:, k, 0:1]).then_inc(h_ready, 1)
                    if k and parts:
                        act.wait_ge(h_ready, KT * n + k)
                        token_parts(slice(k - 1, k))

            def R(name):
                return s5_rows[:, ROWS.index(name), :]

            def last_states(j):
                act.wait_ge(xre_ready, j + 1)
                act.wait_ge(xim_ready, j + 1)
                act.activation(s_last[:, :, j], xri[j % 3][:, :, TP - 1], ACT.Copy)
                act.activation(s_out[:, :, :, j], xri[j % 3][:, :, TP:T], ACT.Copy).then_inc(last_copied, 1)

            act.wait_ge(start_t, 1)
            act.activation(csT[:, :, :].rearrange("p k c -> p (k c)"), bank[4][:, 0:KT * NC], ACT.Silu)\
                .then_inc(cs_ready, 1)
            for i in range(12):
                ada(i)
                if i == 6:
                    for k in range(KT):
                        act.wait_ge(start_copied, k + 2)
                        square(k, xT[:, k, :])
                if i == 10:
                    root()
                    split_dense_hi(act, 0)
                    split_dense_hi(act, 1)
            split_dense_hi(act, 2)
            affine(0, 0, 0)
            evac(pT[0:LOWRANK, GLR, :], rows=LOWRANK)
            for t in range(N_IN0):
                if t < K_:
                    evac(pT[:, t, :], scale=0.125)
                elif OG <= t < CH_H:
                    evac(pT[:, t, :], ACT.Silu)
                else:
                    evac(pT[:, t, :])
            for a in range(2):
                act.wait_ge(z_full, a + 1)
                act.activation(e_pos[:, a, :], bank[6 + a][:, 0:T], ACT.Identity, bias=vecB[:, 64 + a:65 + a])\
                    .then_inc(z_copied, 1)
            act.wait_ge(z_copied, 2)
            step(act.activation(e_neg, e_pos, ACT.Abs))
            step(act.activation(e_neg, e_neg, ACT.Exp, scale=-1.0))
            act.activation(e_neg, e_neg, ACT.Ln, bias=1.0).then_inc(gate_parts, 1)
            act.wait_ge(b_ready, 1)
            act.activation(e_pos, b_cum, ACT.Exp, scale=1.0 / 16)
            act.activation(e_neg, b_cum, ACT.Exp, scale=-1.0 / 16)
            act.wait_ge(b_ready, 2)
            act.activation(e_dec, e_dec, ACT.Exp, scale=1.0 / 16).then_inc(exps_ready, 1)
            for i in range(4):
                ada(12 + i)
            for n in range(12, 15):
                split_dense_hi(act, n)
            act.wait_ge(mixed_y, 1)
            token_parts(slice(4, 8))

            def head_root(h):
                act.wait_ge(oms_ready, h + 1)
                src = bank[5][:, 128:128 + T] if h == 3 else bank[(6, 7, 4)[h]][:, 0:T]
                act.activation(head_rstd[:, h, :], src, ACT.Sqrt, scale=1.0 / P, bias=eps[:, :]).then_inc(oroot_ready, 1)

            for h in range(H):
                act.wait_ge(acc_full, TILES["gla"] + h + 1)
                act.activation(sq_flat[:, T * h:T * h + T], tile_bank(tile[0])[:, 0:T], ACT.Square).then_inc(osq_ready, 1)
                evac(oT[:, h, :])
                if h:
                    head_root(h - 1)
            head_root(H - 1)
            for h in range(H):
                act.wait_ge(mixed_o, h + 1)
                token_parts(slice(h, h + 1))
            act.wait_ge(kv_added, 2 * H)
            act.wait_ge(out_done, 16 * 12)
            for t in range(KT):
                evac_f(t)
            root()
            split_dense_hi(act, 18)
            squares_of_x(0)
            root()
            affine(0, 1, 1)
            for group in GROUPS:
                for t in group:
                    if t >= 4:
                        act.wait_ge(hid_ready, t - 3)
                    evac(silu_g[:, t % 4, :], ACT.Silu)
                for t in group:
                    evac(up_c[:, t % 4, :])
                if 8 in group:
                    act.wait_ge(s5_loaded, 16 * 7)
                    act.activation(log_dt[:, 2:4], log_dt[:, 0:2], ACT.Exp).then_inc(exp_ready, 1)
                    act.wait_ge(s5_rows_ready, 1)
                    act.activation(R("mag"), R("dr"), ACT.Exp).then_inc(exp_ready, 1)
                    act.wait_ge(s5_rows_ready, 2)
                    act.activation(R("sin"), R("turns"), ACT.Sin, scale=TWO_PI)
                    step(act.activation(R("cos"), R("turns"), ACT.Abs))
                    act.activation(R("cos"), R("cos"), ACT.Sin, scale=-TWO_PI, bias=half_pi[0:S5T, :])\
                        .then_inc(trig_ready, 1)
            for t in range(KT):
                evac_f(t)
                if t == 5:
                    split_dense_hi(act, 38)
                    split_dense_hi(act, 39)
            root()
            squares_of_x(1)
            root()
            affine(1, 0, 2)
            split_dense_hi(act, 40)
            for t in range(KT):
                evac(uT[:, t, :])

            def copy(k, n):
                act.wait_ge(tr_full, 3 * k + n + 1)
                if n == 0:
                    out = bbt[:, k % 2, :, :].rearrange("q a b -> q (a b)")
                else:
                    out = ct[:, k % 2, 4 * n - 4:4 * n, :].rearrange("q a b -> q (a b)")
                act.activation(out, bank[7][:, 0:out.shape[1]], ACT.Copy).then_inc(tr_copied, 1)

            def whole(j):
                if j >= 2:
                    act.wait_ge(table_ready, j - 1)
                step(act.activation(turn[j % 2], steps_t, ACT.Identity, scale=cols[:, 5, j:j + 1], bias=magic[:, :]))
                act.activation(turn[j % 2], turn[j % 2], ACT.Identity, bias=minus_magic[:, :])\
                    .then_inc(whole_turns, 1)

            def table(j):
                act.wait_ge(turn_ready, j + 1)
                if j >= 3:
                    act.wait_ge(xre_ready, j - 2)
                    act.wait_ge(xim_ready, j - 2)
                tb = tables[j % 3]
                step(act.activation(tb[:, 0, :], turn[j % 2], ACT.Abs))
                act.activation(tb[:, 0, :], tb[:, 0, :], ACT.Sin, scale=-TWO_PI, bias=half_pi[:, :])
                act.activation(tb[:, 1, :], turn[j % 2], ACT.Sin, scale=TWO_PI).then_inc(table_ready, 1)

            act.wait_ge(s5_cols, 1)
            act.wait_ge(consts_ready, 5)
            act.wait_ge(s5_cols, 2)
            for n in range(3):
                copy(0, n)
            whole(0)
            whole(1)
            table(0)
            whole(2)
            for j in range(S5T):
                if j + 1 < S5T:
                    table(j + 1)
                if j + 3 < S5T:
                    whole(j + 3)
                if j >= 2:
                    last_states(j - 2)
                if j >= 2 and j % 4 != 1 and (j + 2) // 4 < KT:
                    copy((j + 2) // 4, (j + 2) % 4)
                if j % 4 == 3:
                    ada(16 + j // 4)
                if j == S5T - 2:
                    split_dense_hi(act, 42)
                    split_dense_hi(act, 43)
            last_states(S5T - 2)
            last_states(S5T - 1)
            for i in range(2):
                act.wait_ge(s5_t, i + 1)
                if i == 0:
                    act.activation(out_rows.rearrange("q a b -> q (a b)"), bank[1][0:S5T, 0:256], ACT.Copy)\
                        .then_inc(s5_out, 1)
                else:
                    act.activation(s_out_rows.rearrange("q a b -> q (a b)"), bank[2][:, :], ACT.Copy)\
                        .then_inc(s5_out, 1)
            for k in range(KT + 1):
                if k < KT:
                    act.wait_ge(y_used, k + 1)
                    act.activation(hT[:, k, :], hT[:, k, :], ACT.Gelu_apprx_tanh).then_inc(gelu_ready, 1)
                if k:
                    act.wait_ge(gelu_ready, k)
                    token_parts(slice(k - 1, k))
            split_dense_hi(act, 44)
            for group in (range(0, 4), range(4, 8)):
                for t in group:
                    evac(fT[:, t, :])
                for t in (*group, None):
                    if t is not None:
                        evac(zg_sig[:, t % 4, :], ACT.Sigmoid)
                    if t != group[0]:
                        last = group[-1] if t is None else t - 1
                        act.wait_ge(glu_ready, last + 1)
                        square(last, fT[:, last, :])
            root()
            squares_of_x(2)
            root()
            affine(1, 1, 3, parts=False)
            act.wait_ge(logits_full, 1)
            act.activation(logits_t, bank[7][0:EXPERTS, 0:T], ACT.Copy).then_inc(logits_copied, 1)
            for n in range(6):
                rows = P if n < 4 else NS
                act.wait_ge(xt_full, n + 1)
                if n >= 4:
                    act.wait_ge(moe_consts, 2)
                act.activation(x_tok[0:rows, n // 2, W * (n % 2):W * (n % 2) + W], bank[n % 4][0:rows, :], ACT.Copy)\
                    .then_inc(xt_copied, 1)
            act.wait_ge(lg_ready, 1)
            act.activation(ex, ex, ACT.Exp).then_inc(lg_ready, 1)

            def xg_hi(j):
                for half in range(2):
                    act.wait_ge(gath_full, 2 * j + half + 1)
                    act.activation(xg[0][:, 4 * half:4 * half + 4, :].rearrange("q a b -> q (a b)"),
                                   bank[7 if half == 0 else 2][:, :], ACT.Copy).then_inc(xg_hi_ready, 1)

            for h in range(3):
                split_hi(act, 0, h)
            xg_hi(0)

            def job(j):
                act.activation(act_table[:, :], half_pi[:, :], ACT.Silu)

                def ht_hi(c):
                    act.wait_ge(ht_full, NCHK * j + c + 1)
                    act.activation(h_t[c % 2][0], bank[6][:, :], ACT.Copy).then_inc(ht_hi_ready, 1)

                for m, (kind, c) in enumerate(kinds):
                    for h in (2 * m, 2 * m + 1):
                        half_free(act, j, h)
                        if h == NH - 1:
                            act.activation(y_job[:, 0, :], bank[4][:, :], ACT.Copy).then_inc(y_ready, 1)
                        split_hi(act, *half_after(j, h))
                    if kind == "gate":
                        if c >= 2:
                            act.wait_ge(h_act_ready, NCHK * j + c - 1)
                        act.activation(g_act[:, c % 2, :], bank[2 * (c % 2)][:, :], ACT.Silu).then_inc(g_ready, 1)
                        if c:
                            ht_hi(c - 1)
                    if (kind, c) == ("down", NCHK - 2):
                        ht_hi(NCHK - 1)
                        xg_hi(j + 1)

            njobs = for_jobs(act, job)
            for k in range(KT):
                act.wait_ge(back_added, KT * njobs + k + 1)
                square(k, fT[:, k, :])
            root()
            for i in (0, 1, 2, 4):
                n = OUT_ORDER[i]
                rows = P if n < 4 else NS
                act.wait_ge(outs_t, i + 1)
                act.activation(x_tok[0:rows, n // 2, W * (n % 2):W * (n % 2) + W], bank[i % 4][0:rows, :], ACT.Copy)\
                    .then_inc(outs_copied_act, 1)

        @block.vector
        def _(dve):
            count = [0]
            norms = [0]

            def step(ins):
                count[0] += 1
                ins.then_inc(v_step, 1)
                dve.wait_ge(v_step, count[0])

            def mod_rows(i):
                l, j = divmod(i, 12)
                dve.wait_ge(row_t, i + 1)
                rows = row_bank[:, 36 * (i % 2):36 * (i % 2) + 36].rearrange("p (t c) -> p t c", c=NC)
                b = vecA[:, 48 * l + 4 * j:48 * l + 4 * j + 4]
                dve.tensor_tensor(modT[l][:, 4 * j:4 * j + 4, :], rows, bview(b, [P, 4, NC], 2), ALU.add)\
                    .then_inc(mod_ready, 1)

            def coefs(l, part, which):
                g = [bview(vecB[:, (4 * l + 2 * part + j) * KT:(4 * l + 2 * part + j + 1) * KT], [P, KT, NC], 2)
                     for j in range(2)]
                at = 24 * part
                if which == "pre":
                    step(dve.scalar_tensor_tensor(out=coefA[2 * l + part][:, :, :], in0=modT[l][:, at + 8:at + 16, :],
                                                  scalar=1.0, in1=g[0], op0=ALU.add, op1=ALU.mult))
                else:
                    step(dve.tensor_tensor(coefG[2 * l + part][:, :, :], modT[l][:, at + 16:at + 24, :], g[1],
                                           ALU.mult))

            def inverse():
                norms[0] += 1
                dve.wait_ge(root_ready, norms[0])
                step(dve.reciprocal(rstd[:, :], rstd[:, :]))

            wide_rstd = bview(rstd[:, TP:T], [P, KT, NS], 1)

            def token_parts(n, ks):
                dve.wait_ge(part_hi, n + 1)
                dve.tensor_tensor(h_parts[1][:, ks, :], hT[:, ks, :], h_parts[0][:, ks, :].bitcast(F32), ALU.subtract)\
                    .then_inc(part_lo, 1)

            def pre(l, part, product=None, inverted=False):
                if not inverted:
                    inverse()
                A, B = coefA[2 * l + part], modT[l][:, 24 * part:24 * part + 8, :]
                step(dve.tensor_tensor(sq[:, :, TP:T], xT[:, :, TP:T], wide_rstd, ALU.mult))
                step(dve.tensor_tensor(sq[:, :, TP:T], sq[:, :, TP:T], A[:, :, 1:NC], ALU.mult))
                dve.tensor_tensor(hT[:, :, TP:T], sq[:, :, TP:T], B[:, :, 1:NC], ALU.add)
                for k in range(KT):
                    dve.tensor_tensor(sq[:, k, 0:TP], xT[:, k, 0:TP], rstd[:, 0:TP], ALU.mult).then_inc(scaled_ready, 1)
                if product:
                    for k in range(KT):
                        token_parts(PARTS_OF[product] + k, slice(k, k + 1))

            def post(l, part):
                inverse()
                G = coefG[2 * l + part]
                step(dve.tensor_tensor(sq[:, :, TP:T], fT[:, :, TP:T], wide_rstd, ALU.mult))
                step(dve.tensor_tensor(sq[:, :, TP:T], sq[:, :, TP:T], G[:, :, 1:NC], ALU.mult))
                dve.tensor_tensor(xT[:, :, TP:T], xT[:, :, TP:T], sq[:, :, TP:T], ALU.add)

                def scaled(k):
                    count[0] += 1
                    dve.tensor_tensor(sq[:, k, 0:TP], fT[:, k, 0:TP], rstd[:, 0:TP], ALU.mult).then_inc(v_step, 1)
                    return count[0]

                done = scaled(0)
                for k in range(KT):
                    after = scaled(k + 1) if k + 1 < KT else None
                    dve.wait_ge(v_step, done)
                    dve.scalar_tensor_tensor(out=xT[:, k, 0:TP], in0=sq[:, k, 0:TP], scalar=G[:, k, 0:1],
                                             in1=xT[:, k, 0:TP], op0=ALU.mult, op1=ALU.add).then_inc(x_ready, 1)
                    done = after

            dve.wait_ge(start_t, 2)
            dve.tensor_copy(vecA[:, :], bank[7][:, 96:192])
            dve.tensor_copy(vecB[:, :], bank[7][:, 192:279])
            dve.tensor_copy(convT[:, :, :].rearrange("p k r -> p (k r)"), bank[7][:, 288:352]).then_inc(start_copied, 1)
            dve.wait_ge(start_copied, 1)
            for i in range(4):
                mod_rows(i)
            for k in range(KT):
                dve.wait_ge(start_t, 3 + k)
                ins = dve.tensor_copy(xT[:, k, :], bank[(6, 4)[k % 2]][:, 0:T])
                ins.then_inc(start_copied, 1)
            for i in range(4, 10):
                mod_rows(i)
            split_dense_lo(dve, 0)
            split_dense_lo(dve, 1)
            mod_rows(10)
            dve.wait_ge(mod_ready, 11)
            coefs(0, 0, "pre")
            inverse()
            pre(0, 0, "in0", inverted=True)
            mod_rows(11)
            dve.wait_ge(mod_ready, 12)
            coefs(0, 0, "post")
            coefs(0, 1, "pre")
            coefs(0, 1, "post")
            for n in range(2, 12):
                split_dense_lo(dve, n)
            dve.wait_ge(gate_parts, 1)
            step(dve.scalar_tensor_tensor(out=z_gate, in0=e_pos, scalar=0.0, in1=e_neg, op0=ALU.min, op1=ALU.subtract))
            dve.wait_ge(consts_ready, 3)
            for a in range(2):
                dve.tensor_tensor_scan(b_cum[:, a, 0:TP], scan_mask, z_gate[:, a, 0:TP], 0.0, ALU.mult, ALU.add)
            dve.tensor_copy(b_cum[:, :, TP:T], z_gate[:, :, TP:T]).then_inc(b_ready, 1)
            dve.wait_ge(b_ready, 1)
            for a in range(2):
                b4 = b_cum[:, a, 0:TP].rearrange("p (c t) -> p c t", t=CH)
                ins = dve.tensor_tensor(e_dec[:, a, :].rearrange("p (c t) -> p c t", t=CH),
                                        b4[:, :, CH - 1:CH].broadcast_to([P, NCH, CH]), b4, ALU.subtract)
            ins.then_inc(b_ready, 1)
            dve.wait_ge(exps_ready, 1)
            dve.tensor_tensor(e_dec, pT[:, K_:K_ + 2, 0:TP], e_dec, ALU.mult).then_inc(kd_ready, 1)
            dve.tensor_tensor(pT[:, Q:Q + 2, 0:TP], pT[:, Q:Q + 2, 0:TP], e_pos[:, :, 0:TP], ALU.mult)
            dve.tensor_tensor(pT[:, K_:K_ + 2, 0:TP], pT[:, K_:K_ + 2, 0:TP], e_neg[:, :, 0:TP], ALU.mult)\
                .then_inc(qk_ready, 1)
            dve.wait_ge(tok_full, 3)
            dve.tensor_copy(v_tok[:, 0, :], bank[6][:, :]).then_inc(tok_copied, 1)
            dve.tensor_copy(v_tok[:, 1, :], bank[7][:, :]).then_inc(tok_copied, 1)
            dve.tensor_copy(vs_tok, bank[4][0:NS, :]).then_inc(tok_copied, 1)
            mod_rows(12)
            dve.wait_ge(tok_full, 4)
            dve.tensor_copy(ks_tok, bank[6][0:NS, 0:256]).then_inc(tok_copied, 1)
            dve.wait_ge(qk_ready, 1)
            dve.wait_ge(tok_full, 5)
            dve.tensor_copy(kd_tok.rearrange("p b n -> p (b n)"), bank[7][:, :]).then_inc(tok_copied, 1)
            for b in range(2):
                dve.wait_ge(att_full, b + 1)
                dve.tensor_tensor(attn[:, b, :].rearrange("p (h i) -> p h i", i=P),
                                  bank[6 + b][:, :].rearrange("p (h i) -> p h i", i=P),
                                  bview(attn_mask, [P, H, P], 1), ALU.mult).then_inc(att_masked, 1)
            for c in range(NCH):
                src = bank[(4, 6, 7, 4)[c]]
                dve.wait_ge(ds_full, c + 1)
                if c:
                    dve.wait_ge(s_ready, c)
                for h in range(H):
                    rows, a = slice(64 * (h % 2), 64 * (h % 2) + 64), h // 2
                    new, add = s_chunk[rows, c, a, :], src[rows, P * h:P * h + P]
                    if c == 0:
                        ins = dve.tensor_copy(new, add)
                    else:
                        last = CH * c + CH - 1
                        ins = dve.scalar_tensor_tensor(out=new, in0=s_chunk[rows, c - 1, a, :],
                                                       scalar=e_pos[rows, a, last:last + 1], in1=add,
                                                       op0=ALU.mult, op1=ALU.add)
                ins.then_inc(s_ready, 1)
            dve.wait_ge(s0_loaded, 16)
            alpha = e_pos[:, :, TP:T].rearrange("p a s -> p s a")
            step(dve.tensor_tensor(s0, s0, bview(alpha, [P, NS, 2, P], 3), ALU.mult))

            def spread_values(h):
                if h >= 2:
                    dve.wait_ge(kv_full, 2 * h - 2)
                dve.wait_ge(tok_copied, 3)
                dve.tensor_tensor(spread_v[:, h % 2, :, :], bview(vs_tok[:, P * h:P * h + P], [NS, NS, P], 1),
                                  bview(ident[0:NS, 0:NS], [NS, NS, P], 2), ALU.mult).then_inc(spread_ready, 1)

            def add_kv(n):
                h, u = divmod(n, 2)
                dve.wait_ge(kv_full, n + 1)
                rows = slice(64 * (h % 2), 64 * (h % 2) + 64)
                part = s0[rows, 4 * u:4 * u + 4, h // 2, :]
                dve.tensor_tensor(part, part, bank[(6, 7, 4)[n % 3]][rows, :].rearrange("p (s v) -> p s v", v=P),
                                  ALU.add).then_inc(kv_added, 1)

            spread_values(0)
            spread_values(1)
            mod_rows(13)
            for n in range(2):
                add_kv(n)
            spread_values(2)
            add_kv(2)
            mod_rows(14)
            add_kv(3)
            spread_values(3)
            for n in range(4, 6):
                add_kv(n)
            mod_rows(15)
            for n in range(6, 2 * H):
                add_kv(n)
            for n in range(12, 15):
                split_dense_lo(dve, n)
            token_parts(PARTS_OF["out0"], slice(4, 8))
            for h in range(H):
                dve.wait_ge(oroot_ready, h + 1)
                step(dve.reciprocal(head_rstd[:, h, :], head_rstd[:, h, :]))
                step(dve.tensor_tensor(oT[:, h, :], oT[:, h, :], head_rstd[:, h, :], ALU.mult))
                dve.scalar_tensor_tensor(out=hT[:, h, :], in0=oT[:, h, :], scalar=vecB[:, 78:79], in1=pT[:, OG + h, :],
                                         op0=ALU.mult, op1=ALU.mult).then_inc(mixed_o, 1)
                if h:
                    token_parts(PARTS_OF["out0"] + h, slice(h - 1, h))
            token_parts(PARTS_OF["out0"] + H, slice(H - 1, H))
            for n in range(15, 18):
                split_dense_lo(dve, n)
            post(0, 0)
            pre(0, 1, "ffn")
            split_dense_lo(dve, 18)

            def R(name):
                return s5_rows[:, ROWS.index(name), :]

            def prepare(part):
                V = dve
                if part == 0:
                    V.wait_ge(exp_ready, 1)
                    dt = bview(log_dt[:, 2:4], [S5T, 2, 64], 2)
                    wide = lambda name: R(name).rearrange("q (g p) -> q g p", p=64)
                    V.tensor_tensor(wide("dr"), wide("are"), dt, ALU.mult).then_inc(s5_rows_ready, 1)
                    step(V.tensor_tensor(wide("th"), wide("aim"), dt, ALU.mult))
                    step(V.tensor_scalar(R("th"), R("th"), INV_TWO_PI, None, ALU.mult))
                    step(V.tensor_scalar(R("tmp"), R("th"), MAGIC, MAGIC, ALU.add, ALU.subtract))
                    step(V.tensor_tensor(R("turns"), R("th"), R("tmp"), ALU.subtract))
                    step(V.tensor_scalar(R("hi"), R("turns"), 3072.0, 3072.0, ALU.add, ALU.subtract))
                    V.tensor_tensor(R("lo"), R("turns"), R("hi"), ALU.subtract).then_inc(s5_rows_ready, 1)
                    V.tensor_tensor(R("den"), R("are"), R("are"), ALU.mult)
                    step(V.tensor_tensor(R("tmp"), R("aim"), R("aim"), ALU.mult))
                    step(V.tensor_tensor(R("den"), R("den"), R("tmp"), ALU.add))
                    step(V.reciprocal(R("den"), R("den")))
                else:
                    V.wait_ge(trig_ready, 1)
                    V.wait_ge(exp_ready, 2)
                    V.tensor_tensor(R("abre"), R("mag"), R("cos"), ALU.mult)
                    step(V.tensor_tensor(R("abim"), R("mag"), R("sin"), ALU.mult))
                    step(V.tensor_scalar(R("cos"), R("abre"), -1.0, None, ALU.add))
                    V.tensor_tensor(R("fre"), R("cos"), R("are"), ALU.mult)
                    step(V.tensor_tensor(R("tmp"), R("abim"), R("aim"), ALU.mult))
                    step(V.tensor_tensor(R("fre"), R("fre"), R("tmp"), ALU.add))
                    V.tensor_tensor(R("fim"), R("abim"), R("are"), ALU.mult)
                    step(V.tensor_tensor(R("tmp"), R("cos"), R("aim"), ALU.mult))
                    step(V.tensor_tensor(R("fim"), R("fim"), R("tmp"), ALU.subtract))
                    V.tensor_tensor(R("fre"), R("fre"), R("den"), ALU.mult)
                    V.tensor_tensor(R("fim"), R("fim"), R("den"), ALU.mult).then_inc(s5_rows_ready, 1)

            for t in range(FT):
                group = GROUPS[t // 4]
                n = 19 + 4 * (t // 4)
                lows = {0: (n, n + 1, n + 2), 2: (n + 3,)}.get(t % 4, ())
                for n in lows:
                    if n < 38:
                        split_dense_lo(dve, n)
                dve.wait_ge(acc_free, TILES["ffn"] + group[0] + len(group) + t + 1)
                dve.tensor_tensor(hid[:, t, :], silu_g[:, t % 4, :], up_c[:, t % 4, :], ALU.mult).then_inc(hid_ready, 1)
                if t == 8:
                    prepare(0)
                if t == 12:
                    prepare(1)
            dve.wait_ge(s5_cols_t, 1)
            dve.tensor_copy(cols.rearrange("q a b -> q (a b)"), bank[7][:, 0:256]).then_inc(s5_cols, 1)
            dve.wait_ge(s5_cols, 1)
            f = [bview(cols[:, 3 + i, :], [P, S5T, 16], 2) for i in range(2)]
            raw = [b_raw[:, i, :].rearrange("q (t i) -> q t i", i=16) for i in range(2)]
            new = [bb[:, i, :].rearrange("q (t i) -> q t i", i=16) for i in range(2)]
            dve.tensor_tensor(new[0], f[0], raw[0], ALU.mult)
            step(dve.tensor_tensor(new[1], f[0], raw[1], ALU.mult))
            dve.tensor_tensor(raw[0], f[1], raw[0], ALU.mult)
            step(dve.tensor_tensor(raw[1], f[1], raw[1], ALU.mult))
            dve.tensor_tensor(new[0], new[0], raw[1], ALU.subtract)
            dve.tensor_tensor(new[1], new[1], raw[0], ALU.add).then_inc(bb_ready, 1)
            dve.wait_ge(bb_ready, 1)
            dve.wait_ge(s5_cols_t, 2)
            ab = [bview(cols[:, 1 + i, :], [P, NS, S5T], 1) for i in range(2)]
            st = [bank[4][:, 256 * i:256 * i + 256].rearrange("q (s t) -> q s t", t=S5T) for i in range(2)]
            dve.tensor_tensor(s_in[:, 0, :, :], ab[0], st[0], ALU.mult)
            dve.tensor_tensor(s_in[:, 1, :, :], ab[0], st[1], ALU.mult)
            dve.tensor_tensor(s_out[:, 0, :, :], ab[1], st[1], ALU.mult)
            step(dve.tensor_tensor(s_out[:, 1, :, :], ab[1], st[0], ALU.mult))
            dve.tensor_tensor(s_in[:, 0, :, :], s_in[:, 0, :, :], s_out[:, 0, :, :], ALU.subtract)
            dve.tensor_tensor(s_in[:, 1, :, :], s_in[:, 1, :, :], s_out[:, 1, :, :], ALU.add).then_inc(s5_cols, 1)
            split_dense_lo(dve, 38)
            post(0, 1)
            dve.wait_ge(mod_ready, 16)
            coefs(1, 0, "pre")
            pre(1, 0, "in1")
            for n in range(39, 42):
                split_dense_lo(dve, n)
            dve.wait_ge(s5_cols, 2)

            def rest(j):
                dve.wait_ge(whole_turns, j + 1)
                t = turn[j % 2]
                step(dve.scalar_tensor_tensor(out=t, in0=steps_t, scalar=cols[:, 6, j:j + 1], in1=t,
                                              op0=ALU.mult, op1=ALU.subtract))
                dve.scalar_tensor_tensor(out=t, in0=steps_t, scalar=cols[:, 7, j:j + 1], in1=t,
                                         op0=ALU.mult, op1=ALU.add).then_inc(turn_ready, 1)

            def turn_back(j):
                wk, tb = work[j % 3], tables[j % 3]
                re, im = bank[1 + 2 * (j % 2)], bank[2 + 2 * (j % 2)]
                dve.wait_ge(table_ready, j + 1)
                dve.wait_ge(bu_full, j + 1)
                if j >= 3:
                    dve.wait_ge(y_full, j - 2)
                    dve.wait_ge(last_copied, j - 2)
                    dve.wait_ge(xre_ready, j - 2)
                dve.tensor_tensor(wk[:, 0, :], tb[:, 0, :], re[:, 0:TP], ALU.mult)
                dve.tensor_tensor(wk[:, 1, :], tb[:, 1, :], im[:, 0:TP], ALU.mult)
                dve.tensor_tensor(wk[:, 2, :], tb[:, 0, :], im[:, 0:TP], ALU.mult)
                dve.tensor_tensor(wk[:, 3, :], tb[:, 1, :], re[:, 0:TP], ALU.mult)
                dve.tensor_tensor(xri[j % 3][:, 0, TP:T], s_in[:, 0, :, j], re[:, TP:T], ALU.add)
                dve.tensor_tensor(xri[j % 3][:, 1, TP:T], s_in[:, 1, :, j], im[:, TP:T], ALU.add).then_inc(bu_used, 1)

            def scans(j):
                wk = work[j % 3]
                dve.wait_ge(w_ready, j + 1)
                for i in (0, 2):
                    dve.tensor_tensor_scan(wk[:, i, :], cols[:, 0, j:j + 1].broadcast_to([P, TP]), wk[:, i, :], 0.0,
                                           ALU.mult, ALU.add).then_inc(z_ready, 1)

            def rotate_im(j):
                wk, tb, x = work[j % 3], tables[j % 3], xri[j % 3]
                dve.wait_ge(z_ready, 2 * j + 2)
                dve.tensor_tensor(x[:, 1, 0:TP], tb[:, 1, :], wk[:, 0, :], ALU.mult)
                step(dve.tensor_tensor(wk[:, 3, :], tb[:, 0, :], wk[:, 2, :], ALU.mult))
                dve.tensor_tensor(x[:, 1, 0:TP], x[:, 1, 0:TP], wk[:, 3, :], ALU.add).then_inc(xim_ready, 1)

            def s5_y(k):
                dve.wait_ge(y_full, 4 * k + 4)
                dve.scalar_tensor_tensor(out=hT[:, k, :], in0=uT[:, k, :], scalar=vecB[:, 79 + k:80 + k],
                                         in1=bank[6][:, 0:T], op0=ALU.mult, op1=ALU.add).then_inc(y_used, 1)

            rest(0)
            rest(1)
            for j in range(S5T + 1):
                if j < S5T:
                    turn_back(j)
                if j >= 6 and j % 4 == 2:
                    s5_y(j // 4 - 1)
                if j:
                    scans(j - 1)
                if j + 2 < S5T:
                    rest(j + 2)
                if j:
                    rotate_im(j - 1)
                if j % 4 == 1 and j >= 9:
                    mod_rows(14 + j // 4)
            for n in (42, 43):
                split_dense_lo(dve, n)
            s5_y(KT - 1)
            mod_rows(22)
            mod_rows(23)
            for k in range(KT):
                token_parts(PARTS_OF["glu"] + k, slice(k, k + 1))
            split_dense_lo(dve, 44)
            dve.wait_ge(mod_ready, 24)
            coefs(1, 0, "post")
            coefs(1, 1, "pre")
            coefs(1, 1, "post")
            for t in range(KT):
                for n in {0: (45, 46, 47), 2: (48,), 4: (49,)}.get(t, ()):
                    split_dense_lo(dve, n)
                dve.wait_ge(acc_free, TILES["glu"] + 4 * (t // 4) + 4 + t + 1)
                dve.tensor_tensor(fT[:, t, :], fT[:, t, :], zg_sig[:, t % 4, :], ALU.mult).then_inc(glu_ready, 1)
            post(1, 0)
            pre(1, 1)
            dve.wait_ge(moe_consts, 2)
            dve.wait_ge(lg_full, 1)
            dve.tensor_copy(lg[:, 0:2, :], bank[7][:, 0:16].rearrange("q (b e) -> q b e", e=EXPERTS))
            step(dve.tensor_copy(lg[0:NS, 2, :], bank[7][0:NS, 16:24]))
            by_e = lambda x: x.rearrange("q (b e) f -> q b e f", e=EXPERTS)
            mine, other = bview(lg, [P, 3, EXPERTS, EXPERTS], 3), bview(lg, [P, 3, EXPERTS, EXPERTS], 2)
            dve.tensor_reduce(m_tok, lg, AX.X, ALU.max)
            dve.tensor_tensor(by_e(cmp_a), other, mine, ALU.is_gt)
            step(dve.tensor_tensor(by_e(cmp_b), other, mine, ALU.is_equal))
            dve.tensor_tensor(ex, lg, bview(m_tok, [P, 3, EXPERTS], 2), ALU.subtract).then_inc(lg_ready, 1)
            step(dve.tensor_tensor(by_e(cmp_b), by_e(cmp_b), bview(earlier, [P, 3, EXPERTS, EXPERTS], 1), ALU.mult))
            step(dve.tensor_tensor(cmp_a, cmp_a, cmp_b, ALU.add))
            step(dve.tensor_reduce(slot_of.rearrange("q b e -> q (b e)"), cmp_a, AX.X, ALU.add))
            step(dve.tensor_scalar(sel, slot_of, 1.5, None, ALU.is_lt))
            dve.wait_ge(lg_ready, 2)
            step(dve.tensor_tensor(comb, ex, sel, ALU.mult))
            step(dve.tensor_tensor(sel, sel, bview(valid, [P, 3, EXPERTS], 2), ALU.mult))
            dve.tensor_reduce(d_tok, comb, AX.X, ALU.add).then_inc(sel_ready, 1)
            dve.wait_ge(sel_ready, 1)
            step(dve.reciprocal(d_tok, d_tok))
            step(dve.tensor_tensor(d_tok, d_tok, valid, ALU.mult))
            step(dve.tensor_tensor(comb, comb, bview(d_tok, [P, 3, EXPERTS], 2), ALU.mult))
            dve.tensor_copy(job_w[:, :, 0:EXPERTS], comb)
            dve.wait_ge(pos_full, 1)
            pos = bank[7][:, 0:24].rearrange("q (b e) -> q b e", e=EXPERTS)
            step(dve.scalar_tensor_tensor(out=slot_of, in0=pos, scalar=-NO_SLOT, in1=sel, op0=ALU.add, op1=ALU.mult))
            step(dve.tensor_scalar(slot_of, slot_of, NO_SLOT, None, ALU.add))
            step(dve.tensor_copy(job_slot[:, :, 0:EXPERTS], slot_of))

            def picks(j):
                for b in range(3):
                    ins = dve.tensor_scalar(pick[:, b, :], slots, job_slot[:, b, bass.ds(j, 1)], None, ALU.is_equal)
                ins.then_inc(pick_ready, 1)

            for i in range(2):
                ins = dve.tensor_scalar(over[:, :, i], bank[7][:, 24:32], float(P * (i + 1)), None, ALU.is_gt)
            step(ins)
            picks(0)
            dve.tensor_tensor_scan(over_pos, ones[:, 0:16], over.rearrange("q e b -> q (e b)"), 0.0, ALU.mult, ALU.add)\
                .then_inc(over_ready, 1)
            def xg_lo(j):
                for half in range(2):
                    dve.wait_ge(xg_hi_ready, 2 * j + half + 1)
                    hi, lo = (xg[i][:, 4 * half:4 * half + 4, :].rearrange("q a b -> q (a b)") for i in range(2))
                    dve.tensor_tensor(lo, bank[7 if half == 0 else 2][:, :], hi.bitcast(F32), ALU.subtract)\
                        .then_inc(xg_lo_ready, 1)

            for h in range(3):
                split_lo(dve, 0, h)
            xg_lo(0)

            def back(j, pair, second=6):
                for k in range(2 * pair, 2 * pair + 2):
                    dve.wait_ge(back_full, KT * j + k + 1)
                    dve.tensor_tensor(fT[:, k, :], fT[:, k, :], bank[second if k % 2 else 7][:, 0:T], ALU.add)\
                        .then_inc(back_added, 1)

            def job(j):
                def ht_lo(c):
                    dve.wait_ge(ht_hi_ready, NCHK * j + c + 1)
                    dve.tensor_tensor(h_t[c % 2][1], bank[6][:, :], h_t[c % 2][0].bitcast(F32), ALU.subtract)\
                        .then_inc(ht_lo_ready, 1)

                for m, (kind, c) in enumerate(kinds):
                    for h in (2 * m, 2 * m + 1):
                        half_free(dve, j, h)
                        if h == NH - 1:
                            dve.tensor_copy(y_job[:, 1, :], bank[5][:, :]).then_inc(y_ready, 1)
                        if c == 0 and kind != "down":
                            back(j, h)
                        split_lo(dve, *half_after(j, h))
                    if kind == "gate" and c:
                        ht_lo(c - 1)
                    if kind == "up":
                        dve.wait_ge(g_ready, NCHK * j + c + 1)
                        if c >= 2:
                            dve.wait_ge(ht_full, NCHK * j + c - 1)
                        dve.tensor_tensor(h_act[:, c % 2, :], g_act[:, c % 2, :], bank[2 * (c % 2) + 1][:, :],
                                          ALU.mult).then_inc(h_act_ready, 1)
                    if (kind, c) == ("up", 1):
                        for b in range(3):
                            ins = dve.tensor_scalar(pick_w[:, b, :], slots, job_slot[:, b, bass.ds(j, 1)],
                                                    job_w[:, b, bass.ds(j, 1)], ALU.is_equal, ALU.mult)
                        ins.then_inc(pickw_ready, 1)
                    if (kind, c) == ("down", 2):
                        dve.wait_ge(spread_full, j + 1)
                        dve.tensor_copy(spread, bank[7][:, 0:T]).then_inc(spread_copied, 1)
                    if (kind, c) == ("down", 3):
                        dve.wait_ge(jobs_ready, 2)
                        picks(j + 1)
                    if (kind, c) == ("down", NCHK - 2):
                        ht_lo(NCHK - 1)
                        xg_lo(j + 1)

            njobs = for_jobs(dve, job)
            for pair in range(KT // 2):
                back(njobs, pair, second=3)
            post(1, 1)
            for i in (3, 5):
                n = OUT_ORDER[i]
                rows = P if n < 4 else NS
                dve.wait_ge(outs_t, i + 1)
                dve.tensor_copy(x_tok[0:rows, n // 2, W * (n % 2):W * (n % 2) + W], bank[i % 4][0:rows, :])\
                    .then_inc(outs_copied_dve, 1)

        @block.tensor
        def _(pe):
            tile = [0]
            piece = [0]
            dense_half_no = [0]
            norms = [0]

            def mm(out, lhsT, rhs, start, stop):
                return pe.matmul(out, lhsT, rhs, start=start, stop=stop, skip_group_check=True)

            count = [0]

            def step(ins):
                count[0] += 1
                ins.then_inc(t_step, 1)
                pe.wait_ge(t_step, count[0])

            def next_tile():
                n = tile[0]
                if TILES["ada1b"] <= n <= TILES["glu"]:
                    pe.wait_ge(acc_free, n)
                elif n >= 4:
                    pe.wait_ge(acc_free, n - 3)
                tile[0] += 1
                return tile_bank(n)

            def next_piece():
                i = piece[0]
                pe.wait_ge(ring_loaded[i % RING], 16 * (i // RING + 1))
                piece[0] += 1
                return slot(i)

            def product(out, w, c, src, kts, first, last):
                for j, k in enumerate(kts):
                    ins = mm(out, w[:, j, c:c + P], src[:, k, :], first and j == 0, last and j == len(kts) - 1)
                return ins

            def ada_part(w, out, ks):
                for k in ks:
                    ins = mm(out[0:NC, :], csT[:, k, :], w[:, k, :], k == 0, k == KT - 1)
                if k == KT - 1:
                    ins.then_inc(acc_full, 1)

            def ada(i):
                ada_part(next_piece(), next_tile(), range(KT))

            def ada_rows(i):
                l_tile = (TILES["ada0"] + i) if i < 12 else (TILES["ada1a"] + i - 12 if i < 16 else TILES["ada1b"] + i - 16)
                pe.wait_ge(acc_free, l_tile + 1)
                if i:
                    pe.wait_ge(mod_ready, i)
                for q in range(4):
                    at = 36 * (i % 2) + NC * q
                    ins = pe.transpose(row_bank[:, at:at + NC], modrow[:, P * q:P * q + P], ident[0:NC, 0:NC])
                ins.then_inc(row_t, 1)

            def mean_square(ks=range(KT)):
                for k in ks:
                    pe.wait_ge(sq_ready, KT * norms[0] + k + 1)
                    ins = mm(ms_bank[:, 0:T], mean_d[:, :], sq[:, k, :], k == 0, k == KT - 1)
                if KT - 1 in ks:
                    ins.then_inc(ms_ready, 1)
                    norms[0] += 1

            def dense(tiles, product=None, squares=False):
                for t in range(tiles):
                    if t % 2 == 0:
                        n = dense_half_no[0]
                        dense_half_no[0] += 1
                        piece[0] = dense_halves[n][0] + 1
                        _, w = dense_half(n)
                        pe.wait_ge(lo_ready, n + 1)
                    out, c = next_tile()[:, 0:T], P * (t % 2)
                    for k in range(KT):
                        if t == 0 and product == "out0":
                            pe.wait_ge(part_lo, PARTS_OF[product] + min(k + 2, H + 1))
                        elif t == 0 and product:
                            pe.wait_ge(part_lo, PARTS_OF[product] + k + 1)
                        for a, b in ((0, 0), (1, 0), (0, 1)):
                            ins = mm(out, w[b][:, k, c:c + P], h_parts[a][:, k, :], k == a == b == 0,
                                     k == KT - 1 and b == 1)
                    ins.then_inc(acc_full, 1)
                    if squares and t:
                        mean_square([t - 1])

            pe.wait_ge(consts_ready, 2)
            pe.wait_ge(c_loaded, 32)
            for k in range(KT):
                ins = pe.transpose(bank[4][:, NC * k:NC * k + NC], crow[:, P * k:P * k + P], ident[0:NC, 0:NC])
            ins.then_inc(start_t, 1)
            pe.wait_ge(cs_ready, 1)
            ada(0)
            ada(1)
            pe.wait_ge(vec_loaded, 16 * 7)
            pe.transpose(bank[7][:, 96:192], rawA, ident[0:96, 0:96])
            pe.transpose(bank[7][:, 192:279], rawB, ident[0:87, 0:87])
            for k in range(4):
                ins = pe.transpose(bank[7][:, 288 + 16 * k:304 + 16 * k], conv_rows[:, P * k:P * k + P],
                                   ident[0:16, 0:16])
            ins.then_inc(start_t, 1)
            ada_rows(0)
            for i in range(2, 5):
                ada(i)
                ada_rows(i - 1)
            pe.wait_ge(x_loaded, 32)
            for k in range(KT):
                if k >= 2:
                    pe.wait_ge(start_copied, k)
                out = bank[(6, 4)[k % 2]]
                for b in range(2):
                    pe.transpose(out[:, P * b:P * b + P], xrow[:, b, P * k:P * k + P], ident[:, :])
                pe.transpose(out[:, TP:T], xrow[0:NS, 2, P * k:P * k + P], ident[0:NS, 0:NS]).then_inc(start_t, 1)
            for i in range(5, 12):
                ada(i)
                ada_rows(i - 1)
                if i == 9:
                    pe.wait_ge(start_copied, 1 + KT)
                    mean_square()
            ada_rows(11)
            pe.wait_ge(small_loaded, 48)
            out = next_tile()
            for k in range(KT):
                pe.wait_ge(h_ready, k + 1)
                ins = mm(out[0:LOWRANK, 0:T], glr_w[:, k, :], hT[:, k, :], k == 0, k == KT - 1)
            ins.then_inc(acc_full, 1)
            dense(N_IN0, "in0")
            for a in range(2):
                mm(bank[6 + a][:, 0:T], gate_up_w[:, P * a:P * a + P], pT[0:LOWRANK, GLR, :], True, True)\
                    .then_inc(z_full, 1)
            pe.wait_ge(z_copied, 2)
            for b in range(2):
                for h in range(H):
                    ins = pe.transpose(bank[6 + b][:, P * h:P * h + P], pT[:, V + h, P * b:P * b + P], ident[:, :])
                ins.then_inc(tok_full, 1)
            for h in range(H):
                ins = pe.transpose(bank[4][0:NS, P * h:P * h + P], pT[:, V + h, TP:T], ident[:, :])
            ins.then_inc(tok_full, 1)
            for i in range(2):
                ada(12 + i)
            ada_rows(12)
            pe.wait_ge(tok_copied, 1)
            for a in range(2):
                ins = pe.transpose(bank[6][0:NS, P * a:P * a + P], pT[:, K_ + a, TP:T], ident[:, :])
            ins.then_inc(tok_full, 1)
            pe.wait_ge(kd_ready, 1)
            pe.wait_ge(tok_copied, 2)
            for b in range(2):
                for a in range(2):
                    at = TP * b + P * a
                    ins = pe.transpose(bank[7][:, at:at + P], e_dec[:, a, P * b:P * b + P], ident[:, :])
            ins.then_inc(tok_full, 1)
            pe.wait_ge(qk_ready, 1)
            for b in range(2):
                pe.wait_ge(tok_copied, 4 + b)
                for h in (0, 2, 1, 3):
                    rows, a = slice(64 * (h % 2), 64 * (h % 2) + 64), h // 2
                    cols_ = slice(P * b, P * b + P)
                    ins = mm(bank[6 + b][:, P * h:P * h + P], pT[rows, K_ + a, cols_], pT[rows, Q + a, cols_], True, True)
                    if h == 2:
                        step(ins)
                ins.then_inc(att_full, 1)
            for c in range(NCH):
                b, rows = c // 2, slice(64 * (c % 2), 64 * (c % 2) + 64)
                if c in (1, 2):
                    pe.wait_ge(att_masked, c)
                if c == 3:
                    pe.wait_ge(s_ready, 1)
                for a in range(2):
                    ins = mm(bank[(4, 6, 7, 4)[c]][:, 256 * a:256 * a + 256], kd_tok[rows, b, P * a:P * a + P],
                             v_tok[rows, b, 256 * a:256 * a + 256], True, True)
                ins.then_inc(ds_full, 1)

            def kv(n):
                h, u = divmod(n, 2)
                if n < 3:
                    pe.wait_ge(s_ready, n + 2)
                else:
                    pe.wait_ge(kv_added, n - 2)
                pe.wait_ge(spread_ready, h + 1)
                mm(bank[(6, 7, 4)[n % 3]][:, :], ks_tok[:, P * (h // 2):P * (h // 2) + P],
                   spread_v[:, h % 2, 4 * u:4 * u + 4, :].rearrange("p s v -> p (s v)"), True, True).then_inc(kv_full, 1)

            ada(14)
            ada_rows(13)
            for n in range(3):
                kv(n)
            ada(15)
            ada_rows(14)
            for n in range(3, 6):
                kv(n)
            ada_rows(15)
            for n in range(6, 2 * H):
                kv(n)
            pe.wait_ge(kv_added, 2 * H)

            def head_mean_square(h):
                pe.wait_ge(osq_ready, h + 1)
                if h == 3:
                    pe.wait_ge(mod_ready, 16)
                out = bank[5][:, 128:128 + T] if h == 3 else bank[(6, 7, 4)[h]][:, 0:T]
                mm(out, ones[:, :], sq_flat[:, T * h:T * h + T], True, True).then_inc(oms_ready, 1)

            for h in range(H):
                out = next_tile()
                rows, a = slice(64 * (h % 2), 64 * (h % 2) + 64), h // 2
                for b in range(2):
                    mm(out[:, P * b:P * b + P], v_tok[:, b, P * h:P * h + P], attn[:, b, P * h:P * h + P], b == 0, False)
                for c in range(1, NCH):
                    mm(out[:, CH * c:CH * c + CH], s_chunk[rows, c - 1, a, :], pT[rows, Q + a, CH * c:CH * c + CH],
                       False, False)
                for s in range(NS):
                    ins = mm(out[:, TP + s:TP + s + 1], s0[rows, s, a, :], pT[rows, Q + a, TP + s:TP + s + 1],
                             False, s == NS - 1)
                ins.then_inc(acc_full, 1)
                if h:
                    head_mean_square(h - 1)
            head_mean_square(H - 1)
            dense(KT, "out0", squares=True)
            mean_square([KT - 1])
            mean_square()
            for group in GROUPS:
                for kind in ("gate", "up"):
                    dense(len(group), "ffn" if group[0] == 0 and kind == "gate" else None)
                if 16 in group:
                    pe.wait_ge(s5_rows_ready, 3)
                    for i, name in enumerate(("mag", "abre", "abim", "fre", "fim", "turns", "hi", "lo")):
                        ins = pe.transpose(bank[7][:, S5T * i:S5T * i + S5T], s5_rows[:, ROWS.index(name), :],
                                           ident[0:S5T, 0:S5T])
                    ins.then_inc(s5_cols_t, 1)
                    for i in range(2):
                        for h in range(2):
                            at = 256 * i + P * h
                            ins = pe.transpose(bank[4][:, at:at + P], s_rows[:, i, P * h:P * h + P], ident[:, :])
                    ins.then_inc(s5_cols_t, 1)
            for i in range(4):
                outs = [next_tile()[:, 0:T] for _ in range(2)]
                for half in range(2):
                    w = next_piece()
                    kts = range(half * FT // 2, (half + 1) * FT // 2)
                    if i == 0:
                        pe.wait_ge(hid_ready, kts[-1] + 1)
                    for j, out in enumerate(outs):
                        ins = product(out, w, P * j, hid, kts, half == 0, half == 1)
                        if half == 1:
                            ins.then_inc(acc_full, 1)
                if i:
                    mean_square([2 * i - 2, 2 * i - 1])
            mean_square([KT - 2, KT - 1])
            mean_square()
            dense(KT, "in1")

            def tr(k, n):
                pe.wait_ge(pads_ready, k + 1)
                if k or n:
                    pe.wait_ge(tr_copied, 3 * k + n)
                src = bb_pad.rearrange("q a b -> q (a b)") if n == 0 else c_pad[:, n - 1, :]
                for i in range(2 if n == 0 else 4):
                    ins = pe.transpose(bank[7][:, P * i:P * i + P], src[:, P * i:P * i + P], ident[:, :])
                ins.then_inc(tr_full, 1)

            def bu(j):
                k, r = divmod(j, 4)
                rows = slice(32 * r, 32 * r + 32)
                if r == 0:
                    pe.wait_ge(tr_copied, 3 * k + 1)
                if j >= 2:
                    pe.wait_ge(bu_used, j - 1)
                for i in range(2):
                    ins = mm(bank[1 + 2 * (j % 2) + i][:, 0:T], bbt[rows, k % 2, i, :], uT[rows, k, :], True, True)
                ins.then_inc(bu_full, 1)

            def cx(j):
                k, r = divmod(j, 4)
                if r == 0:
                    pe.wait_ge(tr_copied, 3 * k + 3)
                    if k:
                        pe.wait_ge(y_used, k)
                pe.wait_ge(xre_ready, j + 1)
                pe.wait_ge(xim_ready, j + 1)
                for i in range(2):
                    ins = mm(bank[6][:, 0:T], ct[:, k % 2, 4 * i + r, :], xri[j % 3][:, i, :], r == 0 and i == 0,
                             r == 3 and i == 1)
                ins.then_inc(y_full, 1)

            pe.wait_ge(acc_free, TILES["in1"] + KT)
            for n in range(3):
                tr(0, n)
            bu(0)
            for j in range(S5T + 2):
                if j + 1 < S5T:
                    bu(j + 1)
                if j >= 2:
                    cx(j - 2)
                if 2 <= j < S5T and j % 4 != 1 and (j + 2) // 4 < KT:
                    tr((j + 2) // 4, (j + 2) % 4)
                if j < S5T and j % 4:
                    if j % 4 == 1:
                        ada_w, ada_out = next_piece(), next_tile()
                    ada_part(ada_w, ada_out, range(3 * (j % 4) - 3, min(3 * (j % 4), KT)))
                    if j % 4 == 2 and j > 4:
                        ada_rows(15 + j // 4)
            ada_rows(23)
            pe.wait_ge(last_copied, S5T)
            pe.wait_ge(bu_used, S5T)
            for i in range(2):
                ins = pe.transpose(bank[1][0:S5T, P * i:P * i + P], s_last[:, i, :], ident[:, :])
            ins.then_inc(s5_t, 1)
            flat = s_out.rearrange("q i s t -> q i (s t)")
            for i in range(2):
                for h in range(2):
                    ins = pe.transpose(bank[2][:, 256 * i + P * h:256 * i + P * h + P], flat[:, i, P * h:P * h + P],
                                       ident[:, :])
            ins.then_inc(s5_t, 1)
            pe.wait_ge(s5_out, 2)
            dense(12, "glu")
            mean_square(range(4))
            dense(4)
            mean_square(range(4, KT))
            mean_square()
            for k in range(KT):
                pe.wait_ge(h_ready, 3 * KT + k + 1)
                ins = mm(bank[7][0:EXPERTS, 0:T], router_w[:, k, :], hT[:, k, :], k == 0, k == KT - 1)
            ins.then_inc(logits_full, 1)

            def token_rows(src, n, full, at):
                b, cols_ = n // 2, slice(P * (n // 2), min(P * (n // 2) + P, T))
                rows = cols_.stop - cols_.start
                for q in range(4):
                    ins = pe.transpose(bank[at][0:rows, P * q:P * q + P], src[:, 4 * (n % 2) + q, cols_], ident[:, :])
                ins.then_inc(full, 1)

            for n in range(4):
                token_rows(hT, n, xt_full, n % 4)
            pe.wait_ge(logits_copied, 1)
            for b in range(3):
                rows = P if b < 2 else NS
                ins = pe.transpose(bank[7][0:rows, EXPERTS * b:EXPERTS * b + EXPERTS],
                                   logits_t[:, P * b:P * b + rows], ident[0:EXPERTS, 0:EXPERTS])
            ins.then_inc(lg_full, 1)
            for n in range(4, 6):
                pe.wait_ge(xt_copied, n - 3)
                token_rows(hT, n, xt_full, n % 4)
            pe.wait_ge(sel_ready, 1)
            for b in range(3):
                out = bank[7][:, EXPERTS * b:EXPERTS * b + EXPERTS]
                for a in range(b + 1):
                    mm(out, (before if a == b else ones[:, :]), sel[:, a, :], a == 0, a == b)
            for a in range(3):
                ins = mm(bank[7][:, 24:32], ones[:, :], sel[:, a, :], a == 0, a == 2)
            ins.then_inc(pos_full, 1)

            def gather(j):
                pe.wait_ge(pick_ready, j + 1)
                for half in range(2):
                    out = bank[7 if half == 0 else 2]
                    for q in range(4):
                        for b in range(3):
                            ins = mm(out[:, P * q:P * q + P], x_tok[:, b, P * (4 * half + q):P * (4 * half + q) + P],
                                     pick[:, b, :], b == 0, b == 2)
                    ins.then_inc(gath_full, 1)

            def back(j, pair, second=6):
                for k in range(2 * pair, 2 * pair + 2):
                    if k >= 2:
                        pe.wait_ge(back_added, KT * j + k - 1)
                    mm(bank[second if k % 2 else 7][:, 0:T], y_job[:, k // 4, P * (k % 4):P * (k % 4) + P], spread, True, True)\
                        .then_inc(back_full, 1)

            def job(j):
                def hidden(kind, c, full):
                    out = bank[2 * (c % 2) + (kind == "up")]
                    for h in range(2):
                        n = 2 * kinds.index((kind, c)) + h
                        w = [x[half_slot(n)][:, :].rearrange("p (k n) -> p k n", n=W) for x in (w_hi, w_lo)]
                        pe.wait_ge(lo_ready, half_count(j, n))
                        for k in range(4):
                            for a, b in ((0, 0), (1, 0), (0, 1)):
                                ins = mm(out[:, :], xg[a][:, 4 * h + k, :], w[b][:, k, :], n % 2 == k == a == b == 0,
                                         h == 1 and k == 3 and b == 1)
                        ins.then_inc(full if h else first_half_used, 1)
                        if c == 0:
                            if kind == "gate" and h == 0:
                                pe.wait_ge(y_ready, 2 * j + 2)
                            back(j, 2 * (kind == "up") + h)

                def turn_h(c):
                    pe.wait_ge(h_act_ready, NCHK * j + c + 1)
                    if c:
                        pe.wait_ge(ht_lo_ready, NCHK * j + c)
                    for q in range(4):
                        ins = pe.transpose(bank[6][:, P * q:P * q + P], h_act[:, c % 2, P * q:P * q + P], ident[:, :])
                    ins.then_inc(ht_full, 1)

                def down(c):
                    pe.wait_ge(ht_lo_ready, NCHK * j + c + 1)
                    for h in range(2):
                        n = 2 * kinds.index(("down", c)) + h
                        w = [x[half_slot(n)][:, :].rearrange("p (k n) -> p k n", n=D) for x in (w_hi, w_lo)]
                        pe.wait_ge(lo_ready, half_count(j, n))
                        for k in range(2):
                            q = 2 * h + k
                            for a, b in ((0, 0), (1, 0), (0, 1)):
                                for half in range(2):
                                    ins = mm(bank[4 + half][:, :], h_t[c % 2][a][:, P * q:P * q + P],
                                             w[b][:, k, W * half:W * half + W], c == q == a == b == 0,
                                             c == NCHK - 1 and q == 3 and b == 1)
                        ins.then_inc(down_done if h else first_half_used, 1)

                pe.wait_ge(xg_lo_ready, 2 * j + 2)
                hidden("gate", 0, gate_full)
                hidden("up", 0, up_full)
                for c in range(1, NCHK):
                    if c >= 2:
                        pe.wait_ge(h_act_ready, NCHK * j + c - 1)
                    hidden("gate", c, gate_full)
                    if c == 1:
                        pe.wait_ge(back_added, KT * j + KT)
                    turn_h(c - 1)
                    hidden("up", c, up_full)
                    down(c - 1)
                    if c == 3:
                        pe.wait_ge(pickw_ready, j + 1)
                        for b in range(3):
                            rows = P if b < 2 else NS
                            ins = pe.transpose(bank[7][:, P * b:P * b + rows], pick_w[0:rows, b, :],
                                               ident[0:rows, 0:rows])
                        ins.then_inc(spread_full, 1)
                turn_h(NCHK - 1)
                pe.wait_ge(spread_copied, j + 1)
                gather(j + 1)
                down(NCHK - 1)

            pe.wait_ge(xt_copied, 6)
            gather(0)
            njobs = for_jobs(pe, job)
            pe.wait_ge(xg_lo_ready, 2 * njobs + 2)
            pe.wait_ge(y_ready, 2 * njobs + 2)
            for pair in range(KT // 2):
                back(njobs, pair, second=3)
                if pair:
                    mean_square([2 * pair - 2, 2 * pair - 1])
            mean_square([KT - 2, KT - 1])
            for i, n in enumerate(OUT_ORDER):
                pe.wait_ge(x_ready, 3 * KT + 4 * (n % 2) + 4)
                if i >= 4:
                    pe.wait_ge(outs_copied_act, i - 3)
                token_rows(xT, n, outs_t, i % 4)


_INS = ["x_prompt", "x_sample", "c_prompt", "c_sample", "state_gla", "state_conv", "state_s5_re", "state_s5_im",
        "w_ada", "b_ada", "g_norm", "w_in0", "w_gate_up", "b_gate_up", "g_head_norm", "w_conv", "w_out0",
        "w_ffn_gate", "w_ffn_up", "w_ffn_down", "w_in1", "s5_a_re", "s5_a_im", "s5_log_dt", "s5_b_re", "s5_b_im",
        "s5_c_re", "s5_c_im", "s5_d", "w_glu", "w_router", "w_exp_gate", "w_exp_up", "w_exp_down"]
_OUTS = [((1, TP, D), "float32"), ((NS, 1, D), "float32"), ((1, 1, 4, 64, 128), "float32"),
         ((1, 1, 2, 512), "float32"), ((1, 1, 64, 64), "float32"), ((1, 1, 64, 64), "float32"),
         ((NS, 1, 4, 64, 128), "float32"), ((NS, 1, 2, 512), "float32"), ((NS, 1, 64, 64), "float32"),
         ((NS, 1, 64, 64), "float32")]


def kernel(**inputs):
    import numpy as _np
    import concourse.bacc as _bacc
    from concourse import mybir as _mybir
    from concourse.bass_utils import run_bass_kernel_spmd as _run

    nc = _bacc.Bacc("TRN2", target_bir_lowering=False, num_devices=1)
    arrays, args = {}, []
    for name in _INS:
        a = _np.ascontiguousarray(inputs[name])
        arrays[f"in_{name}_dram"] = a
        args.append(nc.dram_tensor(f"in_{name}_dram", a.shape, _mybir.dt.from_np(a.dtype), kind="ExternalInput").ap())
    for i, (shape, dtype) in enumerate(_OUTS):
        dt = _mybir.dt.from_np(_np.dtype(dtype))
        args.append(nc.dram_tensor(f"out_{i}_dram", shape, dt, kind="ExternalOutput").ap())
    hybrid_trunk(nc, *args)
    r = _run(nc, [arrays], core_ids=[0])
    return tuple(r.results[0][f"out_{i}_dram"] for i in range(len(_OUTS)))
```
